# Optimizing a Trainium2 kernel written in Bass

```python
import math
import jax, jax.numpy as jnp
from jax import lax
import numpy as np

D_MODEL = 1024
BATCH = 1
SEQ = 128
DEPTH = 2
DEC_BATCH = 1
DEC_SEQ = 512
PAST_LEN = 128

GRID_W = 64
ROPE_THETA = 10000.0
EPS = 1e-6
Q_BLOCK = 128
N_BRANCH = 4
BRANCH_W = D_MODEL // 4
GDN_HEADS = 4
GDN_DK = BRANCH_W // GDN_HEADS
GDN_DV = BRANCH_W // GDN_HEADS
GDN_CHUNK = 64
CONV_K = 5
DIFF_HEADS = 4
DIFF_DV = BRANCH_W // DIFF_HEADS
DIFF_DQK = DIFF_DV // 2
SGU_GROUPS = 4
SGU_DIM = BRANCH_W // SGU_GROUPS
SPATIAL_CHUNK = 128
GQA_HEADS = 4
GQA_KV_HEADS = 2
GQA_DH = BRANCH_W // GQA_HEADS
N_GROUPS = 4
EXPERTS_PER_GROUP = 4
N_EXPERTS = N_GROUPS * EXPERTS_PER_GROUP
TOP_K_INNER = 2
D_EXPERT = D_MODEL // 4
IN_WIDTHS = (2 * GDN_HEADS * GDN_DK + GDN_HEADS * GDN_DV, GDN_HEADS * GDN_DV, 2 * GDN_HEADS, 2 * GDN_HEADS,
             2 * DIFF_HEADS * DIFF_DQK, 2 * DIFF_HEADS * DIFF_DQK, DIFF_HEADS * DIFF_DV,
             SGU_GROUPS * SGU_DIM, SGU_GROUPS * SGU_DIM,
             GQA_HEADS * GQA_DH, GQA_KV_HEADS * GQA_DH, GQA_KV_HEADS * GQA_DH, N_BRANCH * D_MODEL)
IN_COLS = sum(IN_WIDTHS)

kernel_name = 'hybrid_diffusion_prefix_trunk'

def split_points():
    pts, acc = [], 0
    for w in IN_WIDTHS[:-1]:
        acc += w
        pts.append(acc)
    return pts

def rmsnorm(x, g):
    xf = x.astype(jnp.float32)
    y = xf * lax.rsqrt(jnp.mean(xf * xf, axis=-1, keepdims=True) + EPS)
    return (y * g.astype(jnp.float32)).astype(x.dtype)

def l2norm(x):
    return x * lax.rsqrt(jnp.sum(x * x, axis=-1, keepdims=True) + EPS)

def short_conv(x, w):
    pad = CONV_K // 2
    return lax.conv_general_dilated(x, w.astype(x.dtype)[:, None, :], window_strides=(1,),
                                    padding=[(pad, pad)], dimension_numbers=('NWC', 'WIO', 'NWC'),
                                    feature_group_count=x.shape[-1])

def axial_rope(x):
    T, d = x.shape[1], x.shape[-1]
    rows = T // GRID_W
    row = jnp.repeat(jnp.arange(rows, dtype=jnp.float32), GRID_W)
    col = jnp.tile(jnp.arange(GRID_W, dtype=jnp.float32), rows)
    half = d // 2
    nf = half // 2
    inv = ROPE_THETA ** (-jnp.arange(nf, dtype=jnp.float32) / nf)
    xf = x.astype(jnp.float32)

    def rot(xa, pos):
        ang = pos[:, None] * inv[None, :]
        cos = jnp.cos(ang)[None, :, None, :]
        sin = jnp.sin(ang)[None, :, None, :]
        x1, x2 = xa[..., :nf], xa[..., nf:]
        return jnp.concatenate([x1 * cos - x2 * sin, x1 * sin + x2 * cos], axis=-1)

    return jnp.concatenate([rot(xf[..., :half], row), rot(xf[..., half:], col)], axis=-1).astype(x.dtype)

def attend(q, k, v, scale):
    B, S, Hq, d = q.shape
    Hkv = k.shape[2]
    rep = Hq // Hkv
    dv = v.shape[-1]
    nb = S // Q_BLOCK
    qb = jnp.moveaxis(q.reshape(B, nb, Q_BLOCK, Hkv, rep, d), 1, 0).astype(jnp.float32)
    kf = k.astype(jnp.float32)

    def block(qi):
        s = jnp.einsum('bqgrd,bkgd->bgrqk', qi, kf) * scale
        p = jax.nn.softmax(s, axis=-1)
        return jnp.einsum('bgrqk,bkgv->bqgrv', p.astype(v.dtype), v)

    o = lax.map(block, qb)
    return jnp.moveaxis(o, 0, 1).reshape(B, S, Hq, dv)

def gdn_chunked(q, k, v, log_a, beta, s0):
    B, T, H, DK = q.shape
    DV = v.shape[-1]
    n = T // GDN_CHUNK

    def blocks(x):
        return jnp.moveaxis(x.reshape((B, n, GDN_CHUNK) + x.shape[2:]), 2, 3)

    qc, kc, vc, bc = blocks(q), blocks(k), blocks(v), blocks(beta)
    g = jnp.cumsum(blocks(log_a), axis=-1)
    idx = jnp.arange(GDN_CHUNK)
    incl = idx[:, None] >= idx[None, :]
    strict = idx[:, None] > idx[None, :]
    diff = g[..., :, None] - g[..., None, :]
    dec_incl = jnp.where(incl, jnp.exp(jnp.where(incl, diff, 0.0)), 0.0)
    dec_strict = jnp.where(strict, dec_incl, 0.0)
    kk = jnp.einsum('bnhid,bnhjd->bnhij', kc, kc)
    a_mat = jnp.eye(GDN_CHUNK, dtype=jnp.float32) + bc[..., :, None] * kk * dec_strict
    rhs = jnp.concatenate([bc[..., None] * vc, (bc * jnp.exp(g))[..., None] * kc], axis=-1)
    sol = lax.linalg.triangular_solve(a_mat, rhs, left_side=True, lower=True, unit_diagonal=True)
    u, wk = sol[..., :DV], sol[..., DV:]
    qk = jnp.einsum('bnhid,bnhjd->bnhij', qc, kc) * dec_incl
    qg = qc * jnp.exp(g)[..., None]
    g_last = g[..., -1]
    kd = kc * jnp.exp(g_last[..., None] - g)[..., None]

    def step(s, xs):
        u_i, wk_i, qk_i, qg_i, kd_i, gl_i = xs
        w = u_i - jnp.einsum('bhcd,bhdv->bhcv', wk_i, s)
        o = jnp.einsum('bhcd,bhdv->bhcv', qg_i, s) + jnp.einsum('bhij,bhjv->bhiv', qk_i, w)
        s = jnp.exp(gl_i)[..., None, None] * s + jnp.einsum('bhcd,bhcv->bhdv', kd_i, w)
        return s, o

    xs = tuple(jnp.moveaxis(t, 1, 0) for t in (u, wk, qk, qg, kd, g_last))
    s_fin, o = lax.scan(step, s0, xs)
    o = jnp.moveaxis(jnp.moveaxis(o, 0, 1), 3, 2).reshape(B, T, H, DV)
    return o, s_fin

def gdn_mixer(qkv, gate, a, b, conv_w, a_log, dt_bias, norm_g, s0):
    B, T, _ = qkv.shape
    qkv = jax.nn.silu(short_conv(qkv, conv_w)).astype(jnp.float32)
    q, k, v = jnp.split(qkv, [GDN_HEADS * GDN_DK, 2 * GDN_HEADS * GDN_DK], axis=-1)
    q = l2norm(q.reshape(B, T, GDN_HEADS, GDN_DK)) * (GDN_DK ** -0.5)
    k = l2norm(k.reshape(B, T, GDN_HEADS, GDN_DK))
    v = v.reshape(B, T, GDN_HEADS, GDN_DV)
    a = a.astype(jnp.float32).reshape(B, T, 2, GDN_HEADS)
    b = b.astype(jnp.float32).reshape(B, T, 2, GDN_HEADS)
    log_a = -jnp.exp(a_log.astype(jnp.float32)) * jax.nn.softplus(a + dt_bias.astype(jnp.float32))
    beta = jax.nn.sigmoid(b)
    s0 = s0.astype(jnp.float32)
    o_f, s_f = gdn_chunked(q, k, v, log_a[:, :, 0], beta[:, :, 0], s0[:, 0])
    fl = lambda t: jnp.flip(t, axis=1)
    o_b, s_b = gdn_chunked(fl(q), fl(k), fl(v), fl(log_a[:, :, 1]), fl(beta[:, :, 1]), s0[:, 1])
    o = (o_f + fl(o_b)).astype(gate.dtype)
    o = rmsnorm(o, norm_g) * jax.nn.silu(gate.reshape(B, T, GDN_HEADS, GDN_DV))
    return o.reshape(B, T, GDN_HEADS * GDN_DV), jnp.stack([s_f, s_b], axis=1).astype(gate.dtype)

def diff_attention(q, k, v, lam_p, norm_g, lam_init):
    B, T = q.shape[:2]
    tk = k.shape[1]
    q = q.reshape(B, T, DIFF_HEADS, 2, DIFF_DQK)
    k = k.reshape(B, tk, DIFF_HEADS, 2, DIFF_DQK)
    scale = DIFF_DQK ** -0.5
    a1 = attend(q[..., 0, :], k[..., 0, :], v, scale)
    a2 = attend(q[..., 1, :], k[..., 1, :], v, scale)
    lp32 = lam_p.astype(jnp.float32)
    lam = jnp.exp(jnp.sum(lp32[0] * lp32[1])) - jnp.exp(jnp.sum(lp32[2] * lp32[3])) + lam_init
    o = a1.astype(jnp.float32) - lam * a2.astype(jnp.float32)
    o = rmsnorm(o, norm_g) * (1.0 - lam_init)
    return o.astype(v.dtype).reshape(B, T, DIFF_HEADS * DIFF_DV)

def sgu_mixer(u, v, norm_g, ws, bs):
    B, T, _ = u.shape
    n = T // SPATIAL_CHUNK
    vn = rmsnorm(v, norm_g).reshape(B, n, SPATIAL_CHUNK, SGU_GROUPS, SGU_DIM)
    z = jnp.einsum('gpq,bnqgc->bnpgc', ws.astype(vn.dtype), vn) + bs.T.astype(vn.dtype)[None, None, :, :, None]
    return u * z.reshape(B, T, SGU_GROUPS * SGU_DIM)

def hier_moe(x, wg, bg, we, be, w1, w3, w2):
    B, T, _ = x.shape
    g_logits = (x @ wg + bg).astype(jnp.float32)
    g_prob = jax.nn.softmax(g_logits, axis=-1)
    g_sel = jnp.argmax(g_logits, axis=-1)
    g_onehot = jax.nn.one_hot(g_sel, N_GROUPS, dtype=jnp.float32)
    e_logits = (x @ we + be).astype(jnp.float32).reshape(B, T, N_GROUPS, EXPERTS_PER_GROUP)
    e_in = jnp.sum(e_logits * g_onehot[..., None], axis=2)
    top_v, top_i = lax.top_k(e_in, TOP_K_INNER)
    w_top = jax.nn.softmax(top_v, axis=-1) * jnp.max(g_prob, axis=-1, keepdims=True)
    eid = g_sel[..., None] * EXPERTS_PER_GROUP + top_i
    gates = jnp.sum(jax.nn.one_hot(eid, N_EXPERTS, dtype=jnp.float32) * w_top[..., None], axis=-2)
    hdn = jax.nn.silu(jnp.einsum('btd,edf->btef', x, w1)) * jnp.einsum('btd,edf->btef', x, w3)
    return jnp.einsum('btef,efd->btd', hdn * gates[..., None].astype(x.dtype), w2)

def trunk_layer(h, cond, lp, lam_init, ctx):
    B, T, _ = h.shape
    latent = ctx is not None
    mod = (jax.nn.silu(cond) @ lp['ada_w'] + lp['ada_b'])[:, None, :]
    sh1, sc1, g1, sh2, sc2, g2 = jnp.split(mod, 6, axis=-1)
    xm = rmsnorm(h, lp['norm1']) * (1.0 + sc1) + sh1
    proj = xm @ lp['w_in']
    (qkv_a, gate_a, a_a, b_a, q_b, k_b, v_b, u_c, v_c, q_d, k_d, v_d, mgate) = jnp.split(proj, split_points(), axis=-1)

    s0 = ctx[0] if latent else jnp.zeros((B, 2, GDN_HEADS, GDN_DK, GDN_DV), jnp.float32)
    o_a, s_gdn = gdn_mixer(qkv_a, gate_a, a_a, b_a, lp['gdn_conv'], lp['gdn_a_log'], lp['gdn_dt_bias'], lp['gdn_norm'], s0)

    qb = q_b.reshape(B, T, 2 * DIFF_HEADS, DIFF_DQK)
    kb = k_b.reshape(B, T, 2 * DIFF_HEADS, DIFF_DQK)
    vb = v_b.reshape(B, T, DIFF_HEADS, DIFF_DV)
    if latent:
        tc = ctx[1].shape[1]
        qb_use = axial_rope(qb)
        kb_all = jnp.concatenate([ctx[1].reshape(B, tc, 2 * DIFF_HEADS, DIFF_DQK), axial_rope(kb)], axis=1)
        vb_all = jnp.concatenate([ctx[2], vb], axis=1)
    else:
        qb_use, kb_all, vb_all = qb, kb, vb
    o_b = diff_attention(qb_use, kb_all, vb_all, lp['diff_lambda'], lp['diff_norm'], lam_init)

    o_c = sgu_mixer(u_c, v_c, lp['sgu_norm'], lp['sgu_ws'], lp['sgu_b'])

    qd = rmsnorm(q_d.reshape(B, T, GQA_HEADS, GQA_DH), lp['gqa_qnorm'])
    kd = rmsnorm(k_d.reshape(B, T, GQA_KV_HEADS, GQA_DH), lp['gqa_knorm'])
    vd = v_d.reshape(B, T, GQA_KV_HEADS, GQA_DH)
    if latent:
        qd_use = axial_rope(qd)
        kd_all = jnp.concatenate([ctx[3], axial_rope(kd)], axis=1)
        vd_all = jnp.concatenate([ctx[4], vd], axis=1)
    else:
        qd_use, kd_all, vd_all = qd, kd, vd
    o_d = attend(qd_use, kd_all, vd_all, GQA_DH ** -0.5).reshape(B, T, GQA_HEADS * GQA_DH)

    br = jnp.stack([o_a, o_b, o_c, o_d], axis=2)
    up = jnp.einsum('btnw,nwd->btnd', br, lp['w_branch'])
    gt = jax.nn.sigmoid(mgate.reshape(B, T, N_BRANCH, D_MODEL))
    merged = jnp.sum(gt * up, axis=2)
    h = h + g1 * (merged @ lp['w_out'])

    xm2 = rmsnorm(h, lp['norm2']) * (1.0 + sc2) + sh2
    h = h + g2 * hier_moe(xm2, lp['moe_wg'], lp['moe_bg'], lp['moe_we'], lp['moe_be'], lp['moe_w1'], lp['moe_w3'], lp['moe_w2'])

    if latent:
        return h, None
    new_ctx = (s_gdn, kb.reshape(B, T, DIFF_HEADS, 2 * DIFF_DQK), vb, kd, vd)
    return h, new_ctx

def setup_inputs(seed: int = 0) -> dict:
    key = jax.random.key(seed)
    ks = iter(list(jax.random.split(key, 48)))

    def nrm(shape, s):
        return jax.random.normal(next(ks), shape, jnp.float32) * s

    def gain(shape):
        return 1.0 + nrm(shape, 0.01)

    dt = jnp.exp(jax.random.uniform(next(ks), (DEPTH, 2, GDN_HEADS), jnp.float32, math.log(1e-3), math.log(1e-1)))
    return {
        'x_prompt': nrm((BATCH, SEQ, D_MODEL), 1.0),
        'x_sample': nrm((DEC_BATCH, DEC_SEQ, D_MODEL), 1.0),
        'state_gdn': nrm((DEC_BATCH, DEPTH, 2, GDN_HEADS, GDN_DK, GDN_DV), 0.1),
        'cache_diff_k': nrm((DEC_BATCH, DEPTH, PAST_LEN, DIFF_HEADS, 2 * DIFF_DQK), 1.0),
        'cache_diff_v': nrm((DEC_BATCH, DEPTH, PAST_LEN, DIFF_HEADS, DIFF_DV), 1.0),
        'cache_gqa_k': nrm((DEC_BATCH, DEPTH, PAST_LEN, GQA_KV_HEADS, GQA_DH), 1.0),
        'cache_gqa_v': nrm((DEC_BATCH, DEPTH, PAST_LEN, GQA_KV_HEADS, GQA_DH), 1.0),
        'c': nrm((DEC_BATCH, D_MODEL), 1.0),
        'c_ctx': nrm((D_MODEL,), 1.0),
        'ada_w': nrm((DEPTH, D_MODEL, 6 * D_MODEL), 0.5 * D_MODEL ** -0.5),
        'ada_b': nrm((DEPTH, 6 * D_MODEL), 0.01),
        'norm1': gain((DEPTH, D_MODEL)),
        'norm2': gain((DEPTH, D_MODEL)),
        'w_in': nrm((DEPTH, D_MODEL, IN_COLS), D_MODEL ** -0.5),
        'gdn_conv': nrm((DEPTH, CONV_K, 2 * GDN_HEADS * GDN_DK + GDN_HEADS * GDN_DV), CONV_K ** -0.5),
        'gdn_a_log': jnp.log(jax.random.uniform(next(ks), (DEPTH, 2, GDN_HEADS), jnp.float32, 1.0, 16.0)),
        'gdn_dt_bias': dt + jnp.log(-jnp.expm1(-dt)),
        'gdn_norm': gain((DEPTH, GDN_DV)),
        'diff_lambda': nrm((DEPTH, 4, DIFF_DQK), 0.1),
        'diff_norm': gain((DEPTH, DIFF_DV)),
        'sgu_norm': gain((DEPTH, SGU_GROUPS * SGU_DIM)),
        'sgu_ws': nrm((DEPTH, SGU_GROUPS, SPATIAL_CHUNK, SPATIAL_CHUNK), 0.5 * SPATIAL_CHUNK ** -0.5),
        'sgu_b': gain((DEPTH, SGU_GROUPS, SPATIAL_CHUNK)),
        'gqa_qnorm': gain((DEPTH, GQA_DH)),
        'gqa_knorm': gain((DEPTH, GQA_DH)),
        'w_branch': nrm((DEPTH, N_BRANCH, BRANCH_W, D_MODEL), BRANCH_W ** -0.5),
        'w_out': nrm((DEPTH, D_MODEL, D_MODEL), D_MODEL ** -0.5),
        'moe_wg': nrm((DEPTH, D_MODEL, N_GROUPS), D_MODEL ** -0.5),
        'moe_bg': nrm((DEPTH, N_GROUPS), 0.01),
        'moe_we': nrm((DEPTH, D_MODEL, N_EXPERTS), D_MODEL ** -0.5),
        'moe_be': nrm((DEPTH, N_EXPERTS), 0.01),
        'moe_w1': nrm((DEPTH, N_EXPERTS, D_MODEL, D_EXPERT), D_MODEL ** -0.5),
        'moe_w3': nrm((DEPTH, N_EXPERTS, D_MODEL, D_EXPERT), D_MODEL ** -0.5),
        'moe_w2': nrm((DEPTH, N_EXPERTS, D_EXPERT, D_MODEL), D_EXPERT ** -0.5),
        'final_norm': gain((D_MODEL,)),
    }

def reference(x_prompt, x_sample, state_gdn, cache_diff_k, cache_diff_v, cache_gqa_k, cache_gqa_v, c, c_ctx,
              ada_w, ada_b, norm1, norm2, w_in, gdn_conv, gdn_a_log, gdn_dt_bias, gdn_norm, diff_lambda, diff_norm,
              sgu_norm, sgu_ws, sgu_b, gqa_qnorm, gqa_knorm, w_branch, w_out, moe_wg, moe_bg, moe_we, moe_be,
              moe_w1, moe_w3, moe_w2, final_norm):
    hp, hs = x_prompt, x_sample
    new_s, new_dk, new_dv, new_gk, new_gv = [], [], [], [], []
    for l in range(DEPTH):
        lp = {'ada_w': ada_w[l], 'ada_b': ada_b[l], 'norm1': norm1[l], 'norm2': norm2[l], 'w_in': w_in[l],
              'gdn_conv': gdn_conv[l], 'gdn_a_log': gdn_a_log[l], 'gdn_dt_bias': gdn_dt_bias[l], 'gdn_norm': gdn_norm[l],
              'diff_lambda': diff_lambda[l], 'diff_norm': diff_norm[l],
              'sgu_norm': sgu_norm[l], 'sgu_ws': sgu_ws[l], 'sgu_b': sgu_b[l],
              'gqa_qnorm': gqa_qnorm[l], 'gqa_knorm': gqa_knorm[l], 'w_branch': w_branch[l], 'w_out': w_out[l],
              'moe_wg': moe_wg[l], 'moe_bg': moe_bg[l], 'moe_we': moe_we[l], 'moe_be': moe_be[l],
              'moe_w1': moe_w1[l], 'moe_w3': moe_w3[l], 'moe_w2': moe_w2[l]}
        lam_init = 0.8 - 0.6 * math.exp(-0.3 * l)
        hp, ctx_out = trunk_layer(hp, c_ctx[None, :], lp, lam_init, None)
        new_s.append(ctx_out[0])
        new_dk.append(ctx_out[1])
        new_dv.append(ctx_out[2])
        new_gk.append(ctx_out[3])
        new_gv.append(ctx_out[4])
        ctx_in = (state_gdn[:, l], cache_diff_k[:, l], cache_diff_v[:, l], cache_gqa_k[:, l], cache_gqa_v[:, l])
        hs, _ = trunk_layer(hs, c, lp, lam_init, ctx_in)
    y_prompt = rmsnorm(hp, final_norm)
    y_sample = rmsnorm(hs, final_norm)
    return (y_prompt, y_sample, jnp.stack(new_s, axis=1), jnp.stack(new_dk, axis=1), jnp.stack(new_dv, axis=1),
            jnp.stack(new_gk, axis=1), jnp.stack(new_gv, axis=1))


_drawn_inputs = setup_inputs


def setup_inputs(seed=0):
    import zlib

    import numpy as np

    out = dict(_drawn_inputs(seed))
    spreads = {}
    factors = {'state_gdn': 3.136,
     'cache_gqa_k': 6.943,
     'cache_gqa_v': 6.378,
     'norm1': 3.601,
     'norm2': 5.313,
     'gdn_norm': 8.0,
     'diff_lambda': 5.001,
     'diff_norm': 36.414,
     'sgu_norm': 8.0,
     'sgu_b': 8.0,
     'gqa_qnorm': 8.0,
     'gqa_knorm': 5.901,
     'moe_bg': 8.0,
     'moe_be': 8.0,
     'final_norm': 189.806,
     'cache_diff_k': 8.0,
     'cache_diff_v': 8.0}
    for name, (base, spread) in spreads.items():
        noise = np.random.default_rng([zlib.crc32(name.encode()), seed]).standard_normal(out[name].shape)
        drawn = base * np.exp(spread * noise) if base else spread * noise
        out[name] = __import__('jax').numpy.asarray(drawn.astype(out[name].dtype))
    for name, factor in factors.items():
        out[name] = (out[name] * factor).astype(out[name].dtype)
    return out
```

```python
import math
from contextlib import ExitStack

import numpy as np
import concourse.bass as bass
from concourse import mybir

F32 = mybir.dt.float32
I32 = mybir.dt.int32
ALU = mybir.AluOpType
ACT = mybir.ActivationFunctionType
AX = mybir.AxisListType

P = 128
D = 1024
KD = D // P
DEPTH = 2
CTX, LAT = 128, 512
T = CTX + LAT
NT = T // P
EPS = 1e-6
GRID_W = 64
H = 4
DK = 64
NQKV = 6
CONV = 5
CONV_IN = CTX + LAT + 4 * (CONV // 2)
CONV_OUT = CONV_IN - 2 * (CONV // 2)
QKV_COLS = NQKV * P
TOK_COLS = 2064
GATE_COL = QKV_COLS + TOK_COLS
C_GATE, C_AB, C_QB, C_KB, C_VB, C_U, C_V, C_QD, C_KD, C_VD = 0, 256, 272, 528, 784, 1040, 1296, 1552, 1808, 1936
NE, NG, EPG, FE = 16, 4, 4, 256
MT = 25
LEVELS = [1, 2, 4, 8, 16, 32, 64]
MASKED = -1e30
BIG = 1e30


def constants():
    i = np.arange(P)
    lower = (i[:, None] >= i[None, :])
    upper = (i[:, None] <= i[None, :])
    parts, at, where = [], 0, {}

    def put(name, a):
        nonlocal at
        a = np.asarray(a, np.float32).reshape(P, -1)
        where[name] = (at, a.shape[1])
        at += a.shape[1]
        parts.append(a)

    put("ident", np.eye(P))
    put("ones", np.ones((P, P)))
    put("blockones", (i[:, None] // DK) == (i[None, :] // DK))
    put("tri0", upper)
    put("tri1", lower)
    put("neg0", np.where(upper, 0, MASKED))
    put("neg1", np.where(lower, 0, MASKED))
    put("before", i[:, None] < i[None, :])
    masks = []
    for s in LEVELS:
        pair = (i[:, None] // (2 * s)) == (i[None, :] // (2 * s))
        row_hi, col_hi = (i[:, None] // s) % 2, (i[None, :] // s) % 2
        masks += [pair & (row_hi == 0) & (col_hi == 1), pair & (row_hi == 1) & (col_hi == 0)]
    put("levels", np.stack(masks, 1))
    tok = np.arange(LAT)
    row, col = (tok // GRID_W).astype(np.float32), (tok % GRID_W).astype(np.float32)
    for name, d in (("b", 32), ("d", 64)):
        nf = d // 4
        inv = (np.float32(10000.0) ** (-np.arange(nf, dtype=np.float32) / np.float32(nf))).astype(np.float32)
        ar, ac = row[:, None] * inv[None, :], col[:, None] * inv[None, :]
        c = np.concatenate([np.cos(ar), np.cos(ar), np.cos(ac), np.cos(ac)], 1)
        s = np.concatenate([-np.sin(ar), np.sin(ar), -np.sin(ac), np.sin(ac)], 1)
        put("cos_" + name, c.reshape(NT - 1, P, d).transpose(1, 0, 2))
        put("sin_" + name, s.reshape(NT - 1, P, d).transpose(1, 0, 2))
    put("first", np.tile(4.0 - np.arange(4), (P, 1)))
    put("tile_no", np.tile(np.arange(MT), (P, 1)))
    layer = np.zeros((DEPTH, P, 2), np.float32)
    for l in range(DEPTH):
        init = 0.8 - 0.6 * math.exp(-0.3 * l)
        layer[l, :, 0], layer[l, :, 1] = init, 1.0 - init
    ids = (np.arange(NT)[None, :] * P + i[:, None]).astype(np.int32)
    return np.ascontiguousarray(np.concatenate(parts, 1)), where, layer, ids


XT = 0
MODB = XT + KD * T
PTOK = MODB + 4 * D
MERGED = PTOK
OT = PTOK + NT * D
QPRE = PTOK + NT * TOK_COLS
OALL = QPRE + NQKV * CONV_IN
RING = OALL + NT * D
RING_WORDS = 12288
TMP = RING + RING_WORDS
ARENA = TMP + 2048


class Own:

    def __init__(self, eng, sem):
        self.eng, self.sem, self.n = eng, sem, {}

    def tell(self, ins, sem):
        self.n[sem.name] = self.n.get(sem.name, 0) + 1
        ins.then_inc(sem, 1)
        self.eng.wait_ge(sem, self.n[sem.name])

    def link(self, ins):
        self.tell(ins, self.sem)


def build(nc, a, outs, where):
    ctx = ExitStack()
    ds = bass.ds
    with ctx:
        def sb(name, shape, dt=F32):
            return ctx.enter_context(nc.sbuf_tensor(name, shape, dt))

        h = sb("h", [P, NT, D])
        consts = sb("consts", [P, sum(w for _, w in where.values())])
        cond = sb("cond", [P, KD, 2])
        arena = sb("arena", [P, ARENA])
        small = sb("small", [P, 780])
        ids = sb("ids", [P, NT], I32)
        slots = sb("slots", [P, NT * 2], I32)
        slot_cols = sb("slot_cols", [P, MT, 1], I32)
        slot_ids = slot_cols[:, :, :].rearrange("p j o -> p (j o)")
        tile_expert = sb("tile_expert", [P, MT], I32)
        slot_col = sb("slot_col", [P, NT * 2, 1], I32)
        psum = ctx.enter_context(nc.psum_tensor("psum", [P, 8, 512], F32))
        mod_rows = nc.dram_tensor("mod_rows", [2, 6 * D], F32).ap()
        tok_rows = nc.dram_tensor("tok_rows", [T, D], F32).ap()
        slot_table = nc.dram_tensor("slot_table", [MT * P, 1], I32).ap()
        y_rows = nc.dram_tensor("y_rows", [MT * P, D], F32).ap()

        def c_(name):
            at, w = where[name]
            return consts[:, at:at + w]

        def ar(at, *shape):
            n = int(np.prod(shape))
            v = arena[:, at:at + n]
            if len(shape) == 2:
                v = v.rearrange("p (a b) -> p a b", b=shape[1])
            elif len(shape) == 3:
                v = v.rearrange("p (a b c) -> p a b c", b=shape[1], c=shape[2])
            return v

        def sm(at, *shape):
            n = int(np.prod(shape))
            v = small[:, at:at + n]
            if len(shape) == 2:
                v = v.rearrange("p (a b) -> p a b", b=shape[1])
            elif len(shape) == 3:
                v = v.rearrange("p (a b c) -> p a b c", b=shape[1], c=shape[2])
            return v

        def bank(i, n=1):
            return psum[:, i:i + n, :].rearrange("p a b -> p (a b)")

        ident, ones = c_("ident"), c_("ones")
        levels = c_("levels").rearrange("p (s d i) -> p s d i", s=len(LEVELS), d=2)

        pool_of = dict(pro="b", ada="a", norm1="b", gdn="a", att="b", merge="a", route="b", exp="c", fin="a")
        pools, phase_sems = dict(a=[], b=[], c=[]), {}

        def sems(phase, names):
            pool, names = pools[pool_of[phase]], names.split()
            while len(pool) < len(names):
                pool.append(ctx.enter_context(nc.semaphore(f"{pool_of[phase]}{len(pool)}")))
            phase_sems[phase] = pool[:len(names)]
            return dict(zip(names, pool))

        Q = {n: ctx.enter_context(nc.semaphore(n)) for n in "scat g0 g1 f0 f1 f2 f3".split()}
        q_sems = [Q["scat"], Q["g0"], Q["g1"], Q["f0"], Q["f1"], Q["f2"], Q["f3"]]
        assert [s.num for s in q_sems] == list(range(Q["scat"].num, Q["scat"].num + 7))
        phase_sems["scatter"], phase_sems["gathers"] = q_sems[:1], q_sems[1:]

        def forget(g, phase):
            nums = [s.num for s in phase_sems[phase]]
            g.dma_reset(range(nums[0], nums[-1] + 1))

        def clear(sp, phase):
            for s in phase_sems[phase]:
                sp.sem_clear(s)

        def bc(v, shape, axis):
            return v.unsqueeze(axis).broadcast_to([P, *shape])

        eps_col = sm(0, 1)
        eps64_col = sm(1, 1)
        one_col = sm(2, 1)

        ss, rstd = sm(4, NT), sm(10, NT)

        s = sems("pro", "loaded x_loaded cond_loaded zeroed sig cond_ready table own")
        S0 = s
        with nc.Block() as block:
            @block.sync
            def _(sp):
                sp.dma_start(consts[:, :], a["consts"]).then_inc(S0["loaded"], 16)
                sp.dma_start(ids[:, :], a["ids"]).then_inc(S0["loaded"], 16)
                sp.dma_start(h[:, 0, :], a["x_prompt"][0]).then_inc(S0["x_loaded"], 16)
                sp.dma_start(h[:, 1:NT, :], a["x_sample"][0].rearrange("(t p) d -> p t d", p=P)).then_inc(S0["x_loaded"], 16)
                sp.dma_start(ar(0, KD), a["c_ctx"].rearrange("(k p) -> p k", p=P),
                             allow_slow_non_contiguous=True).then_inc(S0["cond_loaded"], 16)
                sp.dma_start(ar(KD, KD), a["c"][0].rearrange("(k p) -> p k", p=P),
                             allow_slow_non_contiguous=True).then_inc(S0["cond_loaded"], 16)
                sp.wait_ge(S0["zeroed"], 1)
                sp.dma_start(slot_table.rearrange("(p j) o -> p (j o)", p=P), slot_ids).then_inc(S0["table"], 16)
                sp.wait_ge(S0["table"], 16)
                sp.wait_ge(S0["loaded"], 32)
                sp.wait_ge(S0["x_loaded"], 32)

            @block.vector
            def _(v):
                own = Own(v, S0["own"])
                own.tell(nc.vector.memset(slot_ids, 0), S0["zeroed"])
                own.link(nc.vector.memset(eps_col, EPS))
                own.link(nc.vector.memset(eps64_col, EPS * DK))
                own.link(nc.vector.memset(one_col, 1.0))
                v.wait_ge(S0["sig"], 1)
                cin = ar(0, 2, KD).rearrange("p s k -> p k s")
                sg = ar(2 * KD, 2, KD).rearrange("p s k -> p k s")
                own.tell(nc.vector.tensor_tensor(cond[:, :, :], cin, sg, ALU.mult), S0["cond_ready"])

            @block.scalar
            def _(act):
                act.wait_ge(S0["cond_loaded"], 32)
                nc.scalar.activation(ar(2 * KD, 2 * KD), ar(0, 2 * KD), ACT.Sigmoid).then_inc(S0["sig"], 1)

        A = sems("ada", "w0 w1 w2 rows_in mod_ps row_done stored own")
        N1 = sems("norm1", "modb w0 w1 w2 own_a own_v std xm xt_ps xt_done proj_ps evac_a evac_v")
        G = sems("gdn", "conv_in tiny_in own_a own_v own_p conv sig silu sq ssq sqrt qkn tr_ps tr_done ab_abs "
                        "ab_exp la gcol_ps gcols gexps kkg_ps gsub dt dtm bs t_ps t_done u_ps x_new xt_new "
                        "ksqs_ps r_new y_ps y_done my_ps o_done kd st_ps s_new s_in s_out zero osum oreduced "
                        "ostd osig ofin")
        B = sems("att", "in_b in_ws own_a own_v own_p sq rstd_in rstd qd_ready roped tr_ps tr_done ctx_out sc_ps "
                        "mx e comb rl pt_ps pt_done o_ps o_done wt_ps wt_done vn z_ps z_done lam_e lam ssd sstd "
                        "vss")
        M = sems("merge", "g1 wa0 wa1 own_a own_v own_p tr_ps tr_done gate_ps sig up_ps prod sum mt_ps mt_done "
                          "wo0 wo1 out_ps gprod")
        R = sems("route", "modb own_a own_v std xm xt_ps xt_done w_in lg_ps e_in e_out e2_in e2_out assign "
                          "rank_ps slots stored")
        X = sems("exp", "ids_in w0 w1 w2 w3 w4 own_v st0 st1 xt_ps xt_done h_ps sig hdn y_ps y_v g2 fused")

        def modulate_tiles(eng_v, own, S, tmp, A_, B_, want=None):
            for t in range(NT):
                st = 0 if t == 0 else 1
                if t >= 2 and want is not None:
                    want(t)
                own.link(nc.vector.scalar_tensor_tensor(tmp[:, t % 2, :], h[:, t, :], rstd[:, t:t + 1], A_[:, st, :],
                                                        ALU.mult, ALU.mult))
                own.tell(nc.vector.tensor_tensor(tmp[:, t % 2, :], tmp[:, t % 2, :], B_[:, st, :], ALU.add), S["xm"])

        layer_loop = nc.Fori(0, DEPTH)
        l = layer_loop.__enter__()

        rows = ar(PTOK, 6 * D)
        ada_b = ar(PTOK + 6 * D, 6 * D)
        norms = ar(TMP, 2, D)
        ring3 = [ar(RING + i * 4096, KD, 512) for i in range(3)]
        wA = [A["w0"], A["w1"], A["w2"]]
        with nc.Block() as block:
            @block.sync
            def _(sp):
                clear(sp, "exp")
                clear(sp, "pro")
                clear(sp, "gathers")
                for n in range(12):
                    if n >= 3:
                        sp.wait_ge(A["mod_ps"], n - 2)
                    sp.dma_start(ring3[n % 3], a["ada_w"][ds(l, 1), :, n * 512:(n + 1) * 512]
                                 .rearrange("a (k p) n -> p (a k) n", p=P)).then_inc(wA[n % 3], 16)
                    if n == 0:
                        sp.dma_start(ada_b[0:2, :], a["ada_b"][ds(l, 1), :].rearrange("a n -> (a n)")
                                     .partition_broadcast(2)).then_inc(A["rows_in"], 16)
                        sp.dma_start(norms[0:2, 0, :], a["norm1"][ds(l, 1), :].rearrange("a n -> (a n)")
                                     .partition_broadcast(2)).then_inc(A["rows_in"], 16)
                        sp.dma_start(norms[0:2, 1, :], a["norm2"][ds(l, 1), :].rearrange("a n -> (a n)")
                                     .partition_broadcast(2)).then_inc(A["rows_in"], 16)
                sp.wait_ge(A["row_done"], 12)
                sp.dma_start(mod_rows, rows[0:2, :]).then_inc(A["stored"], 16)
                sp.wait_ge(A["stored"], 16)

            @block.tensor
            def _(pe):
                for n in range(12):
                    pe.wait_ge(wA[n % 3], 16 * (n // 3 + 1))
                    if n >= 2:
                        pe.wait_ge(A["row_done"], n - 1)
                    for k in range(KD):
                        ins = nc.tensor.matmul(psum[0:2, n % 2, :], cond[:, k, :], ring3[n % 3][:, k, :],
                                               start=(k == 0), stop=(k == KD - 1))
                    ins.then_inc(A["mod_ps"], 1)

            @block.vector
            def _(v):
                own = Own(v, A["own"])
                v.wait_ge(A["rows_in"], 48)
                for n in range(12):
                    v.wait_ge(A["mod_ps"], n + 1)
                    dst = rows[0:2, n * 512:(n + 1) * 512]
                    add = nc.vector.tensor_tensor(dst, psum[0:2, n % 2, :], ada_b[0:2, n * 512:(n + 1) * 512], ALU.add)
                    if n // 2 in (1, 4):
                        own.link(add)
                        own.tell(nc.vector.scalar_tensor_tensor(
                            dst, dst, 1.0, norms[0:2, n // 8, (n % 2) * 512:(n % 2) * 512 + 512], ALU.add, ALU.mult),
                            A["row_done"])
                    else:
                        own.tell(add, A["row_done"])

        modb = ar(MODB, 4, D)
        xt = ar(XT, KD, T)
        xm2 = ar(TMP, 2, D)
        ptok = ar(PTOK, NT, TOK_COLS)
        qpre = ar(QPRE, NQKV, CONV_IN)
        junk = ar(OALL, D)
        chunks = [(0, 512), (512, 256)] + [(QKV_COLS + 512 * i, 512) for i in range(4)] + [(QKV_COLS + 2048, 16)]
        wN = [N1["w0"], N1["w1"], N1["w2"]]

        def load_modb(sp, sem, scale, shift):
            for j, (st, at) in enumerate(((0, scale), (1, scale), (0, shift), (1, shift))):
                sp.dma_start(modb[:, j, :], mod_rows[st, at * D:(at + 1) * D].partition_broadcast(P)).then_inc(sem, 16)

        with nc.Block() as block:
            items = []
            for n, (at, w) in enumerate(chunks):
                if n < 2:
                    for c in range(w // P):
                        items += [(n, "feat", at // P + c, c, part) for part in (0, 1)]
                else:
                    items += [(n, "tok", at - QKV_COLS, w, t) for t in range(NT)]

            def items_of(n):
                return 1 + max(i for i, x in enumerate(items) if x[0] == n)

            @block.sync
            def _(sp):
                clear(sp, "ada")
                load_modb(sp, N1["modb"], 1, 0)
                for n, (at, w) in enumerate(chunks):
                    if n >= 3:
                        sp.wait_ge(N1["proj_ps"], items_of(n - 3))
                    sp.dma_start(ring3[n % 3][:, :, 0:w], a["w_in"][ds(l, 1), :, at:at + w]
                                 .rearrange("a (k p) n -> p (a k) n", p=P)).then_inc(wN[n % 3], 16)

            def evacuate(i, copy):
                n, kind, x0, x1, x2 = items[i]
                src = psum[:, 4 + i % 4, :]
                if kind == "feat":
                    if x2 == 0:
                        return copy(qpre[:, x0, 2:2 + CTX], src[:, 0:CTX])
                    return copy(qpre[:, x0, 6 + CTX:6 + CTX + LAT], src[:, 0:LAT])
                return copy(ptok[:, x2, x0:x0 + x1], src[:, 0:x1])

            @block.tensor
            def _(pe):
                for t in range(NT):
                    pe.wait_ge(N1["xm"], t + 1)
                    if t >= 2:
                        pe.wait_ge(N1["xt_done"], t - 1)
                    for k in range(KD):
                        ins = nc.tensor.transpose(bank(2 * (t % 2), 2)[:, k * P:(k + 1) * P],
                                                  xm2[:, t % 2, k * P:(k + 1) * P], ident)
                    ins.then_inc(N1["xt_ps"], 1)
                pe.wait_ge(N1["xt_done"], NT)
                for i, (n, kind, x0, x1, x2) in enumerate(items):
                    first = i == 0 or items[i - 1][0] != n
                    if first:
                        pe.wait_ge(wN[n % 3], 16 * (n // 3 + 1))
                    if i >= 4:
                        pe.wait_ge(N1["evac_a"] if i % 2 == 0 else N1["evac_v"], (i - 4) // 2 + 1)
                    for k in range(KD):
                        if kind == "feat":
                            lo, w = (0, CTX) if x2 == 0 else (CTX, LAT)
                            lhs, rhs = ring3[n % 3][:, k, x1 * P:(x1 + 1) * P], xt[:, k, lo:lo + w]
                        else:
                            w = x1
                            lhs, rhs = xt[:, k, x2 * P:(x2 + 1) * P], ring3[n % 3][:, k, 0:w]
                        ins = nc.tensor.matmul(psum[:, 4 + i % 4, 0:w], lhs, rhs, start=(k == 0), stop=(k == KD - 1))
                    ins.then_inc(N1["proj_ps"], 1)

            @block.scalar
            def _(act):
                own = Own(act, N1["own_a"])
                for t in range(NT):
                    own.link(nc.scalar.activation(junk, h[:, t, :], ACT.Square, accum_out=ss[:, t:t + 1]))
                own.tell(nc.scalar.activation(rstd, ss, ACT.Sqrt, bias=eps_col, scale=1.0 / D), N1["std"])
                for t in range(NT):
                    act.wait_ge(N1["xt_ps"], t + 1)
                    own.tell(nc.scalar.activation(xt[:, :, t * P:(t + 1) * P],
                                                  bank(2 * (t % 2), 2).rearrange("p (k t) -> p k t", k=KD), ACT.Copy),
                             N1["xt_done"])
                for i in range(0, len(items), 2):
                    act.wait_ge(N1["proj_ps"], i + 1)
                    own.tell(evacuate(i, lambda o, x: nc.scalar.activation(o, x, ACT.Copy)), N1["evac_a"])

            @block.vector
            def _(v):
                own = Own(v, N1["own_v"])
                for c0, w in ((0, 2), (2 + CTX, 4), (6 + CTX + LAT, 2)):
                    own.link(nc.vector.memset(qpre[:, :, c0:c0 + w], 0.0))
                v.wait_ge(N1["std"], 1)
                own.link(nc.vector.reciprocal(rstd, rstd))
                v.wait_ge(N1["modb"], 64)
                modulate_tiles(v, own, N1, xm2, modb[:, 0:2, :], modb[:, 2:4, :],
                               lambda t: v.wait_ge(N1["xt_ps"], t - 1))
                for i in range(1, len(items), 2):
                    v.wait_ge(N1["proj_ps"], i + 1)
                    own.tell(evacuate(i, lambda o, x: nc.vector.tensor_copy(o, x)), N1["evac_v"])

        qkv = ar(MODB, NQKV, CONV_OUT)
        o_all = ar(OALL, NT, D)
        g0 = RING
        kvtok = ar(g0, NT, 512)
        dtm = ar(g0 + 2560, 2, H, P)
        mm_ = ar(g0 + 3584, 2, H, P)
        bt = ar(g0 + 4608, 2, H, P)
        bs = ar(g0 + 5632, 2, H, P)
        X_ = ar(g0 + 6656, 2, H, P)
        Xt = ar(g0 + 7680, 2, H, P)
        T_ = ar(g0 + 8704, 2, H, P)
        r_ = ar(g0 + 9728, 2, 256)
        y_ = ar(g0 + 10240, 2, 256)
        kd_ = ar(g0 + 10752, 2, 256)
        S_ = ar(g0 + 11264, 4, P)
        sig = ar(TMP, 2, CONV_OUT)
        convw = ar(TMP + 1300, CONV, NQKV)
        oq = ar(TMP + 1300 + 32, 2, 256)
        otmp = ar(TMP, NT, H * DK)
        ab = sm(20, NT, 16)
        abx = sm(100, NT, 16)
        abe = sm(180, NT, 16)
        la = sm(260, NT, 8)
        gcols = sm(300, NT, 16)
        gbk = sm(380, NT, 16)
        eg = sm(460, NT, 8)
        ekd = sm(500, NT, 16)
        dtb, alog = sm(580, 8), sm(588, 8)
        gng = sm(600, DK)
        oss = sm(664, NT * H)

        def pos(t):
            return 0 if t == 0 else 2 * (CONV // 2) + t * P

        def tiles_of(step):
            return (0, 0) if step == 0 else (step, NT - step)

        conv_w = lambda c, k: convw[:, k, c:c + 1]

        def half(x, s, which):
            return x.rearrange("p (b w c) -> p b w c", w=2, c=LEVELS[s])[:, :, which, :]

        def halves(x, s, which):
            return x.rearrange("p h (b w c) -> p h b w c", w=2, c=LEVELS[s])[:, :, :, which, :]

        def blocks(x, s):
            return x.rearrange("p (h b c) -> p h b c", h=H, c=LEVELS[s])

        with nc.Block() as block:
            @block.sync
            def _(sp):
                clear(sp, "norm1")
                for k in range(CONV):
                    sp.dma_start(convw[:, k, :], a["gdn_conv"][ds(l, 1), k, :].rearrange("a (c p) -> p (a c)", p=P),
                                 allow_slow_non_contiguous=True).then_inc(G["conv_in"], 16)
                for dst, src in ((dtb, a["gdn_dt_bias"][ds(l, 1)].rearrange("a d h -> (a d h)")),
                                 (alog, a["gdn_a_log"][ds(l, 1)].rearrange("a d h -> (a d h)")),
                                 (gng, a["gdn_norm"][ds(l, 1)].rearrange("a d -> (a d)"))):
                    sp.dma_start(dst, src.partition_broadcast(P)).then_inc(G["tiny_in"], 16)
                sp.wait_ge(G["s_new"], 2)
                for hf in range(2):
                    for d in range(2):
                        blocks = S_[hf * DK:(hf + 1) * DK, 2 * d:2 * d + 2, hf * DK:(hf + 1) * DK]
                        sp.dma_start(outs["state"][0, ds(l, 1), d, hf::2].rearrange("a c k v -> k (a c) v"), blocks)\
                          .then_inc(G["s_out"], 16)
                sp.wait_ge(G["s_out"], 64)
                for hf in range(2):
                    for d in range(2):
                        blocks = S_[hf * DK:(hf + 1) * DK, 2 * d:2 * d + 2, hf * DK:(hf + 1) * DK]
                        sp.dma_start(blocks, a["state_gdn"][0, ds(l, 1), d, hf::2].rearrange("a c k v -> k (a c) v"))\
                          .then_inc(G["s_in"], 16)
                sp.wait_ge(G["s_in"], 64)

            @block.tensor
            def _(pe):
                for c in range(4):
                    pe.wait_ge(G["sq"], c + 1)
                    if c >= 2:
                        pe.wait_ge(G["sqrt"], c - 1)
                    b = bank(2 * (c % 2), 2)
                    nc.tensor.matmul(b[:, 0:512], c_("blockones"), sig[:, c % 2, 0:512], start=True, stop=True)
                    nc.tensor.matmul(b[:, 512:CONV_OUT], c_("blockones"), sig[:, c % 2, 512:CONV_OUT],
                                     start=True, stop=True).then_inc(G["ssq"], 1)
                pe.wait_ge(G["qkn"], 4)
                pe.wait_ge(G["silu"], 6)
                for t in range(NT):
                    if t >= 2:
                        pe.wait_ge(G["tr_done"], t - 1)
                    for c in range(4):
                        ins = nc.tensor.transpose(psum[:, 4 + t % 2, c * P:(c + 1) * P],
                                                  qkv[:, 2 + c, pos(t):pos(t) + P], ident)
                    ins.then_inc(G["tr_ps"], 1)
                pe.wait_ge(G["la"], 1)
                for t in range(NT):
                    for d in range(2):
                        nc.tensor.matmul(psum[:, 6, t * 16 + 4 * d:t * 16 + 4 * d + 4], c_(f"tri{d}"),
                                         la[:, t, 4 * d:4 * d + 4], start=True, stop=True)
                    ins = nc.tensor.matmul(psum[:, 6, t * 16 + 8:t * 16 + 16], ones, la[:, t, :], start=True, stop=True)
                ins.then_inc(G["gcol_ps"], 1)
                pe.wait_ge(G["tr_done"], NT)
                pe.wait_ge(G["gcols"], 1)
                nl = len(LEVELS)
                for step in range(NT):
                    tiles = tiles_of(step)
                    for d, t in enumerate(tiles):
                        if step:
                            pe.wait_ge(G["xt_new"], 2 * nl * step)
                            pe.wait_ge(G["s_new"], 2 * step)
                            pe.wait_ge(G["o_done"], 2 * step)
                        for hh in range(H):
                            base, c = (hh % 2) * DK, hh // 2
                            kt = qkv[base:base + DK, 2 + c, pos(t):pos(t) + P]
                            qt = qkv[base:base + DK, c, pos(t):pos(t) + P]
                            o = slice(hh * P, (hh + 1) * P)
                            o2 = slice((2 * d + c) * P, (2 * d + c + 1) * P)
                            nc.tensor.matmul(psum[:, hh % 2, o2], kt, kt, start=True, stop=True)
                            nc.tensor.matmul(psum[:, 2 + hh % 2, o2], kt, qt, start=True, stop=True)
                            nc.tensor.matmul(psum[:, 4 + d, o], la[:, t, 4 * d + hh:4 * d + hh + 1].broadcast_to([P, P]),
                                             c_(f"tri{d}"), start=True, stop=False)
                            ins = nc.tensor.matmul(psum[:, 4 + d, o], ident, c_(f"neg{d}"), start=False, stop=True)
                        ins.then_inc(G["kkg_ps"], 1)
                    for s in range(nl):
                        for d in range(2):
                            n = (step * nl + s) * 2 + d
                            pe.wait_ge(G["bs"], n + 1)
                            if s == 0:
                                pe.wait_ge(G["dtm"], 2 * step + 2)
                            if s:
                                pe.wait_ge(G["x_new"], (step * (nl - 1) + s - 1) * 2 + d + 1)
                            for hh in range(H):
                                rhs = ident if s == 0 else X_[:, d, hh, :]
                                ins = nc.tensor.matmul(psum[:, d, hh * P:(hh + 1) * P], bs[:, d, hh, :], rhs,
                                                       start=True, stop=True)
                            ins.then_inc(G["t_ps"], 1)
                        if s == 0:
                            continue
                        for d in range(2):
                            pe.wait_ge(G["xt_new"], (step * nl + s - 1) * 2 + d + 1)
                            pe.wait_ge(G["t_done"], (step * (nl - 1) + s - 1) * 2 + d + 1)
                            for hh in range(H):
                                o = hh * DK
                                if s < nl - 1:
                                    nc.tensor.matmul(psum[:, 2 + d, o:o + DK], Xt[:, d, hh, :],
                                                     half(T_[:, d, hh, :], s, d), start=True, stop=True)
                                o += 256
                                ins = nc.tensor.matmul(psum[:, 2 + d, o:o + DK], T_[:, d, hh, :],
                                                       half(Xt[:, d, hh, :], s, 1 - d), start=True, stop=True)
                            ins.then_inc(G["u_ps"], 1)
                    pe.wait_ge(G["zero"], 1)
                    if step == 1:
                        pe.wait_ge(G["s_in"], 64)
                    for d, t in enumerate(tiles):
                        pe.wait_ge(G["xt_new"], (step * nl + nl - 1) * 2 + d + 1)
                        for c in range(2):
                            nc.tensor.matmul(psum[:, d, c * P:(c + 1) * P], qkv[:, 2 + c, pos(t):pos(t) + P],
                                             S_[:, 2 * d + c, :], start=True, stop=True)
                            ins = nc.tensor.matmul(psum[:, d, 256 + c * P:256 + (c + 1) * P],
                                                   qkv[:, c, pos(t):pos(t) + P], S_[:, 2 * d + c, :],
                                                   start=True, stop=True)
                        ins.then_inc(G["ksqs_ps"], 1)
                    for d, t in enumerate(tiles):
                        pe.wait_ge(G["r_new"], 2 * step + d + 1)
                        for hh in range(H):
                            ins = nc.tensor.matmul(psum[:, 2 + d, hh * DK:(hh + 1) * DK], Xt[:, d, hh, :],
                                                   r_[:, d, hh * DK:(hh + 1) * DK], start=True, stop=True)
                        ins.then_inc(G["y_ps"], 1)
                    for d, t in enumerate(tiles):
                        pe.wait_ge(G["y_done"], 2 * step + d + 1)
                        pe.wait_ge(G["kd"], 2 * step + d + 1)
                        for c in range(2):
                            ins = nc.tensor.matmul(psum[:, 4 + d, c * P:(c + 1) * P], kd_[:, d, c * P:(c + 1) * P],
                                                   y_[:, d, c * P:(c + 1) * P], start=True, stop=True)
                        ins.then_inc(G["st_ps"], 1)
                        for hh in range(H):
                            ins = nc.tensor.matmul(psum[:, 2 + d, 256 + hh * DK:256 + (hh + 1) * DK], mm_[:, d, hh, :],
                                                   y_[:, d, hh * DK:(hh + 1) * DK], start=True, stop=True)
                        ins.then_inc(G["my_ps"], 1)

            @block.scalar
            def _(act):
                own = Own(act, G["own_a"])
                for c in range(NQKV):
                    act.wait_ge(G["conv"], c + 1)
                    if c >= 2:
                        act.wait_ge(G["silu"], c - 1)
                    own.tell(nc.scalar.activation(sig[:, c % 2, :], qkv[:, c, :], ACT.Sigmoid), G["sig"])
                own.link(nc.scalar.activation(alog, alog, ACT.Exp))
                for c in range(4):
                    act.wait_ge(G["silu"], 6 if c < 2 else 6)
                    if c >= 2:
                        act.wait_ge(G["qkn"], c - 1)
                    own.tell(nc.scalar.activation(sig[:, c % 2, :], qkv[:, c, :], ACT.Square), G["sq"])
                    act.wait_ge(G["ssq"], c + 1)
                    own.tell(nc.scalar.activation(sig[:, c % 2, :], bank(2 * (c % 2), 2)[:, 0:CONV_OUT], ACT.Sqrt,
                                                  bias=eps64_col if c < 2 else eps_col,
                                                  scale=float(DK) if c < 2 else 1.0), G["sqrt"])
                act.wait_ge(G["ab_abs"], 1)
                own.link(nc.scalar.activation(abe, abx, ACT.Exp))
                own.tell(nc.scalar.activation(abe, abe, ACT.Ln, bias=one_col), G["ab_exp"])
                for t in range(NT):
                    act.wait_ge(G["tr_ps"], t + 1)
                    own.tell(nc.scalar.activation(kvtok[:, t, :], psum[:, 4 + t % 2, :], ACT.Copy), G["tr_done"])
                act.wait_ge(G["gcols"], 1)
                own.link(nc.scalar.activation(eg, gcols[:, :, 0:8], ACT.Exp))
                own.link(nc.scalar.activation(ekd[:, :, 0:8], gbk[:, :, 8:16], ACT.Exp))
                own.tell(nc.scalar.activation(ekd[:, :, 8:16], gcols[:, :, 8:16], ACT.Exp), G["gexps"])
                nl = len(LEVELS)
                for step in range(NT):
                    for d in range(2):
                        act.wait_ge(G["gsub"], 2 * step + d + 1)
                        own.tell(nc.scalar.activation(dtm[:, d], dtm[:, d], ACT.Exp), G["dt"])
                    for s in range(1, nl):
                        for d in range(2):
                            act.wait_ge(G["t_ps"], (step * nl + s) * 2 + d + 1)
                            if s >= 2:
                                act.wait_ge(G["u_ps"], (step * (nl - 1) + s - 2) * 2 + d + 1)
                            own.tell(nc.scalar.activation(T_[:, d].rearrange("p a b -> p (a b)"), psum[:, d, :],
                                                          ACT.Copy), G["t_done"])
                    for d in range(2):
                        act.wait_ge(G["y_ps"], 2 * step + d + 1)
                        own.tell(nc.scalar.activation(y_[:, d, :], psum[:, 2 + d, 0:256], ACT.Copy), G["y_done"])
                act.wait_ge(G["oreduced"], 1)
                own.tell(nc.scalar.activation(oss, oss, ACT.Sqrt, bias=eps_col, scale=1.0 / DK), G["ostd"])
                own.tell(nc.scalar.activation(otmp, ptok[:, :, C_GATE:C_GATE + 256], ACT.Sigmoid), G["osig"])

            @block.vector
            def _(v):
                own = Own(v, G["own_v"])
                vec = nc.vector
                v.wait_ge(G["conv_in"], 16 * CONV)
                v.wait_ge(G["tiny_in"], 48)
                own.link(vec.memset(S_, 0.0))
                own.tell(vec.memset(o_all[:, :, 0:256], 0.0), G["zero"])
                for c in range(NQKV):
                    own.link(vec.tensor_scalar(qkv[:, c, :], qpre[:, c, 0:CONV_OUT], conv_w(c, 0), None, ALU.mult))
                    for k in range(1, CONV):
                        ins = vec.scalar_tensor_tensor(qkv[:, c, :], qpre[:, c, k:k + CONV_OUT], conv_w(c, k),
                                                       qkv[:, c, :], ALU.mult, ALU.add)
                        (own.link if k < CONV - 1 else lambda x: own.tell(x, G["conv"]))(ins)
                own.link(vec.tensor_copy(ab, ptok[:, :, C_AB:C_AB + 16]))
                own.link(vec.tensor_tensor(ab[:, :, 0:8], ab[:, :, 0:8], bc(dtb, [NT, 8], 1), ALU.add))
                own.tell(vec.scalar_tensor_tensor(abx, ab, -1.0, ab, ALU.mult, ALU.min), G["ab_abs"])
                v.wait_ge(G["sqrt"], 1)
                for c in range(4):
                    v.wait_ge(G["sqrt"], c + 1)
                    own.link(vec.reciprocal(sig[:, c % 2, :], sig[:, c % 2, :]))
                    own.tell(vec.tensor_tensor(qkv[:, c, :], qkv[:, c, :], sig[:, c % 2, :], ALU.mult), G["qkn"])
                v.wait_ge(G["ab_exp"], 1)
                own.link(vec.scalar_tensor_tensor(la, ab[:, :, 0:8], 0.0, abe[:, :, 0:8], ALU.max, ALU.add))
                own.link(vec.tensor_tensor(la, la, bc(alog, [NT, 8], 1), ALU.mult))
                own.tell(vec.tensor_scalar(la, la, -1.0, None, ALU.mult), G["la"])
                own.link(vec.scalar_tensor_tensor(abx[:, :, 8:16], ab[:, :, 8:16], 0.0, abe[:, :, 8:16],
                                                  ALU.min, ALU.subtract))
                v.wait_ge(G["gcol_ps"], 1)
                own.link(vec.tensor_copy(gcols, psum[:, 6, 0:NT * 16].rearrange("p (t x) -> p t x", t=NT)))
                own.link(vec.tensor_tensor(gbk[:, :, 0:8], gcols[:, :, 0:8], abx[:, :, 8:16], ALU.subtract))
                own.tell(vec.tensor_tensor(gbk[:, :, 8:16], gcols[:, :, 8:16], gbk[:, :, 0:8], ALU.subtract), G["gcols"])
                v.wait_ge(G["gexps"], 1)
                nl = len(LEVELS)
                for step in range(NT):
                    tiles = tiles_of(step)
                    for d, t in enumerate(tiles):
                        v.wait_ge(G["kkg_ps"], 2 * step + d + 1)
                        own.tell(vec.tensor_tensor(dtm[:, d], psum[:, 4 + d, :].rearrange("p (a b) -> p a b", a=H),
                                                   bc(gbk[:, t, 4 * d:4 * d + 4], [H, P], 2), ALU.subtract), G["gsub"])
                    for d in range(2):
                        v.wait_ge(G["dt"], 2 * step + d + 1)
                        v.wait_ge(G["kkg_ps"], 2 * step + 2)
                        heads = lambda x: x.rearrange("p (c r) i -> p r c i", r=2)
                        prod = lambda b: psum[:, b:b + 2, 2 * d * P:2 * (d + 1) * P]\
                            .rearrange("p r (c i) -> p r c i", c=2)
                        own.link(vec.tensor_tensor(heads(mm_[:, d]), prod(2), heads(dtm[:, d]), ALU.mult))
                        own.tell(vec.tensor_tensor(heads(bt[:, d]), prod(0), heads(dtm[:, d]), ALU.mult), G["dtm"])
                    idb = bc(ident, [H, P], 1)
                    for s in range(nl):
                        for d in range(2):
                            if s == 0:
                                v.wait_ge(G["t_ps"], (step * nl) * 2 + d + 1)
                                own.tell(vec.tensor_tensor(X_[:, d], idb, psum[:, d, :].rearrange(
                                    "p (a b) -> p a b", a=H), ALU.subtract), G["x_new"])
                                own.tell(vec.tensor_tensor(Xt[:, d], idb, bs[:, d], ALU.subtract), G["xt_new"])
                                continue
                            v.wait_ge(G["u_ps"], (step * (nl - 1) + s - 1) * 2 + d + 1)
                            if s < nl - 1:
                                x = halves(X_[:, d], s, d)
                                own.tell(vec.tensor_tensor(x, x, blocks(psum[:, 2 + d, 0:256], s), ALU.subtract),
                                         G["x_new"])
                            x = halves(Xt[:, d], s, 1 - d)
                            own.tell(vec.tensor_tensor(x, x, blocks(psum[:, 2 + d, 256:512], s), ALU.subtract),
                                     G["xt_new"])
                    hd = lambda x: x.rearrange("p (a b) -> p a b", a=H)
                    for d, t in enumerate(tiles):
                        v.wait_ge(G["ksqs_ps"], 2 * step + d + 1)
                        egb = bc(eg[:, t, 4 * d:4 * d + 4], [H, DK], 2)
                        own.link(vec.tensor_tensor(hd(r_[:, d, :]), hd(psum[:, d, 0:256]), egb, ALU.mult))
                        own.tell(vec.tensor_tensor(r_[:, d, :], kvtok[:, t, 256:512], r_[:, d, :], ALU.subtract),
                                 G["r_new"])
                    for d, t in enumerate(tiles):
                        egb = bc(eg[:, t, 4 * d:4 * d + 4], [H, DK], 2)
                        own.link(vec.tensor_tensor(hd(oq[:, d, :]), hd(psum[:, d, 256:512]), egb, ALU.mult))
                    for d, t in enumerate(tiles):
                        v.wait_ge(G["st_ps"], 2 * step + d + 1)
                        if step == 1 and d == 0:
                            v.wait_ge(G["s_in"], 64)
                        for c in range(2):
                            for hf in range(2):
                                q = slice(hf * DK, (hf + 1) * DK)
                                hh = 8 + 4 * d + 2 * c + hf
                                ins = vec.scalar_tensor_tensor(
                                    S_[q, 2 * d + c, q], S_[q, 2 * d + c, q], ekd[q, t, hh:hh + 1],
                                    psum[q, 4 + d, c * P + hf * DK:c * P + (hf + 1) * DK], ALU.mult, ALU.add)
                                if c and hf:
                                    own.tell(ins, G["s_new"])
                                else:
                                    own.link(ins)
                    for d, t in enumerate(tiles):
                        v.wait_ge(G["my_ps"], 2 * step + d + 1)
                        own.link(vec.tensor_tensor(oq[:, d, :], oq[:, d, :], psum[:, 2 + d, 256:512], ALU.add))
                        own.tell(vec.tensor_tensor(o_all[:, t, 0:256], o_all[:, t, 0:256], oq[:, d, :], ALU.add),
                                 G["o_done"])
                oA = lambda t: hd(o_all[:, t, 0:256])
                v.wait_ge(G["osum"], 1)
                own.tell(vec.tensor_reduce(oss, otmp.rearrange("p t (h d) -> p (t h) d", h=H), AX.X, ALU.add),
                         G["oreduced"])
                v.wait_ge(G["ostd"], 1)
                own.link(vec.reciprocal(oss, oss))
                for t in range(NT):
                    own.link(vec.tensor_tensor(oA(t), oA(t), bc(oss[:, t * H:(t + 1) * H], [H, DK], 2), ALU.mult))
                    own.link(vec.tensor_tensor(oA(t), oA(t), bc(gng, [H, DK], 1), ALU.mult))
                    own.link(vec.tensor_tensor(o_all[:, t, 0:256], o_all[:, t, 0:256], ptok[:, t, C_GATE:C_GATE + 256],
                                               ALU.mult))
                v.wait_ge(G["osig"], 1)
                own.tell(vec.tensor_tensor(o_all[:, :, 0:256], o_all[:, :, 0:256], otmp, ALU.mult), G["ofin"])

            @block.gpsimd
            def _(g):
                own = Own(g, G["own_p"])
                for c in range(NQKV):
                    g.wait_ge(G["sig"], c + 1)
                    own.tell(nc.gpsimd.tensor_tensor(qkv[:, c, :], qkv[:, c, :], sig[:, c % 2, :], ALU.mult), G["silu"])
                nl = len(LEVELS)
                g.wait_ge(G["tr_done"], NT)
                g.wait_ge(G["gexps"], 1)
                for step in range(NT):
                    tiles = tiles_of(step)
                    for d, t in enumerate(tiles):
                        if step:
                            g.wait_ge(G["st_ps"], 2 * (step - 1) + d + 1)
                        own.tell(nc.gpsimd.tensor_tensor(
                            kd_[:, d, :].rearrange("p (a b) -> p a b", a=H),
                            kvtok[:, t, 0:256].rearrange("p (a b) -> p a b", a=H),
                            bc(ekd[:, t, 4 * d:4 * d + 4], [H, DK], 2), ALU.mult), G["kd"])
                    for s in range(nl):
                        for d in range(2):
                            if s == 0:
                                g.wait_ge(G["dtm"], 2 * step + d + 1)
                            else:
                                g.wait_ge(G["t_ps"], (step * nl + s - 1) * 2 + d + 1)
                                if s == 1:
                                    g.wait_ge(G["xt_new"], (step * nl) * 2 + d + 1)
                            own.tell(nc.gpsimd.tensor_tensor(bs[:, d], bt[:, d], bc(levels[:, s, d, :], [H, P], 1),
                                                             ALU.mult), G["bs"])
                g.wait_ge(G["o_done"], 2 * NT)
                own.tell(nc.gpsimd.tensor_tensor(otmp, o_all[:, :, 0:256], o_all[:, :, 0:256], ALU.mult), G["osum"])

        QK_COLS = T + P
        qk = ar(g0, 7, QK_COLS)
        vcb, vcd = ar(g0 + 5376, 256), ar(g0 + 5632, 128)
        kcb, kcd = ar(g0 + 5760, 256), ar(g0 + 6016, 128)
        E2 = [ar(g0 + 6144, 2, 640), ar(TMP, 2, 640)]
        PT = [ar(g0 + 7424, 5, P), ar(TMP + 1280, 5, P)]
        ws = ar(g0 + 8064, H, P)
        wsT = ar(g0 + 8576, H, P)
        vn = ar(g0 + 9088, NT, 256)
        qdn = ar(g0 + 10368, NT, 384)
        rt1 = ar(MODB, NT, 512)
        rt2 = ar(MODB + 2560, 512)
        cb, sb_ = (c_(f"{x}_b").rearrange("p (t d) -> p t d", d=32) for x in ("cos", "sin"))
        cd, sd = (c_(f"{x}_d").rearrange("p (t d) -> p t d", d=64) for x in ("cos", "sin"))
        qg, kg = sm(20, DK), sm(84, DK)
        dng, sgn = sm(148, DK), sm(212, 256)
        lamp = sm(468, 4, 32)
        lamc = sm(596, 2)
        lprod = sm(600, 2, 32)
        lsum, neglam = sm(664, 2), sm(666, 1)
        qss = sm(668, NT * 6)
        vss = sm(700, NT)
        bT = sm(706, H)
        mx, lsm, rl = sm(712, 2), sm(766, 2, 2), sm(740, 2, 4)
        dss = sm(720, NT * H)
        SC_B = 32 ** -0.5
        units = []
        for t in range(NT):
            for j in range(2 * H):
                for u in range(2 if j < H else 1):
                    units.append((t, j, u))
        att_items = [(t, j) for t in range(NT) for j in range(2 * H)]
        units_of = [[n for n, x in enumerate(units) if x[:2] == item] for item in att_items]
        with nc.Block() as block:
            @block.sync
            def _(sp):
                clear(sp, "gdn")
                for dst, src in ((qg, a["gqa_qnorm"]), (kg, a["gqa_knorm"]), (dng, a["diff_norm"]), (sgn, a["sgu_norm"])):
                    sp.dma_start(dst, src[ds(l, 1)].rearrange("a d -> (a d)").partition_broadcast(P)).then_inc(B["in_b"], 16)
                sp.dma_start(sm(468, 128), a["diff_lambda"][ds(l, 1)].rearrange("a i d -> (a i d)")
                             .partition_broadcast(P)).then_inc(B["in_b"], 16)
                sp.dma_start(lamc, a["layer_consts"][ds(l, 1)].rearrange("a p c -> p (a c)")).then_inc(B["in_b"], 16)
                sp.dma_start(bT, a["sgu_b"][ds(l, 1)].rearrange("a g p -> p (a g)"),
                             allow_slow_non_contiguous=True).then_inc(B["in_b"], 16)
                sp.dma_start(ws, a["sgu_ws"][ds(l, 1)].rearrange("a g p q -> p (a g) q")).then_inc(B["in_ws"], 16)
                for dst, src in ((kcb, a["cache_diff_k"]), (vcb, a["cache_diff_v"]), (kcd, a["cache_gqa_k"]),
                                 (vcd, a["cache_gqa_v"])):
                    sp.dma_start(dst, src[0, ds(l, 1)].rearrange("a s h d -> (a s) (h d)")).then_inc(B["in_ws"], 16)
                for dst, src in ((outs["dk"], ptok[:, 0, C_KB:C_KB + 256]), (outs["dv"], ptok[:, 0, C_VB:C_VB + 256]),
                                 (outs["gv"], ptok[:, 0, C_VD:C_VD + 128])):
                    sp.dma_start(dst[0, ds(l, 1)].rearrange("a s h d -> (a s) (h d)"), src).then_inc(B["ctx_out"], 16)
                sp.wait_ge(B["qd_ready"], NT)
                sp.dma_start(outs["gk"][0, ds(l, 1)].rearrange("a s h d -> (a s) (h d)"), qdn[:, 0, 256:384])\
                  .then_inc(B["ctx_out"], 16)
                sp.wait_ge(B["ctx_out"], 64)

            @block.tensor
            def _(pe):
                tr = nc.tensor.transpose
                pe.wait_ge(B["in_ws"], 80)
                for g in range(H):
                    ins = tr(psum[:, 6, g * P:(g + 1) * P], ws[:, g, :], ident)
                ins.then_inc(B["wt_ps"], 1)
                pe.wait_ge(B["wt_done"], 1)
                pe.wait_ge(B["vn"], 1)
                for g in range(H):
                    if g >= 2:
                        pe.wait_ge(B["z_done"], g - 1)
                    nc.tensor.matmul(psum[:, 6 + g % 2, 0:NT * DK], wsT[:, g, :],
                                     vn[:, :, g * DK:(g + 1) * DK], start=True, stop=True).then_inc(B["z_ps"], 1)
                for i, t in enumerate((0, None, 1, 2, 3, 4)):
                    if t is not None:
                        pe.wait_ge(B["roped"], t + 1)
                    if i >= 1:
                        pe.wait_ge(B["tr_done"], i)
                    q4 = lambda k: psum[:, 0, k * P:(k + 1) * P]
                    k3 = lambda k: psum[:, 1, k * P:(k + 1) * P]
                    if t is None:
                        tr(k3(0), kcb[:, 0:P], ident)
                        tr(k3(1), kcb[:, P:2 * P], ident)
                        ins = tr(k3(2), kcd, ident)
                    else:
                        for k in range(2):
                            tr(q4(k), ptok[:, t, C_QB + k * P:C_QB + (k + 1) * P], ident)
                            tr(q4(2 + k), qdn[:, t, k * P:(k + 1) * P], ident)
                            tr(k3(k), ptok[:, t, C_KB + k * P:C_KB + (k + 1) * P], ident)
                        ins = tr(k3(2), qdn[:, t, 256:384], ident)
                    ins.then_inc(B["tr_ps"], 1)
                pe.wait_ge(B["tr_done"], 6)
                pe.wait_ge(B["z_done"], H)
                def scores(i):
                    for n in units_of[i]:
                        t, j, u = units[n]
                        qcol = 0 if t == 0 else P + P * t
                        kcol, nk = (0, P) if t == 0 else (P, 5 * P)
                        if j < H:
                            hh = 2 * j + u
                            chunk, kchunk, base, w = hh // 4, 4 + hh // 4, 32 * (hh % 4), 32
                        else:
                            g = j - H
                            chunk, kchunk, base, w = 2 + g % 2, 6, DK * (g // 2), DK
                        if n >= 2:
                            pe.wait_ge(B["e"], n - 1)
                        ps = bank(2 * (n % 2), 2)
                        q = qk[base:base + w, chunk, qcol:qcol + P]
                        for k0 in range(0, nk, 512):
                            k1 = min(k0 + 512, nk)
                            ins = nc.tensor.matmul(ps[:, k0:k1], q, qk[base:base + w, kchunk, kcol + k0:kcol + k1],
                                                   start=True, stop=True)
                        ins.then_inc(B["sc_ps"], 1)

                def turn_p(i):
                    t, j = att_items[i]
                    if j < H:
                        pe.wait_ge(B["comb"], t * H + j + 1)
                    else:
                        pe.wait_ge(B["e"], units_of[i][-1] + 1)
                    if i:
                        pe.wait_ge(B["pt_done"], i)
                    for k in range(1 if t == 0 else 5):
                        ins = tr(bank(4, 2)[:, k * P:(k + 1) * P], E2[i % 2][:, 0, k * P:(k + 1) * P], ident)
                    ins.then_inc(B["pt_ps"], 1)

                def values(i):
                    t, j = att_items[i]
                    nkt = 1 if t == 0 else 5
                    pe.wait_ge(B["pt_done"], i + 1)
                    if i:
                        pe.wait_ge(B["o_done"], i)
                    for k in range(nkt):
                        if j < H:
                            val = (vcb if t and k == 0 else ptok[:, k, C_VB:C_VB + 256])[:, j * DK:(j + 1) * DK]
                        else:
                            kv = (j - H) // 2
                            val = (vcd if t and k == 0 else ptok[:, k, C_VD:C_VD + 128])[:, kv * DK:(kv + 1) * DK]
                        ins = nc.tensor.matmul(psum[:, 6, 0:DK], PT[i % 2][:, k, :], val,
                                               start=(k == 0), stop=(k == nkt - 1))
                    ins.then_inc(B["o_ps"], 1)

                scores(0)
                for i in range(len(att_items) + 1):
                    if i + 1 < len(att_items):
                        scores(i + 1)
                    if i < len(att_items):
                        turn_p(i)
                    if i:
                        values(i - 1)

            @block.scalar
            def _(act):
                own = Own(act, B["own_a"])
                act.wait_ge(B["in_b"], 16 * 7)
                act.wait_ge(B["lam_e"], 1)
                own.tell(nc.scalar.activation(lsum, lsum, ACT.Exp), B["lam"])
                act.wait_ge(B["rstd_in"], 1)
                own.link(nc.scalar.activation(qss, qss, ACT.Sqrt, bias=eps_col, scale=1.0 / DK))
                act.wait_ge(B["vss"], 1)
                own.tell(nc.scalar.activation(vss, vss, ACT.Sqrt, bias=eps_col, scale=1.0 / 256), B["rstd"])
                act.wait_ge(B["wt_ps"], 1)
                own.tell(nc.scalar.activation(wsT, psum[:, 6, :].rearrange("p (a b) -> p a b", a=H), ACT.Copy),
                         B["wt_done"])
                for i in range(6):
                    act.wait_ge(B["tr_ps"], i + 1)
                    cols = slice(i * P, (i + 1) * P)
                    if i != 1:
                        own.link(nc.scalar.activation(qk[:, 0:2, cols], psum[:, 0, 0:256]
                                                      .rearrange("p (a b) -> p a b", a=2), ACT.Copy, scale=SC_B))
                        own.link(nc.scalar.activation(qk[:, 2:4, cols], psum[:, 0, 256:512]
                                                      .rearrange("p (a b) -> p a b", a=2), ACT.Copy, scale=DK ** -0.5))
                    own.tell(nc.scalar.activation(qk[:, 4:7, cols], psum[:, 1, 0:384]
                                                  .rearrange("p (a b) -> p a b", a=3), ACT.Copy), B["tr_done"])

                def exps(i):
                    for u, n in enumerate(units_of[i]):
                        nk = P if units[n][0] == 0 else 5 * P
                        act.wait_ge(B["mx"], n + 1)
                        if i >= 2:
                            act.wait_ge(B["pt_ps"], i - 1)
                            act.wait_ge(B["rl"], i - 1)
                        own.tell(nc.scalar.activation(E2[i % 2][:, u, 0:nk], bank(2 * (n % 2), 2)[:, 0:nk], ACT.Exp,
                                                      bias=mx[:, n % 2:n % 2 + 1], accum_out=lsm[:, i % 2, u:u + 1]),
                                 B["e"])

                exps(0)
                for i, (t, j) in enumerate(att_items):
                    nk = P if t == 0 else 5 * P
                    if i + 1 < len(att_items):
                        exps(i + 1)
                    act.wait_ge(B["pt_ps"], i + 1)
                    if i >= 2:
                        act.wait_ge(B["o_ps"], i - 1)
                    own.tell(nc.scalar.activation(PT[i % 2][:, 0:nk // P, :].rearrange("p a b -> p (a b)"),
                                                  bank(4, 2)[:, 0:nk], ACT.Copy), B["pt_done"])
                act.wait_ge(B["ssd"], 1)
                own.tell(nc.scalar.activation(dss, dss, ACT.Sqrt, bias=eps_col, scale=1.0 / DK), B["sstd"])

            @block.vector
            def _(v):
                own = Own(v, B["own_v"])
                vec = nc.vector
                v.wait_ge(B["in_b"], 16 * 7)
                own.link(vec.tensor_tensor(lprod, lamp[:, 0::2, :], lamp[:, 1::2, :], ALU.mult))
                own.tell(vec.tensor_reduce(lsum, lprod, AX.X, ALU.add), B["lam_e"])
                v.wait_ge(B["lam"], 1)
                own.link(vec.tensor_tensor(neglam, lsum[:, 1:2], lsum[:, 0:1], ALU.subtract))
                own.link(vec.tensor_tensor(neglam, neglam, lamc[:, 0:1], ALU.subtract))
                own.link(vec.tensor_scalar(dng, dng, lamc[:, 1:2], None, ALU.mult))
                v.wait_ge(B["sq"], 1)
                own.tell(vec.tensor_reduce(qss, rt1[:, :, 0:384].rearrange("p t (h d) -> p t h d", h=6), AX.X, ALU.add),
                         B["rstd_in"])
                own.link(vec.tensor_tensor(vn, ptok[:, :, C_V:C_V + 256], ptok[:, :, C_V:C_V + 256], ALU.mult))
                own.tell(vec.tensor_reduce(vss, vn, AX.X, ALU.add), B["vss"])
                v.wait_ge(B["rstd"], 1)
                own.link(vec.reciprocal(qss, qss))
                own.link(vec.reciprocal(vss, vss))
                for t in range(NT):
                    x = ptok[:, t, C_QD:C_QD + 384].rearrange("p (h d) -> p h d", h=6)
                    own.link(vec.tensor_tensor(x, x, bc(qss[:, t * 6:(t + 1) * 6], [6, DK], 2), ALU.mult))
                    xq = ptok[:, t, C_QD:C_QD + 256].rearrange("p (a c d) -> p a c d", a=2, c=2)
                    oq_ = qdn[:, t, 0:256].rearrange("p (c a d) -> p a c d", a=2, c=2)
                    own.link(vec.tensor_tensor(oq_, xq, qg.unsqueeze(1).unsqueeze(1).broadcast_to([P, 2, 2, DK]),
                                               ALU.mult))
                    own.tell(vec.tensor_tensor(qdn[:, t, 256:384].rearrange("p (h d) -> p h d", h=2), x[:, 4:6, :],
                                               bc(kg, [2, DK], 1), ALU.mult), B["qd_ready"])
                for t in range(NT):
                    own.link(vec.scalar_tensor_tensor(vn[:, t, :], ptok[:, t, C_V:C_V + 256], vss[:, t:t + 1], sgn,
                                                      ALU.mult, ALU.mult))
                own.tell(vec.memset(rl[:, 0, 3:4], 0.0), B["vn"])
                for g in range(H):
                    v.wait_ge(B["z_ps"], g + 1)
                    own.tell(vec.scalar_tensor_tensor(
                        o_all[:, :, 512 + g * DK:512 + (g + 1) * DK],
                        psum[:, 6 + g % 2, 0:NT * DK].rearrange("p (t d) -> p t d", t=NT), bT[:, g:g + 1],
                        ptok[:, :, C_U + g * DK:C_U + (g + 1) * DK], ALU.add, ALU.mult), B["z_done"])

                def maxima(i):
                    for n in units_of[i]:
                        nk = P if units[n][0] == 0 else 5 * P
                        v.wait_ge(B["sc_ps"], n + 1)
                        if n >= 2:
                            v.wait_ge(B["e"], n - 1)
                        own.tell(vec.tensor_reduce(mx[:, n % 2:n % 2 + 1], bank(2 * (n % 2), 2)[:, 0:nk], AX.X,
                                                   ALU.max, negate=True), B["mx"])

                def combine(i):
                    t, j = att_items[i]
                    nk = P if t == 0 else 5 * P
                    v.wait_ge(B["e"], units_of[i][-1] + 1)
                    r, sums, E_ = rl[:, i % 2, :], lsm[:, i % 2, :], E2[i % 2]
                    if j < H:
                        own.link(vec.reciprocal(r[:, 0:2], sums))
                        own.tell(vec.scalar_tensor_tensor(r[:, 2:3], sums[:, 0:1], r[:, 1:2], neglam,
                                                          ALU.mult, ALU.mult), B["rl"])
                        own.tell(vec.scalar_tensor_tensor(E_[:, 0, 0:nk], E_[:, 1, 0:nk], r[:, 2:3], E_[:, 0, 0:nk],
                                                          ALU.mult, ALU.add), B["comb"])
                    else:
                        own.tell(vec.reciprocal(r[:, 0:1], sums[:, 0:1]), B["rl"])

                def outputs(i):
                    t, j = att_items[i]
                    v.wait_ge(B["o_ps"], i + 1)
                    at = (256 + j * DK) if j < H else (768 + (j - H) * DK)
                    own.tell(vec.tensor_scalar(o_all[:, t, at:at + DK], psum[:, 6, 0:DK], rl[:, i % 2, 0:1],
                                               None, ALU.mult), B["o_done"])

                maxima(0)
                for i in range(len(att_items) + 1):
                    if i + 1 < len(att_items):
                        maxima(i + 1)
                    if i < len(att_items):
                        combine(i)
                    if i:
                        outputs(i - 1)
                own.link(vec.tensor_tensor(vn, o_all[:, :, 256:512], o_all[:, :, 256:512], ALU.mult))
                own.tell(vec.tensor_reduce(dss, vn.rearrange("p t (h d) -> p (t h) d", h=H), AX.X, ALU.add), B["ssd"])
                v.wait_ge(B["sstd"], 1)
                own.link(vec.reciprocal(dss, dss))
                for t in range(NT):
                    x = o_all[:, t, 256:512].rearrange("p (h d) -> p h d", h=H)
                    own.link(vec.tensor_tensor(x, x, bc(dss[:, t * H:(t + 1) * H], [H, DK], 2), ALU.mult))
                    own.link(vec.tensor_tensor(x, x, bc(dng, [H, DK], 1), ALU.mult))

            @block.gpsimd
            def _(g):
                own = Own(g, B["own_p"])
                gt = nc.gpsimd.tensor_tensor
                own.tell(gt(rt1[:, :, 0:384], ptok[:, :, C_QD:C_QD + 384], ptok[:, :, C_QD:C_QD + 384], ALU.mult), B["sq"])
                g.wait_ge(B["rstd_in"], 1)
                g.wait_ge(B["qd_ready"], 1)
                own.tell(nc.gpsimd.memset(rt2[:, 0:1], 0.0), B["roped"])
                for t in range(1, NT):
                    for heads, d, x, co, si in ((16, 32, ptok[:, t, C_QB:C_QB + 512], cb, sb_),
                                                (6, 64, qdn[:, t, :], cd, sd)):
                        if heads == 6:
                            g.wait_ge(B["qd_ready"], t + 1)
                        w, nf = heads * d, d // 4
                        p1 = rt1[:, 0, 0:w]
                        own.link(gt(p1.rearrange("p (h d) -> p h d", h=heads), x.rearrange("p (h d) -> p h d", h=heads),
                                    bc(co[:, t - 1, :], [heads, d], 1), ALU.mult))
                        x5 = x.rearrange("p (h f s n) -> p h f s n", h=heads, f=2, s=2)
                        o5 = rt2[:, 0:w].rearrange("p (h f s n) -> p h f s n", h=heads, f=2, s=2)
                        s4 = si[:, t - 1, :].rearrange("p (f s n) -> p f s n", f=2, s=2)
                        for sw in range(2):
                            own.link(gt(o5[:, :, :, sw, :], x5[:, :, :, 1 - sw, :],
                                        bc(s4[:, :, sw, :], [heads, 2, nf], 1), ALU.mult))
                        ins = gt(x, p1, rt2[:, 0:w], ALU.add)
                        if heads == 6:
                            own.tell(ins, B["roped"])
                        else:
                            own.link(ins)

        merged = ar(MERGED, NT, D)
        oT = ar(OT, KD, T)
        ring2 = [ar(RING + i * 5120, 5120) for i in range(2)]
        sg = ar(RING + 10240, 2, 512)
        pr = ar(TMP, 2, 512)
        wM, wO = [M["wa0"], M["wa1"]], [M["wo0"], M["wo1"]]
        gparts = [(n, c, t) for c in range(2) for n in range(H) for t in range(NT)]
        with nc.Block() as block:
            @block.sync
            def _(sp):
                clear(sp, "att")
                for st in range(2):
                    sp.dma_start(modb[:, st, :], mod_rows[st, 2 * D:3 * D].partition_broadcast(P)).then_inc(M["g1"], 16)
                for i in range(2 * H):
                    c, n = i // H, i % H
                    if i >= 2:
                        sp.wait_ge(M["up_ps"], NT * (i - 1))
                    r = ring2[i % 2]
                    sp.dma_start(r[:, 0:4096].rearrange("p (k n) -> p k n", k=KD),
                                 a["w_in"][ds(l, 1), :, GATE_COL + n * D + c * 512:GATE_COL + n * D + c * 512 + 512]
                                 .rearrange("a (k p) n -> p (a k) n", p=P)).then_inc(wM[i % 2], 16)
                    sp.dma_start(r[:, 4096:5120].rearrange("p (k n) -> p k n", k=2),
                                 a["w_branch"][ds(l, 1), n, :, c * 512:(c + 1) * 512]
                                 .rearrange("a (k p) n -> p (a k) n", p=P)).then_inc(wM[i % 2], 16)
                for c in range(2):
                    sp.wait_ge(M["up_ps"], NT * (7 + c))
                    sp.dma_start(ring2[c][:, 0:4096].rearrange("p (k n) -> p k n", k=KD),
                                 a["w_out"][ds(l, 1), :, c * 512:(c + 1) * 512]
                                 .rearrange("a (k p) n -> p (a k) n", p=P)).then_inc(wO[c], 16)

            @block.tensor
            def _(pe):
                def turn(src, S_done, S_ps, want=None):
                    for t in range(NT):
                        if want is not None:
                            want(t)
                        if t >= 2:
                            pe.wait_ge(S_done, t - 1)
                        for k in range(KD):
                            ins = nc.tensor.transpose(bank(2 * (t % 2), 2)[:, k * P:(k + 1) * P],
                                                      src[:, t, k * P:(k + 1) * P], ident)
                        ins.then_inc(S_ps, 1)
                turn(o_all, M["tr_done"], M["tr_ps"])
                pe.wait_ge(M["tr_done"], NT)
                for i, (n, c, t) in enumerate(gparts):
                    slot = (i // NT) % 2
                    w = ring2[slot]
                    if t == 0:
                        pe.wait_ge(wM[slot], 32 * (i // NT // 2 + 1))
                    if i >= 2:
                        pe.wait_ge(M["sig"], i - 1)
                    for k in range(KD):
                        ins = nc.tensor.matmul(psum[:, 4 + i % 2, :], xt[:, k, t * P:(t + 1) * P],
                                               w[:, k * 512:(k + 1) * 512], start=(k == 0), stop=(k == KD - 1))
                    ins.then_inc(M["gate_ps"], 1)
                    if i >= 2:
                        pe.wait_ge(M["prod"], i - 1)
                    for k in range(2):
                        ins = nc.tensor.matmul(psum[:, 6 + i % 2, :], oT[:, 2 * n + k, t * P:(t + 1) * P],
                                               w[:, 4096 + k * 512:4096 + (k + 1) * 512], start=(k == 0), stop=(k == 1))
                    ins.then_inc(M["up_ps"], 1)
                turn(merged, M["mt_done"], M["mt_ps"], lambda t: pe.wait_ge(M["sum"], len(gparts) - NT + t + 1))
                pe.wait_ge(M["mt_done"], NT)
                for i in range(2 * NT):
                    c, t = i // NT, i % NT
                    pe.wait_ge(wO[c], 16)
                    if i >= 2:
                        pe.wait_ge(M["gprod"], i - 1)
                    for k in range(KD):
                        ins = nc.tensor.matmul(psum[:, 4 + i % 2, :], xt[:, k, t * P:(t + 1) * P],
                                               ring2[c][:, k * 512:(k + 1) * 512], start=(k == 0), stop=(k == KD - 1))
                    ins.then_inc(M["out_ps"], 1)

            @block.scalar
            def _(act):
                own = Own(act, M["own_a"])
                for dst, S_ps, S_done in ((oT, M["tr_ps"], M["tr_done"]), (None, None, None), (xt, M["mt_ps"], M["mt_done"])):
                    if dst is None:
                        for i in range(len(gparts)):
                            act.wait_ge(M["gate_ps"], i + 1)
                            if i >= 2:
                                act.wait_ge(M["prod"], i - 1)
                            own.tell(nc.scalar.activation(sg[:, i % 2, :], psum[:, 4 + i % 2, :], ACT.Sigmoid), M["sig"])
                        continue
                    for t in range(NT):
                        act.wait_ge(S_ps, t + 1)
                        own.tell(nc.scalar.activation(dst[:, :, t * P:(t + 1) * P],
                                                      bank(2 * (t % 2), 2).rearrange("p (k t) -> p k t", k=KD),
                                                      ACT.Copy), S_done)

            @block.vector
            def _(v):
                own = Own(v, M["own_v"])
                for i, (n, c, t) in enumerate(gparts):
                    v.wait_ge(M["sig"], i + 1)
                    v.wait_ge(M["up_ps"], i + 1)
                    if i >= 2:
                        v.wait_ge(M["sum"], i - 1)
                    own.tell(nc.vector.tensor_tensor(pr[:, i % 2, :], sg[:, i % 2, :], psum[:, 6 + i % 2, :], ALU.mult),
                             M["prod"])
                v.wait_ge(M["g1"], 32)
                v.wait_ge(M["sum"], len(gparts))
                for i in range(2 * NT):
                    c, t = i // NT, i % NT
                    v.wait_ge(M["out_ps"], i + 1)
                    own.tell(nc.vector.tensor_tensor(pr[:, i % 2, :], psum[:, 4 + i % 2, :],
                                                     modb[:, 0 if t == 0 else 1, c * 512:(c + 1) * 512], ALU.mult),
                             M["gprod"])
                    own.link(nc.vector.tensor_tensor(h[:, t, c * 512:(c + 1) * 512], h[:, t, c * 512:(c + 1) * 512],
                                                     pr[:, i % 2, :], ALU.add))

            @block.gpsimd
            def _(g):
                own = Own(g, M["own_p"])
                for i, (n, c, t) in enumerate(gparts):
                    g.wait_ge(M["prod"], i + 1)
                    dst = merged[:, t, c * 512:(c + 1) * 512]
                    if n == 0:
                        own.tell(nc.gpsimd.tensor_copy(dst, pr[:, i % 2, :]), M["sum"])
                    else:
                        own.tell(nc.gpsimd.tensor_tensor(dst, dst, pr[:, i % 2, :], ALU.add), M["sum"])

        xm5 = ar(PTOK, NT, D)
        wge = ar(RING, KD, 20)
        junk2 = ar(OALL, D)
        lg = sm(20, NT, 20)
        bge = sm(120, 20)
        m4, oh_g = sm(140, NT, 4), sm(160, NT, 4)
        gmax, gsum = sm(180, NT), sm(185, NT)
        ein, oh1, oh2 = sm(190, NT, 4), sm(210, NT, 4), sm(230, NT, 4)
        v1, v2, ee = sm(250, NT), sm(255, NT), sm(260, NT)
        wtop = sm(266, NT, 2)
        e16 = sm(280, NT, 16)
        sel1, sel2, assign = sm(360, NT, 16), sm(440, NT, 16), sm(520, NT, 16)
        slot_f = sm(600, NT, 16)
        tiles_e, cum, cum2 = sm(680, 16), sm(696, 16), sm(712, 16)
        stile = sm(728, NT * 2)
        cmp_ = ar(TMP, MT, 16)
        texp = sm(740, MT)
        with nc.Block() as block:
            @block.sync
            def _(sp):
                clear(sp, "merge")
                load_modb(sp, R["modb"], 4, 3)
                sp.dma_start(wge[:, :, 0:4], a["moe_wg"][ds(l, 1)].rearrange("a (k p) n -> p (a k) n", p=P)).then_inc(R["w_in"], 16)
                sp.dma_start(wge[:, :, 4:20], a["moe_we"][ds(l, 1)].rearrange("a (k p) n -> p (a k) n", p=P)).then_inc(R["w_in"], 16)
                sp.dma_start(bge[:, 0:4], a["moe_bg"][ds(l, 1)].rearrange("a n -> (a n)").partition_broadcast(P)).then_inc(R["w_in"], 16)
                sp.dma_start(bge[:, 4:20], a["moe_be"][ds(l, 1)].rearrange("a n -> (a n)").partition_broadcast(P)).then_inc(R["w_in"], 16)
                for t in range(NT):
                    sp.wait_ge(R["xm"], t + 1)
                    sp.dma_start(tok_rows[t * P:(t + 1) * P, :], xm5[:, t, :]).then_inc(R["stored"], 16)
                sp.wait_ge(R["stored"], 16 * NT)

            @block.tensor
            def _(pe):
                for t in range(NT):
                    pe.wait_ge(R["xm"], t + 1)
                    if t >= 2:
                        pe.wait_ge(R["xt_done"], t - 1)
                    for k in range(KD):
                        ins = nc.tensor.transpose(bank(2 * (t % 2), 2)[:, k * P:(k + 1) * P],
                                                  xm5[:, t, k * P:(k + 1) * P], ident)
                    ins.then_inc(R["xt_ps"], 1)
                pe.wait_ge(R["xt_done"], NT)
                pe.wait_ge(R["w_in"], 64)
                for t in range(NT):
                    for k in range(KD):
                        ins = nc.tensor.matmul(psum[:, 4, t * 20:(t + 1) * 20], xt[:, k, t * P:(t + 1) * P],
                                               wge[:, k, :], start=(k == 0), stop=(k == KD - 1))
                ins.then_inc(R["lg_ps"], 1)
                pe.wait_ge(R["assign"], 1)
                for t in range(NT):
                    o = psum[:, 5, t * 16:(t + 1) * 16]
                    for t2 in range(t):
                        nc.tensor.matmul(o, ones, assign[:, t2, :], start=(t2 == 0), stop=False)
                    nc.tensor.matmul(o, c_("before"), assign[:, t, :], start=(t == 0), stop=True)
                for t in range(NT):
                    ins = nc.tensor.matmul(psum[:, 5, NT * 16:(NT + 1) * 16], ones, assign[:, t, :],
                                           start=(t == 0), stop=(t == NT - 1))
                ins.then_inc(R["rank_ps"], 1)

            @block.scalar
            def _(act):
                own = Own(act, R["own_a"])
                for t in range(NT):
                    own.link(nc.scalar.activation(junk2, h[:, t, :], ACT.Square, accum_out=ss[:, t:t + 1]))
                own.tell(nc.scalar.activation(rstd, ss, ACT.Sqrt, bias=eps_col, scale=1.0 / D), R["std"])
                for t in range(NT):
                    act.wait_ge(R["xt_ps"], t + 1)
                    own.tell(nc.scalar.activation(xt[:, :, t * P:(t + 1) * P],
                                                  bank(2 * (t % 2), 2).rearrange("p (k t) -> p k t", k=KD), ACT.Copy),
                             R["xt_done"])
                act.wait_ge(R["e_in"], 1)
                own.tell(nc.scalar.activation(m4, m4, ACT.Exp), R["e_out"])
                act.wait_ge(R["e2_in"], 1)
                own.tell(nc.scalar.activation(ee, ee, ACT.Exp), R["e2_out"])

            @block.vector
            def _(v):
                own = Own(v, R["own_v"])
                vec, link = nc.vector, own.link
                v.wait_ge(R["std"], 1)
                link(vec.reciprocal(rstd, rstd))
                v.wait_ge(R["modb"], 64)
                for t in range(NT):
                    st = 0 if t == 0 else 1
                    link(vec.scalar_tensor_tensor(xm5[:, t, :], h[:, t, :], rstd[:, t:t + 1], modb[:, st, :],
                                                  ALU.mult, ALU.mult))
                    own.tell(vec.tensor_tensor(xm5[:, t, :], xm5[:, t, :], modb[:, 2 + st, :], ALU.add), R["xm"])
                v.wait_ge(R["w_in"], 64)
                v.wait_ge(R["lg_ps"], 1)
                link(vec.tensor_tensor(lg, psum[:, 4, 0:NT * 20].rearrange("p (t n) -> p t n", t=NT),
                                       bc(bge, [NT, 20], 1), ALU.add))
                first = bc(c_("first"), [NT, 4], 1)

                def argmax(onehot, x, top):
                    link(vec.tensor_reduce(top, x, AX.X, ALU.max))
                    link(vec.tensor_tensor(onehot, x, bc(top, [NT, 4], 2), ALU.is_equal))
                    link(vec.tensor_tensor(onehot, onehot, first, ALU.mult))
                    link(vec.tensor_reduce(gsum, onehot, AX.X, ALU.max))
                    link(vec.tensor_tensor(onehot, onehot, bc(gsum, [NT, 4], 2), ALU.is_equal))

                gl = lg[:, :, 0:4]
                argmax(oh_g, gl, gmax)
                own.tell(vec.tensor_tensor(m4, gl, bc(gmax, [NT, 4], 2), ALU.subtract), R["e_in"])
                el = lg[:, :, 4:20].rearrange("p t (g e) -> p t g e", g=NG)
                for t in range(NT):
                    link(vec.tensor_tensor(e16[:, t, :].rearrange("p (g e) -> p g e", g=NG), el[:, t],
                                           bc(oh_g[:, t, :], [NG, EPG], 2), ALU.mult))
                link(vec.tensor_reduce(ein, e16.rearrange("p t (g e) -> p t e g", g=NG), AX.X, ALU.add))
                argmax(oh1, ein, v1)
                link(vec.scalar_tensor_tensor(ein, oh1, -BIG, ein, ALU.mult, ALU.add))
                argmax(oh2, ein, v2)
                own.tell(vec.tensor_tensor(ee, v2, v1, ALU.subtract), R["e2_in"])
                v.wait_ge(R["e_out"], 1)
                link(vec.tensor_reduce(gsum, m4, AX.X, ALU.add))
                v.wait_ge(R["e2_out"], 1)
                link(vec.tensor_scalar(v1, ee, 1.0, None, ALU.add))
                link(vec.tensor_tensor(v1, v1, gsum, ALU.mult))
                link(vec.reciprocal(v1, v1))
                link(vec.tensor_copy(wtop[:, :, 0], v1))
                link(vec.tensor_tensor(wtop[:, :, 1], v1, ee, ALU.mult))
                for sel, oh in ((sel1, oh1), (sel2, oh2)):
                    for t in range(NT):
                        link(vec.tensor_tensor(sel[:, t, :].rearrange("p (g e) -> p g e", g=NG),
                                               bc(oh_g[:, t, :], [NG, EPG], 2), bc(oh[:, t, :], [NG, EPG], 1), ALU.mult))
                own.tell(vec.tensor_tensor(assign, sel1, sel2, ALU.add), R["assign"])
                v.wait_ge(R["rank_ps"], 1)
                link(vec.tensor_copy(slot_f, psum[:, 5, 0:NT * 16].rearrange("p (t e) -> p t e", t=NT)))
                link(vec.tensor_copy(cum2, psum[:, 5, NT * 16:(NT + 1) * 16]))
                link(vec.tensor_scalar(tiles_e, cum2, 0.0, None, ALU.is_gt))
                for k in range(1, NT):
                    link(vec.scalar_tensor_tensor(tiles_e, cum2, float(k * P), tiles_e, ALU.is_gt, ALU.add))
                link(vec.tensor_copy(cum, tiles_e))
                bufs = [cum, cum2]
                for i, sh in enumerate((1, 2, 4, 8)):
                    x, y = bufs[i % 2], bufs[1 - i % 2]
                    link(vec.tensor_copy(y[:, 0:sh], x[:, 0:sh]))
                    link(vec.tensor_tensor(y[:, sh:16], x[:, sh:16], x[:, 0:16 - sh], ALU.add))
                link(vec.tensor_tensor(cum2, cum, tiles_e, ALU.subtract))
                link(vec.tensor_scalar(cum2, cum2, float(P), None, ALU.mult))
                link(vec.tensor_tensor(slot_f, slot_f, bc(cum2, [NT, 16], 1), ALU.add))
                for k, sel in enumerate((sel1, sel2)):
                    link(vec.tensor_tensor(e16, slot_f, sel, ALU.mult))
                    link(vec.tensor_reduce(stile[:, k * NT:(k + 1) * NT], e16, AX.X, ALU.add))
                link(vec.tensor_copy(slots[:, :], stile))
                own.tell(vec.tensor_copy(slot_col[:, :, 0], slots[:, :]), R["slots"])
                link(vec.tensor_tensor(cmp_, bc(c_("tile_no"), [MT, 16], 2), bc(cum, [MT, 16], 1), ALU.is_ge))
                link(vec.tensor_reduce(texp, cmp_, AX.X, ALU.add))
                link(vec.tensor_scalar(texp, texp, float(NE - 1), None, ALU.min))
                link(vec.tensor_copy(tile_expert[:, :], texp))

            @block.gpsimd
            def _(g):
                g.wait_ge(R["slots"], 1)
                for k in range(2):
                    for t in range(NT):
                        nc.gpsimd.indirect_dma_start(
                            out=slot_table, out_offset=bass.IndirectOffsetOnAxis(ap=slot_col[:, k * NT + t, :], axis=0),
                            in_=ids[:, t:t + 1], in_offset=None).then_inc(Q["scat"], 16)
                g.wait_ge(Q["scat"], 16 * 2 * NT)
                forget(g, "scatter")

        U = 5
        wslot = [ar(u * 6144, 6144) for u in range(U)]
        xg = ar(30720, 2, D)
        xgT = ar(32768, 2, D)
        hT = ar(34816, 2, 256)
        sgx = ar(35328, 2, 256)
        yv = ar(35840, 2, D)
        fin = [ar(i * D, D) for i in range(8)]
        g2b = ar(8 * D, 2, D)
        wX = [X["w0"], X["w1"], X["w2"], X["w3"], X["w4"]]
        gX = [Q["g0"], Q["g1"]]
        stX = [X["st0"], X["st1"]]
        fX = [Q["f0"], Q["f1"], Q["f2"], Q["f3"]]
        C, CY = 2, U
        PER = (3, 2)

        def free(j, u):
            return j if u == 0 else j - 1

        with nc.Block() as block:
            @block.sync
            def _(sp):
                clear(sp, "route")
                clear(sp, "scatter")
                sp.dma_start(slot_ids, slot_table.rearrange("(j p) o -> p (j o)", p=P),
                             allow_slow_non_contiguous=True).then_inc(X["ids_in"], 16)
                with sp.Fori(0, MT // U) as i:
                    for u in range(U):
                        e = sp.value_load(tile_expert[0:1, ds(i * U + u, 1)], min_val=0, max_val=NE - 1)
                        sp.wait_ge(X["y_ps"], i * U + u + 1)
                        w = wslot[u]
                        w13 = w[:, 0:4096].rearrange("p (k n) -> p k n", k=KD)
                        sp.dma_start(w13[:, :, 0:FE], a["moe_w1"][ds(l, 1), ds(e, 1)]
                                     .rearrange("a e (k p) n -> p (a e k) n", p=P)).then_inc(wX[u], 16)
                        sp.dma_start(w13[:, :, FE:2 * FE], a["moe_w3"][ds(l, 1), ds(e, 1)]
                                     .rearrange("a e (k p) n -> p (a e k) n", p=P)).then_inc(wX[u], 16)
                        sp.dma_start(w[:, 4096:6144].rearrange("p (k n) -> p k n", k=2), a["moe_w2"][ds(l, 1), ds(e, 1)]
                                     .rearrange("a e (k p) n -> p (a e k) n", p=P)).then_inc(wX[u], 16)
                sp.wait_ge(X["y_ps"], MT + CY)
                for st in range(2):
                    sp.dma_start(g2b[:, st, :], mod_rows[st, 5 * D:6 * D].partition_broadcast(P)).then_inc(X["g2"], 16)

            @block.gpsimd
            def _(g):
                g.wait_ge(X["ids_in"], 16)
                for j in range(MT):
                    u = j % U
                    g.wait_ge(X["xt_ps"], free(j, u) + C)
                    nc.gpsimd.indirect_dma_start(
                        out=xg[:, u % 2, :], out_offset=None, in_=tok_rows,
                        in_offset=bass.IndirectOffsetOnAxis(ap=slot_cols[:, j, :], axis=0)).then_inc(gX[u % 2], 16)
                for b in range(2):
                    g.wait_ge(stX[b], 16 * (PER[b] * (MT // U) + 1))
                for t in range(NT):
                    if t == 4:
                        g.wait_ge(X["fused"], 1)
                    for k in range(2):
                        nc.gpsimd.indirect_dma_start(
                            out=fin[2 * (t % 4) + k], out_offset=None, in_=y_rows,
                            in_offset=bass.IndirectOffsetOnAxis(ap=slot_col[:, k * NT + t, :], axis=0))\
                            .then_inc(fX[t % 4], 16)
                g.wait_ge(X["fused"], NT)
                forget(g, "gathers")

            @block.tensor
            def _(pe):
                pe.sem_inc(X["xt_ps"], C)
                pe.sem_inc(X["h_ps"], C)
                pe.sem_inc(X["y_ps"], CY)

                def turn(i, u):
                    j = i * U + u
                    pe.wait_ge(gX[u % 2], (i * PER[u % 2] + u // 2 + 1) * 16)
                    pe.wait_ge(X["xt_done"], j + C)
                    for k in range(KD):
                        ins = nc.tensor.transpose(bank(0, 2)[:, k * P:(k + 1) * P], xg[:, u % 2, k * P:(k + 1) * P],
                                                  ident)
                    ins.then_inc(X["xt_ps"], 1)

                with pe.Fori(0, MT // U) as i:
                    turn(i, 0)
                    for u in range(U):
                        j = i * U + u
                        w13 = wslot[u][:, 0:4096].rearrange("p (k n) -> p k n", k=KD)
                        w2 = wslot[u][:, 4096:6144].rearrange("p (k n) -> p k n", k=2)
                        pe.wait_ge(X["xt_done"], j + 1 + C)
                        pe.wait_ge(wX[u], (i + 1) * 48)
                        pe.wait_ge(X["hdn"], free(j, u) + C)
                        for c in range(4):
                            for k in range(KD):
                                ins = nc.tensor.matmul(psum[:, 2 + u % 2, c * P:(c + 1) * P],
                                                       w13[:, k, c * P:(c + 1) * P], xgT[:, u % 2, k * P:(k + 1) * P],
                                                       start=(k == 0), stop=(k == KD - 1))
                        ins.then_inc(X["h_ps"], 1)
                        if u < U - 1:
                            turn(i, u + 1)
                        pe.wait_ge(X["hdn"], j + 1 + C)
                        pe.wait_ge(X["y_v"], free(j, u) + C)
                        for c in range(2):
                            for k in range(2):
                                ins = nc.tensor.matmul(psum[:, 4 + 2 * (u % 2) + c, :], hT[:, u % 2, k * P:(k + 1) * P],
                                                       w2[:, k, c * 512:(c + 1) * 512], start=(k == 0), stop=(k == 1))
                        ins.then_inc(X["y_ps"], 1)

            @block.scalar
            def _(act):
                act.sem_inc(X["xt_done"], C)
                for b in range(2):
                    act.sem_inc(stX[b], 16)

                def evac(i, u):
                    j = i * U + u
                    act.wait_ge(X["xt_ps"], j + 1 + C)
                    act.wait_ge(X["h_ps"], free(j, u) + C)
                    nc.scalar.activation(xgT[:, u % 2, :], bank(0, 2), ACT.Copy).then_inc(X["xt_done"], 1)

                with act.Fori(0, MT // U) as i:
                    evac(i, 0)
                    for u in range(U):
                        j = i * U + u
                        act.wait_ge(X["h_ps"], j + 1 + C)
                        act.wait_ge(X["hdn"], free(j, u) + C)
                        nc.scalar.activation(sgx[:, u % 2, :], psum[:, 2 + u % 2, 0:256], ACT.Silu).then_inc(X["sig"], 1)
                        if u < U - 1:
                            evac(i, u + 1)
                        act.wait_ge(X["y_v"], j + 1 + C)
                        act.dma_start(y_rows[ds(j * P, P), :], yv[:, u % 2, :]).then_inc(stX[u % 2], 16)

            @block.vector
            def _(v):
                vec = nc.vector
                v.sem_inc(X["hdn"], C)
                v.sem_inc(X["y_v"], C)
                with v.Fori(0, MT // U) as i:
                    for u in range(U):
                        j = i * U + u
                        v.wait_ge(X["sig"], j + 1)
                        v.wait_ge(X["y_ps"], free(j, u) + CY)
                        vec.tensor_tensor(hT[:, u % 2, :], sgx[:, u % 2, :], psum[:, 2 + u % 2, 256:512], ALU.mult)\
                            .then_inc(X["hdn"], 1)
                        v.wait_ge(X["y_ps"], j + 1 + CY)
                        v.wait_ge(stX[u % 2], (i * PER[u % 2] + u // 2 + 1) * 16)
                        vec.tensor_copy(yv[:, u % 2, :], bank(4 + 2 * (u % 2), 2)).then_inc(X["y_v"], 1)
                v.wait_ge(X["g2"], 32)
                own = Own(v, X["own_v"])
                for t in range(NT):
                    f1, f2 = fin[2 * (t % 4)], fin[2 * (t % 4) + 1]
                    v.wait_ge(fX[t % 4], 32 * (t // 4 + 1))
                    own.link(vec.tensor_scalar(f1, f1, wtop[:, t, 0:1], None, ALU.mult))
                    own.link(vec.scalar_tensor_tensor(f1, f2, wtop[:, t, 1:2], f1, ALU.mult, ALU.add))
                    own.link(vec.tensor_tensor(f1, f1, g2b[:, 0 if t == 0 else 1, :], ALU.mult))
                    own.tell(vec.tensor_tensor(h[:, t, :], h[:, t, :], f1, ALU.add), X["fused"])

        layer_loop.__exit__(None, None, None)

        F = sems("fin", "gain own_a own_v std done out")
        fout = ar(0, NT, D)
        fgain = ar(NT * D, D)
        fjunk = ar(NT * D + D, D)
        with nc.Block() as block:
            @block.sync
            def _(sp):
                sp.dma_start(fgain, a["final_norm"].partition_broadcast(P)).then_inc(F["gain"], 16)
                for t in range(NT):
                    sp.wait_ge(F["done"], t + 1)
                    dst = outs["y_prompt"][0] if t == 0 else outs["y_sample"][0, (t - 1) * P:t * P, :]
                    sp.dma_start(dst, fout[:, t, :]).then_inc(F["out"], 16)
                sp.wait_ge(F["out"], 16 * NT)

            @block.scalar
            def _(act):
                own = Own(act, F["own_a"])
                for t in range(NT):
                    own.link(nc.scalar.activation(fjunk, h[:, t, :], ACT.Square, accum_out=ss[:, t:t + 1]))
                own.tell(nc.scalar.activation(rstd, ss, ACT.Sqrt, bias=eps_col, scale=1.0 / D), F["std"])

            @block.vector
            def _(v):
                own = Own(v, F["own_v"])
                v.wait_ge(F["std"], 1)
                own.link(nc.vector.reciprocal(rstd, rstd))
                v.wait_ge(F["gain"], 16)
                for t in range(NT):
                    own.tell(nc.vector.scalar_tensor_tensor(fout[:, t, :], h[:, t, :], rstd[:, t:t + 1], fgain,
                                                            ALU.mult, ALU.mult), F["done"])


_INS = ['x_prompt', 'x_sample', 'state_gdn', 'cache_diff_k', 'cache_diff_v', 'cache_gqa_k', 'cache_gqa_v', 'c', 'c_ctx',
        'ada_w', 'ada_b', 'norm1', 'norm2', 'w_in', 'gdn_conv', 'gdn_a_log', 'gdn_dt_bias', 'gdn_norm', 'diff_lambda',
        'diff_norm', 'sgu_norm', 'sgu_ws', 'sgu_b', 'gqa_qnorm', 'gqa_knorm', 'w_branch', 'w_out', 'moe_wg', 'moe_bg',
        'moe_we', 'moe_be', 'moe_w1', 'moe_w3', 'moe_w2', 'final_norm']
_OUTS = [('y_prompt', (1, CTX, D)), ('y_sample', (1, LAT, D)), ('state', (1, DEPTH, 2, H, DK, DK)),
         ('dk', (1, DEPTH, CTX, H, DK)), ('dv', (1, DEPTH, CTX, H, DK)),
         ('gk', (1, DEPTH, CTX, 2, DK)), ('gv', (1, DEPTH, CTX, 2, DK))]


def kernel(**inputs):
    import concourse.bacc as _bacc
    from concourse.bass_utils import run_bass_kernel_spmd as _run

    nc = _bacc.Bacc("TRN2", target_bir_lowering=False, num_devices=1)
    table, where, layer, ids = constants()
    arrays, args = {}, {}
    given = {name: np.ascontiguousarray(inputs[name]) for name in _INS}
    given.update(consts=table, layer_consts=layer, ids=ids)
    for name, x in given.items():
        arrays[f"in_{name}"] = x
        args[name] = nc.dram_tensor(f"in_{name}", x.shape, mybir.dt.from_np(x.dtype), kind="ExternalInput").ap()
    outs = {name: nc.dram_tensor(f"out_{name}", shape, F32, kind="ExternalOutput").ap() for name, shape in _OUTS}
    build(nc, args, outs, where)
    r = _run(nc, [arrays], core_ids=[0])
    return tuple(r.results[0][f"out_{name}"] for name, _ in _OUTS)
```

```python
import math
from contextlib import ExitStack

import numpy as np
import concourse.bass as bass
from concourse import mybir

F32 = mybir.dt.float32
I32 = mybir.dt.int32
ALU = mybir.AluOpType
ACT = mybir.ActivationFunctionType
AX = mybir.AxisListType

P = 128
D = 1024
KD = D // P
DEPTH = 2
CTX, LAT = 128, 512
T = CTX + LAT
NT = T // P
EPS = 1e-6
GRID_W = 64
H = 4
DK = 64
NQKV = 6
CONV = 5
CONV_IN = CTX + LAT + 4 * (CONV // 2)
CONV_OUT = CONV_IN - 2 * (CONV // 2)
QKV_COLS = NQKV * P
TOK_COLS = 2064
GATE_COL = QKV_COLS + TOK_COLS
C_GATE, C_AB, C_QB, C_KB, C_VB, C_U, C_V, C_QD, C_KD, C_VD = 0, 256, 272, 528, 784, 1040, 1296, 1552, 1808, 1936
NE, NG, EPG, FE = 16, 4, 4, 256
MT = 25
LEVELS = [1, 2, 4, 8, 16, 32, 64]
MASKED = -1e30
BIG = 1e30


def constants():
    i = np.arange(P)
    lower = (i[:, None] >= i[None, :])
    upper = (i[:, None] <= i[None, :])
    parts, at, where = [], 0, {}

    def put(name, a):
        nonlocal at
        a = np.asarray(a, np.float32).reshape(P, -1)
        where[name] = (at, a.shape[1])
        at += a.shape[1]
        parts.append(a)

    put("ident", np.eye(P))
    put("ones", np.ones((P, P)))
    put("blockones", (i[:, None] // DK) == (i[None, :] // DK))
    put("tri0", upper)
    put("tri1", lower)
    put("neg0", np.where(upper, 0, MASKED))
    put("neg1", np.where(lower, 0, MASKED))
    put("before", i[:, None] < i[None, :])
    masks = []
    for s in LEVELS:
        pair = (i[:, None] // (2 * s)) == (i[None, :] // (2 * s))
        row_hi, col_hi = (i[:, None] // s) % 2, (i[None, :] // s) % 2
        masks += [pair & (row_hi == 0) & (col_hi == 1), pair & (row_hi == 1) & (col_hi == 0)]
    put("levels", np.stack(masks, 1))
    tok = np.arange(LAT)
    row, col = (tok // GRID_W).astype(np.float32), (tok % GRID_W).astype(np.float32)
    for name, d in (("b", 32), ("d", 64)):
        nf = d // 4
        inv = (np.float32(10000.0) ** (-np.arange(nf, dtype=np.float32) / np.float32(nf))).astype(np.float32)
        ar, ac = row[:, None] * inv[None, :], col[:, None] * inv[None, :]
        c = np.concatenate([np.cos(ar), np.cos(ar), np.cos(ac), np.cos(ac)], 1)
        s = np.concatenate([-np.sin(ar), np.sin(ar), -np.sin(ac), np.sin(ac)], 1)
        put("cos_" + name, c.reshape(NT - 1, P, d).transpose(1, 0, 2))
        put("sin_" + name, s.reshape(NT - 1, P, d).transpose(1, 0, 2))
    put("first", np.tile(4.0 - np.arange(4), (P, 1)))
    put("tile_no", np.tile(np.arange(MT), (P, 1)))
    layer = np.zeros((DEPTH, P, 2), np.float32)
    for l in range(DEPTH):
        init = 0.8 - 0.6 * math.exp(-0.3 * l)
        layer[l, :, 0], layer[l, :, 1] = init, 1.0 - init
    ids = (np.arange(NT)[None, :] * P + i[:, None]).astype(np.int32)
    return np.ascontiguousarray(np.concatenate(parts, 1)), where, layer, ids


XT = 0
MODB = XT + KD * T
PTOK = MODB + 4 * D
MERGED = PTOK
OT = PTOK + NT * D
QPRE = PTOK + NT * TOK_COLS
OALL = QPRE + NQKV * CONV_IN
RING = OALL + NT * D
RING_WORDS = 12288
TMP = RING + RING_WORDS
ARENA = TMP + 2048


class Own:

    def __init__(self, eng, sem):
        self.eng, self.sem, self.n = eng, sem, {}

    def tell(self, ins, sem):
        self.n[sem.name] = self.n.get(sem.name, 0) + 1
        ins.then_inc(sem, 1)
        self.eng.wait_ge(sem, self.n[sem.name])

    def link(self, ins):
        self.tell(ins, self.sem)

    def send(self, ins, sem):
        self.n[sem.name] = self.n.get(sem.name, 0) + 1
        ins.then_inc(sem, 1)

    def settle(self, sem):
        self.eng.wait_ge(sem, self.n[sem.name])


def build(nc, a, outs, where):
    ctx = ExitStack()
    ds = bass.ds
    with ctx:
        def sb(name, shape, dt=F32):
            return ctx.enter_context(nc.sbuf_tensor(name, shape, dt))

        h = sb("h", [P, NT, D])
        consts = sb("consts", [P, sum(w for _, w in where.values())])
        cond = sb("cond", [P, KD, 2])
        arena = sb("arena", [P, ARENA])
        small = sb("small", [P, 780])
        ids = sb("ids", [P, NT], I32)
        slots = sb("slots", [P, NT * 2], I32)
        slot_cols = sb("slot_cols", [P, MT, 1], I32)
        slot_ids = slot_cols[:, :, :].rearrange("p j o -> p (j o)")
        tile_expert = sb("tile_expert", [P, MT], I32)
        slot_col = sb("slot_col", [P, NT * 2, 1], I32)
        psum = ctx.enter_context(nc.psum_tensor("psum", [P, 8, 512], F32))
        mod_rows = nc.dram_tensor("mod_rows", [2, 6 * D], F32).ap()
        tok_rows = nc.dram_tensor("tok_rows", [T, D], F32).ap()
        slot_table = nc.dram_tensor("slot_table", [MT * P, 1], I32).ap()
        y_rows = nc.dram_tensor("y_rows", [MT * P, D], F32).ap()
        h_rows = nc.dram_tensor("h_rows", [P, NT, D], F32).ap()
        gate_rows = nc.dram_tensor("gate_rows", [NT, P, 4 * D], F32).ap()

        def c_(name):
            at, w = where[name]
            return consts[:, at:at + w]

        def ar(at, *shape):
            n = int(np.prod(shape))
            v = arena[:, at:at + n]
            if len(shape) == 2:
                v = v.rearrange("p (a b) -> p a b", b=shape[1])
            elif len(shape) == 3:
                v = v.rearrange("p (a b c) -> p a b c", b=shape[1], c=shape[2])
            return v

        def sm(at, *shape):
            n = int(np.prod(shape))
            v = small[:, at:at + n]
            if len(shape) == 2:
                v = v.rearrange("p (a b) -> p a b", b=shape[1])
            elif len(shape) == 3:
                v = v.rearrange("p (a b c) -> p a b c", b=shape[1], c=shape[2])
            return v

        def bank(i, n=1):
            return psum[:, i:i + n, :].rearrange("p a b -> p (a b)")

        ident, ones = c_("ident"), c_("ones")
        levels = c_("levels").rearrange("p (s d i) -> p s d i", s=len(LEVELS), d=2)

        pool_of = dict(pro="b", ada="a", norm1="b", gdn="a", att="b", merge="a", route="b", exp="c", fin="a")
        pools, phase_sems = dict(a=[], b=[], c=[]), {}

        def sems(phase, names):
            pool, names = pools[pool_of[phase]], names.split()
            while len(pool) < len(names):
                pool.append(ctx.enter_context(nc.semaphore(f"{pool_of[phase]}{len(pool)}")))
            phase_sems[phase] = pool[:len(names)]
            return dict(zip(names, pool))

        Q = {n: ctx.enter_context(nc.semaphore(n)) for n in "scat g0 g1 f0 f1 f2 f3".split()}
        q_sems = [Q["scat"], Q["g0"], Q["g1"], Q["f0"], Q["f1"], Q["f2"], Q["f3"]]
        assert [s.num for s in q_sems] == list(range(Q["scat"].num, Q["scat"].num + 7))
        phase_sems["scatter"], phase_sems["gathers"] = q_sems[:1], q_sems[1:]

        def forget(g, phase):
            nums = [s.num for s in phase_sems[phase]]
            g.dma_reset(range(nums[0], nums[-1] + 1))

        def clear(sp, phase):
            for s in phase_sems[phase]:
                sp.sem_clear(s)

        def bc(v, shape, axis):
            return v.unsqueeze(axis).broadcast_to([P, *shape])

        eps_col = sm(0, 1)
        eps64_col = sm(1, 1)
        one_col = sm(2, 1)

        ss, rstd = sm(4, NT), sm(10, NT)

        s = sems("pro", "loaded x_loaded cond_loaded zeroed sig cond_ready table own")
        S0 = s
        with nc.Block() as block:
            @block.sync
            def _(sp):
                sp.dma_start(consts[:, :], a["consts"]).then_inc(S0["loaded"], 16)
                sp.dma_start(ids[:, :], a["ids"]).then_inc(S0["loaded"], 16)
                sp.dma_start(h[:, 0, :], a["x_prompt"][0]).then_inc(S0["x_loaded"], 16)
                sp.dma_start(h[:, 1:NT, :], a["x_sample"][0].rearrange("(t p) d -> p t d", p=P)).then_inc(S0["x_loaded"], 16)
                sp.dma_start(ar(0, KD), a["c_ctx"].rearrange("(k p) -> p k", p=P),
                             allow_slow_non_contiguous=True).then_inc(S0["cond_loaded"], 16)
                sp.dma_start(ar(KD, KD), a["c"][0].rearrange("(k p) -> p k", p=P),
                             allow_slow_non_contiguous=True).then_inc(S0["cond_loaded"], 16)
                sp.wait_ge(S0["zeroed"], 1)
                sp.dma_start(slot_table.rearrange("(p j) o -> p (j o)", p=P), slot_ids).then_inc(S0["table"], 16)
                sp.wait_ge(S0["table"], 16)
                sp.wait_ge(S0["loaded"], 32)
                sp.wait_ge(S0["x_loaded"], 32)

            @block.vector
            def _(v):
                own = Own(v, S0["own"])
                own.tell(nc.vector.memset(slot_ids, 0), S0["zeroed"])
                own.link(nc.vector.memset(eps_col, EPS))
                own.link(nc.vector.memset(eps64_col, EPS * DK))
                own.link(nc.vector.memset(one_col, 1.0))
                v.wait_ge(S0["sig"], 1)
                cin = ar(0, 2, KD).rearrange("p s k -> p k s")
                sg = ar(2 * KD, 2, KD).rearrange("p s k -> p k s")
                own.tell(nc.vector.tensor_tensor(cond[:, :, :], cin, sg, ALU.mult), S0["cond_ready"])

            @block.scalar
            def _(act):
                act.wait_ge(S0["cond_loaded"], 32)
                nc.scalar.activation(ar(2 * KD, 2 * KD), ar(0, 2 * KD), ACT.Sigmoid).then_inc(S0["sig"], 1)

        A = sems("ada", "w0 w1 w2 rows_in mod_ps row_done stored own")
        N1 = sems("norm1", "h_out gate_w modb w0 w1 w2 own_a own_v std xm xt_ps xt_done proj_ps evac_a evac_v")
        G = sems("gdn", "gl_ps gl_done gw0 gw1 gs0 gs1 gs2 conv_in tiny_in own_a own_v own_p conv sig silu sq ssq sqrt qkn tr_ps tr_done ab_abs "
                        "ab_exp la gcol_ps gcols gexps g_ps kk_ps kq_ps gsub dt bt mm bs t_ps t_done u_ps x_new xt_new "
                        "ksqs_ps r_new y_ps y_done my_ps o_done kd st_ps s_new s_in s_out zero osum oreduced "
                        "ostd osig ofin")
        B = sems("att", "gl_ps gl_done gw0 gw1 gs0 gs1 gs2 in_b in_ws own_a own_v own_p sq rstd_in rstd qd_ready roped tr_ps tr_done ctx_out sc_ps "
                        "mx e comb rl pt_ps pt_done o_ps o_done wt_ps wt_done vn z_ps z_done lam_e lam ssd sstd "
                        "vss")
        M = sems("merge", "lg0 lg1 lg2 h_in wo g1 wa0 wa1 own_a own_v own_p tr_ps tr_done sig up_ps prod sum mt_ps mt_done "
                          "out_ps gprod")
        R = sems("route", "modb own_a own_v std xm xt_ps xt_done w_in lg_ps e_in e_out e2_in e2_out assign "
                          "rank_ps slots stored")
        X = sems("exp", "f1 ids_in w0 w1 w2 w3 w4 own_v st0 st1 xt_ps xt_done h_ps sig hdn y_ps y_v g2 fused")

        def modulate_tiles(eng_v, own, S, tmp, A_, B_, want=None):
            for t in range(NT):
                st = 0 if t == 0 else 1
                if t >= 2 and want is not None:
                    want(t)
                own.link(nc.vector.scalar_tensor_tensor(tmp[:, t % 2, :], h[:, t, :], rstd[:, t:t + 1], A_[:, st, :],
                                                        ALU.mult, ALU.mult))
                own.tell(nc.vector.tensor_tensor(tmp[:, t % 2, :], tmp[:, t % 2, :], B_[:, st, :], ALU.add), S["xm"])

        GW = 256
        GCHUNKS = 4 * D // GW // 2
        GITEMS = GCHUNKS * NT
        gw = [h[:, 2 * i:2 * i + 2, :].rearrange("p a b -> p (a b)").rearrange("p (k n) -> p k n", k=KD) for i in range(2)]
        gout = h[:, 4, :].rearrange("p (s n) -> p s n", s=4)
        gate_xt = ar(XT, KD, T)

        def load_gate_weights(sp, sem, chunk):
            at = GATE_COL + chunk * GW
            sp.dma_start(gw[chunk % 2], a["w_in"][ds(l, 1), :, at:at + GW].rearrange("a (k p) n -> p (a k) n", p=P))\
              .then_inc(sem, 16)

        def move_gates(sp, S, first, items):
            for i in items:
                c, t = i // NT, i % NT
                if t == NT - 1 and first + c + 2 < 2 * GCHUNKS:
                    sp.wait_ge(S["gl_ps"], i + 1)
                    load_gate_weights(sp, S[f"gw{c % 2}"], first + c + 2)
                sp.wait_ge(S["gl_done"], i + 1)
                sp.dma_start(gate_rows[t, :, (first + c) * GW:(first + c + 1) * GW], gout[:, i % 3, :])\
                  .then_inc(S[f"gs{i % 3}"], 16)

        def gate_moves_done(sp, S, first):
            for j in range(3):
                sp.wait_ge(S[f"gs{j}"], 16 * ((GITEMS - j + 2) // 3))
            for j in range(2):
                n = len([c for c in range(GCHUNKS) if c % 2 == j and first + c + 2 < 2 * GCHUNKS])
                sp.wait_ge(S[f"gw{j}"], 16 * n)

        def gate_filler(pe, S, bank_of):
            issued = [0]

            def fill(n):
                for _ in range(n):
                    i, k = issued[0] // KD, issued[0] % KD
                    c, t = i // NT, i % NT
                    if k == 0:
                        if t == 0 and c >= 2:
                            pe.wait_ge(S[f"gw{c % 2}"], 16 * (c // 2))
                        before = [j for j in range(i) if bank_of(j) == bank_of(i)]
                        if before:
                            pe.wait_ge(S["gl_done"], before[-1] + 1)
                    ins = nc.tensor.matmul(psum[:, bank_of(i), 0:GW], gate_xt[:, k, t * P:(t + 1) * P], gw[c % 2][:, k, :],
                                           start=(k == 0), stop=(k == KD - 1))
                    if k == KD - 1:
                        ins.then_inc(S["gl_ps"], 1)
                    issued[0] += 1
            return fill

        def gate_evacuator(act, own, S, bank_of):
            copied = [0]

            def evac(n):
                for i in range(copied[0], n):
                    act.wait_ge(S["gl_ps"], i + 1)
                    if i >= 3:
                        act.wait_ge(S[f"gs{i % 3}"], 16 * (i // 3))
                    own.send(nc.scalar.activation(gout[:, i % 3, :], psum[:, bank_of(i), 0:GW], ACT.Copy), S["gl_done"])
                copied[0] = max(copied[0], n)
            return evac

        layer_loop = nc.Fori(0, DEPTH)
        l = layer_loop.__enter__()

        rows = ar(PTOK, 6 * D)
        ada_b = ar(PTOK + 6 * D, 6 * D)
        norms = ar(TMP, 2, D)
        ring3 = [ar(RING + i * 4096, KD, 512) for i in range(3)]
        wA = [A["w0"], A["w1"], A["w2"]]
        with nc.Block() as block:
            @block.sync
            def _(sp):
                clear(sp, "exp")
                clear(sp, "pro")
                clear(sp, "gathers")
                for n in range(12):
                    if n >= 3:
                        sp.wait_ge(A["mod_ps"], n - 2)
                    sp.dma_start(ring3[n % 3], a["ada_w"][ds(l, 1), :, n * 512:(n + 1) * 512]
                                 .rearrange("a (k p) n -> p (a k) n", p=P)).then_inc(wA[n % 3], 16)
                    if n == 0:
                        sp.dma_start(ada_b[0:2, :], a["ada_b"][ds(l, 1), :].rearrange("a n -> (a n)")
                                     .partition_broadcast(2)).then_inc(A["rows_in"], 16)
                        sp.dma_start(norms[0:2, 0, :], a["norm1"][ds(l, 1), :].rearrange("a n -> (a n)")
                                     .partition_broadcast(2)).then_inc(A["rows_in"], 16)
                        sp.dma_start(norms[0:2, 1, :], a["norm2"][ds(l, 1), :].rearrange("a n -> (a n)")
                                     .partition_broadcast(2)).then_inc(A["rows_in"], 16)
                sp.wait_ge(A["row_done"], 12)
                sp.dma_start(mod_rows, rows[0:2, :]).then_inc(A["stored"], 16)
                sp.wait_ge(A["stored"], 16)

            @block.tensor
            def _(pe):
                for n in range(12):
                    pe.wait_ge(wA[n % 3], 16 * (n // 3 + 1))
                    if n >= 2:
                        pe.wait_ge(A["row_done"], n - 1)
                    for k in range(KD):
                        ins = nc.tensor.matmul(psum[0:2, n % 2, :], cond[:, k, :], ring3[n % 3][:, k, :],
                                               start=(k == 0), stop=(k == KD - 1))
                    ins.then_inc(A["mod_ps"], 1)

            @block.vector
            def _(v):
                own = Own(v, A["own"])
                v.wait_ge(A["rows_in"], 48)
                for n in range(12):
                    v.wait_ge(A["mod_ps"], n + 1)
                    dst = rows[0:2, n * 512:(n + 1) * 512]
                    add = nc.vector.tensor_tensor(dst, psum[0:2, n % 2, :], ada_b[0:2, n * 512:(n + 1) * 512], ALU.add)
                    if n // 2 in (1, 4):
                        own.link(add)
                        own.tell(nc.vector.scalar_tensor_tensor(
                            dst, dst, 1.0, norms[0:2, n // 8, (n % 2) * 512:(n % 2) * 512 + 512], ALU.add, ALU.mult),
                            A["row_done"])
                    else:
                        own.tell(add, A["row_done"])

        modb = ar(MODB, 4, D)
        xt = ar(XT, KD, T)
        xm2 = ar(TMP, 2, D)
        ptok = ar(PTOK, NT, TOK_COLS)
        qpre = ar(QPRE, NQKV, CONV_IN)
        junk = ar(OALL, NT, D)
        chunks = [(QKV_COLS, 512), (0, 512), (512, 256)] + [(QKV_COLS + 512 * i, 512) for i in range(1, 4)] \
            + [(QKV_COLS + 2048, 16)]
        wN = [N1["w0"], N1["w1"], N1["w2"]]

        def load_modb(sp, sem, scale, shift):
            for j, (st, at) in enumerate(((0, scale), (1, scale), (0, shift), (1, shift))):
                sp.dma_start(modb[:, j, :], mod_rows[st, at * D:(at + 1) * D].partition_broadcast(P)).then_inc(sem, 16)

        with nc.Block() as block:
            items = []
            for n, (at, w) in enumerate(chunks):
                if at < QKV_COLS:
                    for c in range(w // P):
                        items += [(n, "feat", at // P + c, c, part) for part in (0, 1)]
                else:
                    items += [(n, "tok", at - QKV_COLS, w, t) for t in range(NT)]

            def items_of(n):
                return 1 + max(i for i, x in enumerate(items) if x[0] == n)

            @block.sync
            def _(sp):
                clear(sp, "ada")
                load_modb(sp, N1["modb"], 1, 0)
                for n, (at, w) in enumerate(chunks):
                    if n >= 3:
                        sp.wait_ge(N1["proj_ps"], items_of(n - 3))
                    sp.dma_start(ring3[n % 3][:, :, 0:w], a["w_in"][ds(l, 1), :, at:at + w]
                                 .rearrange("a (k p) n -> p (a k) n", p=P)).then_inc(wN[n % 3], 16)
                    if n == 2:
                        sp.dma_start(h_rows, h[:, :, :]).then_inc(N1["h_out"], 16)
                sp.wait_ge(N1["xm"], NT)
                sp.wait_ge(N1["h_out"], 16)
                for c in range(2):
                    load_gate_weights(sp, N1["gate_w"], c)
                sp.wait_ge(N1["gate_w"], 32)

            def evacuate(i, copy):
                n, kind, x0, x1, x2 = items[i]
                src = psum[:, 4 + i % 4, :]
                if kind == "feat":
                    if x2 == 0:
                        return copy(qpre[:, x0, 2:2 + CTX], src[:, 0:CTX])
                    return copy(qpre[:, x0, 6 + CTX:6 + CTX + LAT], src[:, 0:LAT])
                return copy(ptok[:, x2, x0:x0 + x1], src[:, 0:x1])

            @block.tensor
            def _(pe):
                def turn(t):
                    pe.wait_ge(N1["xm"], t + 1)
                    if t >= 2:
                        pe.wait_ge(N1["xt_done"], t - 1)
                    for k in range(KD):
                        ins = nc.tensor.transpose(bank(2 * (t % 2), 2)[:, k * P:(k + 1) * P],
                                                  xm2[:, t % 2, k * P:(k + 1) * P], ident)
                    ins.then_inc(N1["xt_ps"], 1)

                def project(i):
                    n, kind, x0, x1, x2 = items[i]
                    first = i == 0 or items[i - 1][0] != n
                    if first:
                        pe.wait_ge(wN[n % 3], 16 * (n // 3 + 1))
                    if i >= 4:
                        pe.wait_ge(N1["evac_a"] if i % 2 == 0 else N1["evac_v"], (i - 4) // 2 + 1)
                    for k in range(KD):
                        if kind == "feat":
                            lo, w = (0, CTX) if x2 == 0 else (CTX, LAT)
                            lhs, rhs = ring3[n % 3][:, k, x1 * P:(x1 + 1) * P], xt[:, k, lo:lo + w]
                        else:
                            w = x1
                            lhs, rhs = xt[:, k, x2 * P:(x2 + 1) * P], ring3[n % 3][:, k, 0:w]
                        ins = nc.tensor.matmul(psum[:, 4 + i % 4, 0:w], lhs, rhs, start=(k == 0), stop=(k == KD - 1))
                    ins.then_inc(N1["proj_ps"], 1)

                turn(0)
                for i in range(len(items)):
                    if i + 1 < NT:
                        turn(i + 1)
                    if i < NT:
                        pe.wait_ge(N1["xt_done"], i + 1)
                    project(i)

            @block.scalar
            def _(act):
                own = Own(act, N1["own_a"])
                for t in range(NT):
                    own.send(nc.scalar.activation(junk[:, t, :], h[:, t, :], ACT.Square, accum_out=ss[:, t:t + 1]), N1["own_a"])
                own.settle(N1["own_a"])
                own.tell(nc.scalar.activation(rstd, ss, ACT.Sqrt, bias=eps_col, scale=1.0 / D), N1["std"])
                for t in range(NT):
                    act.wait_ge(N1["xt_ps"], t + 1)
                    own.tell(nc.scalar.activation(xt[:, :, t * P:(t + 1) * P],
                                                  bank(2 * (t % 2), 2).rearrange("p (k t) -> p k t", k=KD), ACT.Copy),
                             N1["xt_done"])
                for i in range(0, len(items), 2):
                    act.wait_ge(N1["proj_ps"], i + 1)
                    own.send(evacuate(i, lambda o, x: nc.scalar.activation(o, x, ACT.Copy)), N1["evac_a"])

            @block.vector
            def _(v):
                own = Own(v, N1["own_v"])
                for c0, w in ((0, 2), (2 + CTX, 4), (6 + CTX + LAT, 2)):
                    own.link(nc.vector.memset(qpre[:, :, c0:c0 + w], 0.0))
                v.wait_ge(N1["std"], 1)
                own.link(nc.vector.reciprocal(rstd, rstd))
                v.wait_ge(N1["modb"], 64)
                modulate_tiles(v, own, N1, xm2, modb[:, 0:2, :], modb[:, 2:4, :],
                               lambda t: v.wait_ge(N1["xt_ps"], t - 1))
                for i in range(1, len(items), 2):
                    v.wait_ge(N1["proj_ps"], i + 1)
                    own.send(evacuate(i, lambda o, x: nc.vector.tensor_copy(o, x)), N1["evac_v"])

        qkv = ar(MODB, NQKV, CONV_OUT)
        o_all = ar(OALL, NT, D)
        g0 = RING
        kvtok = ar(g0, NT, 512)
        dtm = ar(g0 + 2560, 2, H, P)
        mm_ = ar(g0 + 3584, 2, H, P)
        bt = ar(g0 + 4608, 2, H, P)
        bs = ar(g0 + 5632, 2, H, P)
        X_ = ar(g0 + 6656, 2, H, P)
        Xt = ar(g0 + 7680, 2, H, P)
        T_ = ar(g0 + 8704, 2, H, P)
        r_ = ar(g0 + 9728, 2, 256)
        y_ = ar(g0 + 10240, 2, 256)
        kd_ = ar(g0 + 10752, 2, 256)
        S_ = ar(g0 + 11264, 4, P)
        sig = ar(TMP, 2, CONV_OUT)
        convw = ar(TMP + 1300, CONV, NQKV)
        oq = ar(TMP + 1300 + 32, 2, 256)
        otmp = ar(TMP, NT, H * DK)
        ab = sm(20, NT, 16)
        abx = sm(100, NT, 16)
        abe = sm(180, NT, 16)
        la = sm(260, NT, 8)
        gcols = sm(300, NT, 16)
        gbk = sm(380, NT, 16)
        eg = sm(460, NT, 8)
        ekd = sm(500, NT, 16)
        dtb, alog = sm(580, 8), sm(588, 8)
        gng = sm(600, DK)
        oss = sm(664, NT * H)

        def pos(t):
            return 0 if t == 0 else 2 * (CONV // 2) + t * P

        def tiles_of(step):
            return (0, 0) if step == 0 else (step, NT - step)

        conv_w = lambda c, k: convw[:, k, c:c + 1]

        gdn_gate_bank = lambda i: 6 + i % 2

        def half(x, s, which):
            return x.rearrange("p (b w c) -> p b w c", w=2, c=LEVELS[s])[:, :, which, :]

        def halves(x, s, which):
            return x.rearrange("p h (b w c) -> p h b w c", w=2, c=LEVELS[s])[:, :, :, which, :]

        def blocks(x, s):
            return x.rearrange("p (h b c) -> p h b c", h=H, c=LEVELS[s])

        with nc.Block() as block:
            @block.sync
            def _(sp):
                clear(sp, "norm1")
                for k in range(CONV):
                    sp.dma_start(convw[:, k, :], a["gdn_conv"][ds(l, 1), k, :].rearrange("a (c p) -> p (a c)", p=P),
                                 allow_slow_non_contiguous=True).then_inc(G["conv_in"], 16)
                for dst, src in ((dtb, a["gdn_dt_bias"][ds(l, 1)].rearrange("a d h -> (a d h)")),
                                 (alog, a["gdn_a_log"][ds(l, 1)].rearrange("a d h -> (a d h)")),
                                 (gng, a["gdn_norm"][ds(l, 1)].rearrange("a d -> (a d)"))):
                    sp.dma_start(dst, src.partition_broadcast(P)).then_inc(G["tiny_in"], 16)
                move_gates(sp, G, 0, range(17))
                sp.wait_ge(G["s_new"], 8)
                for hf in range(2):
                    for d in range(2):
                        blocks = S_[hf * DK:(hf + 1) * DK, 2 * d:2 * d + 2, hf * DK:(hf + 1) * DK]
                        sp.dma_start(outs["state"][0, ds(l, 1), d, hf::2].rearrange("a c k v -> k (a c) v"), blocks)\
                          .then_inc(G["s_out"], 16)
                sp.wait_ge(G["s_out"], 64)
                for hf in range(2):
                    for d in range(2):
                        blocks = S_[hf * DK:(hf + 1) * DK, 2 * d:2 * d + 2, hf * DK:(hf + 1) * DK]
                        sp.dma_start(blocks, a["state_gdn"][0, ds(l, 1), d, hf::2].rearrange("a c k v -> k (a c) v"))\
                          .then_inc(G["s_in"], 16)
                sp.wait_ge(G["s_in"], 64)
                move_gates(sp, G, 0, range(17, GITEMS))
                gate_moves_done(sp, G, 0)

            @block.tensor
            def _(pe):
                fill = gate_filler(pe, G, gdn_gate_bank)
                fill(9 * KD)
                for c in range(4):
                    pe.wait_ge(G["sq"], c + 1)
                    if c >= 2:
                        pe.wait_ge(G["sqrt"], c - 1)
                    b = bank(2 * (c % 2), 2)
                    nc.tensor.matmul(b[:, 0:512], c_("blockones"), sig[:, c % 2, 0:512], start=True, stop=True)
                    nc.tensor.matmul(b[:, 512:CONV_OUT], c_("blockones"), sig[:, c % 2, 512:CONV_OUT],
                                     start=True, stop=True).then_inc(G["ssq"], 1)
                    fill(KD)
                pe.wait_ge(G["qkn"], 4)
                pe.wait_ge(G["silu"], 6)
                for t in range(NT):
                    if t >= 2:
                        pe.wait_ge(G["tr_done"], t - 1)
                    for c in range(4):
                        ins = nc.tensor.transpose(psum[:, 4 + t % 2, c * P:(c + 1) * P],
                                                  qkv[:, 2 + c, pos(t):pos(t) + P], ident)
                    ins.then_inc(G["tr_ps"], 1)
                    if t in (1, 3):
                        fill(KD)
                pe.wait_ge(G["la"], 1)
                for t in range(NT):
                    for d in range(2):
                        nc.tensor.matmul(psum[:, 0, t * 16 + 4 * d:t * 16 + 4 * d + 4], c_(f"tri{d}"),
                                         la[:, t, 4 * d:4 * d + 4], start=True, stop=True)
                    ins = nc.tensor.matmul(psum[:, 0, t * 16 + 8:t * 16 + 16], ones, la[:, t, :], start=True, stop=True)
                ins.then_inc(G["gcol_ps"], 1)
                pe.wait_ge(G["tr_done"], NT)
                pe.wait_ge(G["gcols"], 1)
                nl = len(LEVELS)

                def decay_rows(step):
                    for d, t in enumerate(tiles_of(step)):
                        for hh in range(H):
                            o = slice(hh * P, (hh + 1) * P)
                            ins = nc.tensor.matmul(psum[:, 4 + d, o],
                                                   la[:, t, 4 * d + hh:4 * d + hh + 1].broadcast_to([P, P]),
                                                   c_(f"tri{d}"), start=True, stop=True)
                        ins.then_inc(G["g_ps"], 1)

                decay_rows(0)
                for step in range(NT):
                    tiles = tiles_of(step)
                    for S_free, first, col in (("s_new", 0, 2), ("o_done", 2, 0)):
                        if step:
                            pe.wait_ge(G[S_free], (8 if first == 0 else 2) * step)
                            pe.wait_ge(G["xt_new"], 2 * nl * step)
                        for d, t in enumerate(tiles):
                            for hh in range(H):
                                base, c = (hh % 2) * DK, hh // 2
                                kt = qkv[base:base + DK, 2 + c, pos(t):pos(t) + P]
                                other = qkv[base:base + DK, col + c, pos(t):pos(t) + P]
                                ins = nc.tensor.matmul(psum[:, first + hh % 2, (2 * d + c) * P:(2 * d + c + 1) * P],
                                                       kt, other, start=True, stop=True)
                        ins.then_inc(G["kk_ps"] if first == 0 else G["kq_ps"], 1)
                    fill(4)
                    for s in range(nl):
                        for d in range(2):
                            n = (step * nl + s) * 2 + d
                            pe.wait_ge(G["bs"], n + 1)
                            if s == 0:
                                pe.wait_ge(G["bt"], 2 * step + 2)
                            if s:
                                pe.wait_ge(G["x_new"], (step * (nl - 1) + s - 1) * 2 + d + 1)
                            for hh in range(H):
                                rhs = ident if s == 0 else X_[:, d, hh, :]
                                ins = nc.tensor.matmul(psum[:, d, hh * P:(hh + 1) * P], bs[:, d, hh, :], rhs,
                                                       start=True, stop=True)
                            ins.then_inc(G["t_ps"], 1)
                        if s == 2 and step < NT - 1:
                            decay_rows(step + 1)
                        fill(2)
                        if s == 0:
                            pe.wait_ge(G["mm"], 2 * step + 2)
                            continue
                        for d in range(2):
                            pe.wait_ge(G["xt_new"], (step * nl + s - 1) * 2 + d + 1)
                            pe.wait_ge(G["t_done"], (step * (nl - 1) + s - 1) * 2 + d + 1)
                            for hh in range(H):
                                o = hh * DK
                                if s < nl - 1:
                                    nc.tensor.matmul(psum[:, 2 + d, o:o + DK], Xt[:, d, hh, :],
                                                     half(T_[:, d, hh, :], s, d), start=True, stop=True)
                                o += 256
                                ins = nc.tensor.matmul(psum[:, 2 + d, o:o + DK], T_[:, d, hh, :],
                                                       half(Xt[:, d, hh, :], s, 1 - d), start=True, stop=True)
                            ins.then_inc(G["u_ps"], 1)
                        fill(2)
                    pe.wait_ge(G["zero"], 1)
                    if step == 1:
                        pe.wait_ge(G["s_in"], 64)
                    for d, t in enumerate(tiles):
                        pe.wait_ge(G["xt_new"], (step * nl + nl - 1) * 2 + d + 1)
                        for c in range(2):
                            nc.tensor.matmul(psum[:, d, c * P:(c + 1) * P], qkv[:, 2 + c, pos(t):pos(t) + P],
                                             S_[:, 2 * d + c, :], start=True, stop=True)
                            ins = nc.tensor.matmul(psum[:, d, 256 + c * P:256 + (c + 1) * P],
                                                   qkv[:, c, pos(t):pos(t) + P], S_[:, 2 * d + c, :],
                                                   start=True, stop=True)
                        ins.then_inc(G["ksqs_ps"], 1)
                    fill(4)
                    for d, t in enumerate(tiles):
                        pe.wait_ge(G["r_new"], 2 * step + d + 1)
                        for hh in range(H):
                            ins = nc.tensor.matmul(psum[:, 2 + d, hh * DK:(hh + 1) * DK], Xt[:, d, hh, :],
                                                   r_[:, d, hh * DK:(hh + 1) * DK], start=True, stop=True)
                        ins.then_inc(G["y_ps"], 1)
                    fill(4)
                    for d, t in enumerate(tiles):
                        pe.wait_ge(G["y_done"], 2 * step + d + 1)
                        pe.wait_ge(G["kd"], 2 * step + d + 1)
                        if step < NT - 1:
                            pe.wait_ge(G["gsub"], H * (2 * step + d + 3))
                        for c in range(2):
                            ins = nc.tensor.matmul(psum[:, 4 + d, c * P:(c + 1) * P], kd_[:, d, c * P:(c + 1) * P],
                                                   y_[:, d, c * P:(c + 1) * P], start=True, stop=True)
                        ins.then_inc(G["st_ps"], 1)
                        for hh in range(H):
                            ins = nc.tensor.matmul(psum[:, 2 + d, 256 + hh * DK:256 + (hh + 1) * DK], mm_[:, d, hh, :],
                                                   y_[:, d, hh * DK:(hh + 1) * DK], start=True, stop=True)
                        ins.then_inc(G["my_ps"], 1)
                    fill(2)

            @block.scalar
            def _(act):
                own = Own(act, G["own_a"])
                evac = gate_evacuator(act, own, G, gdn_gate_bank)
                evac(2)
                for c in range(NQKV):
                    act.wait_ge(G["conv"], c + 1)
                    if c >= 2:
                        act.wait_ge(G["silu"], c - 1)
                    own.tell(nc.scalar.activation(sig[:, c % 2, :], qkv[:, c, :], ACT.Sigmoid), G["sig"])
                    evac(c + 3)
                own.link(nc.scalar.activation(alog, alog, ACT.Exp))
                for c in range(4):
                    act.wait_ge(G["silu"], 6 if c < 2 else 6)
                    if c >= 2:
                        act.wait_ge(G["qkn"], c - 1)
                    own.tell(nc.scalar.activation(sig[:, c % 2, :], qkv[:, c, :], ACT.Square), G["sq"])
                    act.wait_ge(G["ssq"], c + 1)
                    own.tell(nc.scalar.activation(sig[:, c % 2, :], bank(2 * (c % 2), 2)[:, 0:CONV_OUT], ACT.Sqrt,
                                                  bias=eps64_col if c < 2 else eps_col,
                                                  scale=float(DK) if c < 2 else 1.0), G["sqrt"])
                    evac(9 + c)
                act.wait_ge(G["ab_abs"], 1)
                own.link(nc.scalar.activation(abe, abx, ACT.Exp))
                own.tell(nc.scalar.activation(abe, abe, ACT.Ln, bias=one_col), G["ab_exp"])
                for t in range(NT):
                    act.wait_ge(G["tr_ps"], t + 1)
                    own.tell(nc.scalar.activation(kvtok[:, t, :], psum[:, 4 + t % 2, :], ACT.Copy), G["tr_done"])
                    evac(13 + t // 2)
                act.wait_ge(G["gcols"], 1)
                own.link(nc.scalar.activation(eg, gcols[:, :, 0:8], ACT.Exp))
                own.link(nc.scalar.activation(ekd[:, :, 0:8], gbk[:, :, 8:16], ACT.Exp))
                own.tell(nc.scalar.activation(ekd[:, :, 8:16], gcols[:, :, 8:16], ACT.Exp), G["gexps"])
                nl = len(LEVELS)

                def decays(step):
                    for d in range(2):
                        act.wait_ge(G["gsub"], H * (2 * step + d + 1))
                        own.send(nc.scalar.activation(dtm[:, d], dtm[:, d], ACT.Exp), G["dt"])

                decays(0)
                for step in range(NT):
                    for s in range(1, nl):
                        for d in range(2):
                            act.wait_ge(G["t_ps"], (step * nl + s) * 2 + d + 1)
                            if s >= 2:
                                act.wait_ge(G["u_ps"], (step * (nl - 1) + s - 2) * 2 + d + 1)
                            own.send(nc.scalar.activation(T_[:, d].rearrange("p a b -> p (a b)"), psum[:, d, :],
                                                          ACT.Copy), G["t_done"])
                        evac(15 + (40 * step + 4 * s + 2) // KD)
                        if s == 4 and step < NT - 1:
                            decays(step + 1)
                    for d in range(2):
                        act.wait_ge(G["y_ps"], 2 * step + d + 1)
                        own.send(nc.scalar.activation(y_[:, d, :], psum[:, 2 + d, 0:256], ACT.Copy), G["y_done"])
                    evac(15 + 5 * (step + 1))
                evac(GITEMS)
                act.wait_ge(G["oreduced"], 1)
                own.tell(nc.scalar.activation(oss, oss, ACT.Sqrt, bias=eps_col, scale=1.0 / DK), G["ostd"])
                own.tell(nc.scalar.activation(otmp, ptok[:, :, C_GATE:C_GATE + 256], ACT.Sigmoid), G["osig"])

            @block.vector
            def _(v):
                own = Own(v, G["own_v"])
                vec = nc.vector
                v.wait_ge(G["conv_in"], 16 * CONV)
                v.wait_ge(G["tiny_in"], 48)
                own.link(vec.memset(S_, 0.0))
                own.tell(vec.memset(o_all[:, :, 0:256], 0.0), G["zero"])
                for c in range(NQKV):
                    own.link(vec.tensor_scalar(qkv[:, c, :], qpre[:, c, 0:CONV_OUT], conv_w(c, 0), None, ALU.mult))
                    for k in range(1, CONV):
                        ins = vec.scalar_tensor_tensor(qkv[:, c, :], qpre[:, c, k:k + CONV_OUT], conv_w(c, k),
                                                       qkv[:, c, :], ALU.mult, ALU.add)
                        (own.link if k < CONV - 1 else lambda x: own.tell(x, G["conv"]))(ins)
                own.link(vec.tensor_copy(ab, ptok[:, :, C_AB:C_AB + 16]))
                own.link(vec.tensor_tensor(ab[:, :, 0:8], ab[:, :, 0:8], bc(dtb, [NT, 8], 1), ALU.add))
                own.tell(vec.scalar_tensor_tensor(abx, ab, -1.0, ab, ALU.mult, ALU.min), G["ab_abs"])
                v.wait_ge(G["sqrt"], 1)
                for c in range(4):
                    v.wait_ge(G["sqrt"], c + 1)
                    own.link(vec.reciprocal(sig[:, c % 2, :], sig[:, c % 2, :]))
                    own.tell(vec.tensor_tensor(qkv[:, c, :], qkv[:, c, :], sig[:, c % 2, :], ALU.mult), G["qkn"])
                v.wait_ge(G["ab_exp"], 1)
                own.link(vec.scalar_tensor_tensor(la, ab[:, :, 0:8], 0.0, abe[:, :, 0:8], ALU.max, ALU.add))
                own.link(vec.tensor_tensor(la, la, bc(alog, [NT, 8], 1), ALU.mult))
                own.tell(vec.tensor_scalar(la, la, -1.0, None, ALU.mult), G["la"])
                own.link(vec.scalar_tensor_tensor(abx[:, :, 8:16], ab[:, :, 8:16], 0.0, abe[:, :, 8:16],
                                                  ALU.min, ALU.subtract))
                v.wait_ge(G["gcol_ps"], 1)
                own.link(vec.tensor_copy(gcols, psum[:, 0, 0:NT * 16].rearrange("p (t x) -> p t x", t=NT)))
                own.link(vec.tensor_tensor(gbk[:, :, 0:8], gcols[:, :, 0:8], abx[:, :, 8:16], ALU.subtract))
                own.tell(vec.tensor_tensor(gbk[:, :, 8:16], gcols[:, :, 8:16], gbk[:, :, 0:8], ALU.subtract), G["gcols"])
                v.wait_ge(G["gexps"], 1)
                nl = len(LEVELS)

                def decay_exponents(step):
                    for d, t in enumerate(tiles_of(step)):
                        v.wait_ge(G["g_ps"], 2 * step + d + 1)
                        for hh in range(H):
                            own.send(vec.scalar_tensor_tensor(
                                dtm[:, d, hh, :], psum[:, 4 + d, hh * P:(hh + 1) * P],
                                gbk[:, t, 4 * d + hh:4 * d + hh + 1], c_(f"neg{d}"), ALU.subtract, ALU.add), G["gsub"])

                decay_exponents(0)
                for step in range(NT):
                    tiles = tiles_of(step)
                    heads = lambda x: x.rearrange("p (c r) i -> p r c i", r=2)
                    prod = lambda b, d: psum[:, b:b + 2, 2 * d * P:2 * (d + 1) * P].rearrange("p r (c i) -> p r c i", c=2)
                    v.wait_ge(G["dt"], 2 * step + 2)
                    v.wait_ge(G["kk_ps"], step + 1)
                    for d in range(2):
                        own.send(vec.tensor_tensor(heads(bt[:, d]), prod(0, d), heads(dtm[:, d]), ALU.mult), G["bt"])
                    v.wait_ge(G["kq_ps"], step + 1)
                    for d in range(2):
                        own.send(vec.tensor_tensor(heads(mm_[:, d]), prod(2, d), heads(dtm[:, d]), ALU.mult), G["mm"])
                    idb = bc(ident, [H, P], 1)
                    for s in range(nl):
                        if s == 3 and step < NT - 1:
                            own.settle(G["mm"])
                            decay_exponents(step + 1)
                        for d in range(2):
                            if s == 0:
                                v.wait_ge(G["t_ps"], (step * nl) * 2 + d + 1)
                                own.send(vec.tensor_tensor(X_[:, d], idb, psum[:, d, :].rearrange(
                                    "p (a b) -> p a b", a=H), ALU.subtract), G["x_new"])
                                own.send(vec.tensor_tensor(Xt[:, d], idb, bs[:, d], ALU.subtract), G["xt_new"])
                                continue
                            v.wait_ge(G["u_ps"], (step * (nl - 1) + s - 1) * 2 + d + 1)
                            if s < nl - 1:
                                x = halves(X_[:, d], s, d)
                                own.send(vec.tensor_tensor(x, x, blocks(psum[:, 2 + d, 0:256], s), ALU.subtract),
                                         G["x_new"])
                            x = halves(Xt[:, d], s, 1 - d)
                            own.send(vec.tensor_tensor(x, x, blocks(psum[:, 2 + d, 256:512], s), ALU.subtract),
                                     G["xt_new"])
                    hd = lambda x: x.rearrange("p (a b) -> p a b", a=H)
                    for d, t in enumerate(tiles):
                        v.wait_ge(G["ksqs_ps"], 2 * step + d + 1)
                        egb = bc(eg[:, t, 4 * d:4 * d + 4], [H, DK], 2)
                        own.link(vec.tensor_tensor(hd(r_[:, d, :]), hd(psum[:, d, 0:256]), egb, ALU.mult))
                        own.send(vec.tensor_tensor(r_[:, d, :], kvtok[:, t, 256:512], r_[:, d, :], ALU.subtract),
                                 G["r_new"])
                    for d, t in enumerate(tiles):
                        egb = bc(eg[:, t, 4 * d:4 * d + 4], [H, DK], 2)
                        own.link(vec.tensor_tensor(hd(oq[:, d, :]), hd(psum[:, d, 256:512]), egb, ALU.mult))
                    for d, t in enumerate(tiles):
                        v.wait_ge(G["st_ps"], 2 * step + d + 1)
                        if step == 1 and d == 0:
                            v.wait_ge(G["s_in"], 64)
                        for c in range(2):
                            for hf in range(2):
                                q = slice(hf * DK, (hf + 1) * DK)
                                hh = 8 + 4 * d + 2 * c + hf
                                ins = vec.scalar_tensor_tensor(
                                    S_[q, 2 * d + c, q], S_[q, 2 * d + c, q], ekd[q, t, hh:hh + 1],
                                    psum[q, 4 + d, c * P + hf * DK:c * P + (hf + 1) * DK], ALU.mult, ALU.add)
                                own.send(ins, G["s_new"])
                    for d, t in enumerate(tiles):
                        v.wait_ge(G["my_ps"], 2 * step + d + 1)
                        own.link(vec.tensor_tensor(oq[:, d, :], oq[:, d, :], psum[:, 2 + d, 256:512], ALU.add))
                        own.tell(vec.tensor_tensor(o_all[:, t, 0:256], o_all[:, t, 0:256], oq[:, d, :], ALU.add),
                                 G["o_done"])
                oA = lambda t: hd(o_all[:, t, 0:256])
                v.wait_ge(G["osum"], 1)
                own.tell(vec.tensor_reduce(oss, otmp.rearrange("p t (h d) -> p (t h) d", h=H), AX.X, ALU.add),
                         G["oreduced"])
                v.wait_ge(G["ostd"], 1)
                own.link(vec.reciprocal(oss, oss))
                for t in range(NT):
                    own.link(vec.tensor_tensor(oA(t), oA(t), bc(oss[:, t * H:(t + 1) * H], [H, DK], 2), ALU.mult))
                    own.link(vec.tensor_tensor(oA(t), oA(t), bc(gng, [H, DK], 1), ALU.mult))
                    own.link(vec.tensor_tensor(o_all[:, t, 0:256], o_all[:, t, 0:256], ptok[:, t, C_GATE:C_GATE + 256],
                                               ALU.mult))
                v.wait_ge(G["osig"], 1)
                own.tell(vec.tensor_tensor(o_all[:, :, 0:256], o_all[:, :, 0:256], otmp, ALU.mult), G["ofin"])

            @block.gpsimd
            def _(g):
                own = Own(g, G["own_p"])
                for c in range(NQKV):
                    g.wait_ge(G["sig"], c + 1)
                    own.tell(nc.gpsimd.tensor_tensor(qkv[:, c, :], qkv[:, c, :], sig[:, c % 2, :], ALU.mult), G["silu"])
                nl = len(LEVELS)
                g.wait_ge(G["tr_done"], NT)
                g.wait_ge(G["gexps"], 1)
                for step in range(NT):
                    tiles = tiles_of(step)
                    for d, t in enumerate(tiles):
                        if step:
                            g.wait_ge(G["st_ps"], 2 * (step - 1) + d + 1)
                        own.send(nc.gpsimd.tensor_tensor(
                            kd_[:, d, :].rearrange("p (a b) -> p a b", a=H),
                            kvtok[:, t, 0:256].rearrange("p (a b) -> p a b", a=H),
                            bc(ekd[:, t, 4 * d:4 * d + 4], [H, DK], 2), ALU.mult), G["kd"])
                    for s in range(nl):
                        for d in range(2):
                            if s == 0:
                                g.wait_ge(G["bt"], 2 * step + d + 1)
                            else:
                                g.wait_ge(G["t_ps"], (step * nl + s - 1) * 2 + d + 1)
                                if s == 1:
                                    g.wait_ge(G["xt_new"], (step * nl) * 2 + d + 1)
                            own.send(nc.gpsimd.tensor_tensor(bs[:, d], bt[:, d], bc(levels[:, s, d, :], [H, P], 1),
                                                             ALU.mult), G["bs"])
                g.wait_ge(G["o_done"], 2 * NT)
                own.tell(nc.gpsimd.tensor_tensor(otmp, o_all[:, :, 0:256], o_all[:, :, 0:256], ALU.mult), G["osum"])

        QK_COLS = T + P
        qk = ar(g0, 7, QK_COLS)
        vcb, vcd = ar(g0 + 5376, 256), ar(g0 + 5632, 128)
        kcb, kcd = ar(g0 + 5760, 256), ar(g0 + 6016, 128)
        E2 = [ar(g0 + 6144, 2, 640), ar(TMP, 2, 640)]
        PT = [ar(g0 + 7424, 5, P), ar(TMP + 1280, 5, P)]
        ws = ar(g0 + 8064, H, P)
        wsT = ar(g0 + 8576, H, P)
        vn = ar(g0 + 9088, NT, 256)
        qdn = ar(g0 + 10368, NT, 384)
        rt1 = ar(MODB, NT, 512)
        rt2 = ar(MODB + 2560, 512)
        cb, sb_ = (c_(f"{x}_b").rearrange("p (t d) -> p t d", d=32) for x in ("cos", "sin"))
        cd, sd = (c_(f"{x}_d").rearrange("p (t d) -> p t d", d=64) for x in ("cos", "sin"))
        qg, kg = sm(20, DK), sm(84, DK)
        dng, sgn = sm(148, DK), sm(212, 256)
        lamp = sm(468, 4, 32)
        lamc = sm(596, 2)
        lprod = sm(600, 2, 32)
        lsum, neglam = sm(664, 2), sm(666, 1)
        qss = sm(668, NT * 6)
        vss = sm(700, NT)
        bT = sm(706, H)
        mx, lsm, rl = sm(712, 2), sm(766, 2, 2), sm(740, 2, 4)
        dss = sm(720, NT * H)
        SC_B = 32 ** -0.5
        ATT_PRE = 10
        att_gate_bank = lambda i: 6 + i % 2 if i < ATT_PRE else 7
        units = []
        for t in range(NT):
            for j in range(2 * H):
                for u in range(2 if j < H else 1):
                    units.append((t, j, u))
        att_items = [(t, j) for t in range(NT) for j in range(2 * H)]
        units_of = [[n for n, x in enumerate(units) if x[:2] == item] for item in att_items]
        with nc.Block() as block:
            @block.sync
            def _(sp):
                clear(sp, "gdn")
                for dst, src in ((qg, a["gqa_qnorm"]), (kg, a["gqa_knorm"]), (dng, a["diff_norm"]), (sgn, a["sgu_norm"])):
                    sp.dma_start(dst, src[ds(l, 1)].rearrange("a d -> (a d)").partition_broadcast(P)).then_inc(B["in_b"], 16)
                sp.dma_start(sm(468, 128), a["diff_lambda"][ds(l, 1)].rearrange("a i d -> (a i d)")
                             .partition_broadcast(P)).then_inc(B["in_b"], 16)
                sp.dma_start(lamc, a["layer_consts"][ds(l, 1)].rearrange("a p c -> p (a c)")).then_inc(B["in_b"], 16)
                sp.dma_start(bT, a["sgu_b"][ds(l, 1)].rearrange("a g p -> p (a g)"),
                             allow_slow_non_contiguous=True).then_inc(B["in_b"], 16)
                sp.dma_start(ws, a["sgu_ws"][ds(l, 1)].rearrange("a g p q -> p (a g) q")).then_inc(B["in_ws"], 16)
                for dst, src in ((kcb, a["cache_diff_k"]), (vcb, a["cache_diff_v"]), (kcd, a["cache_gqa_k"]),
                                 (vcd, a["cache_gqa_v"])):
                    sp.dma_start(dst, src[0, ds(l, 1)].rearrange("a s h d -> (a s) (h d)")).then_inc(B["in_ws"], 16)
                for dst, src in ((outs["dk"], ptok[:, 0, C_KB:C_KB + 256]), (outs["dv"], ptok[:, 0, C_VB:C_VB + 256]),
                                 (outs["gv"], ptok[:, 0, C_VD:C_VD + 128])):
                    sp.dma_start(dst[0, ds(l, 1)].rearrange("a s h d -> (a s) (h d)"), src).then_inc(B["ctx_out"], 16)
                move_gates(sp, B, GCHUNKS, range(2))
                sp.wait_ge(B["qd_ready"], NT)
                sp.dma_start(outs["gk"][0, ds(l, 1)].rearrange("a s h d -> (a s) (h d)"), qdn[:, 0, 256:384])\
                  .then_inc(B["ctx_out"], 16)
                move_gates(sp, B, GCHUNKS, range(2, GITEMS))
                gate_moves_done(sp, B, GCHUNKS)
                sp.wait_ge(B["ctx_out"], 64)

            @block.tensor
            def _(pe):
                tr = nc.tensor.transpose
                fill = gate_filler(pe, B, att_gate_bank)
                fill(2 * KD)
                pe.wait_ge(B["in_ws"], 80)
                for g in range(H):
                    ins = tr(psum[:, 2, g * P:(g + 1) * P], ws[:, g, :], ident)
                ins.then_inc(B["wt_ps"], 1)
                fill(2 * KD)
                pe.wait_ge(B["wt_done"], 1)
                pe.wait_ge(B["vn"], 1)
                for g in range(H):
                    if g >= 2:
                        pe.wait_ge(B["z_done"], g - 1)
                    nc.tensor.matmul(psum[:, 2 + g % 2, 0:NT * DK], wsT[:, g, :],
                                     vn[:, :, g * DK:(g + 1) * DK], start=True, stop=True).then_inc(B["z_ps"], 1)
                for i, t in enumerate((0, None, 1, 2, 3, 4)):
                    fill(KD)
                    if t is not None:
                        pe.wait_ge(B["roped"], t + 1)
                    if i >= 1:
                        pe.wait_ge(B["tr_done"], i)
                    q4 = lambda k: psum[:, 0, k * P:(k + 1) * P]
                    k3 = lambda k: psum[:, 1, k * P:(k + 1) * P]
                    if t is None:
                        tr(k3(0), kcb[:, 0:P], ident)
                        tr(k3(1), kcb[:, P:2 * P], ident)
                        ins = tr(k3(2), kcd, ident)
                    else:
                        for k in range(2):
                            tr(q4(k), ptok[:, t, C_QB + k * P:C_QB + (k + 1) * P], ident)
                            tr(q4(2 + k), qdn[:, t, k * P:(k + 1) * P], ident)
                            tr(k3(k), ptok[:, t, C_KB + k * P:C_KB + (k + 1) * P], ident)
                        ins = tr(k3(2), qdn[:, t, 256:384], ident)
                    ins.then_inc(B["tr_ps"], 1)
                pe.wait_ge(B["tr_done"], 6)
                pe.wait_ge(B["z_done"], H)
                def scores(i):
                    for n in units_of[i]:
                        t, j, u = units[n]
                        qcol = 0 if t == 0 else P + P * t
                        kcol, nk = (0, P) if t == 0 else (P, 5 * P)
                        if j < H:
                            hh = 2 * j + u
                            chunk, kchunk, base, w = hh // 4, 4 + hh // 4, 32 * (hh % 4), 32
                        else:
                            g = j - H
                            chunk, kchunk, base, w = 2 + g % 2, 6, DK * (g // 2), DK
                        if n >= 2:
                            pe.wait_ge(B["e"], n - 1)
                        ps = bank(2 * (n % 2), 2)
                        q = qk[base:base + w, chunk, qcol:qcol + P]
                        for k0 in range(0, nk, 512):
                            k1 = min(k0 + 512, nk)
                            ins = nc.tensor.matmul(ps[:, k0:k1], q, qk[base:base + w, kchunk, kcol + k0:kcol + k1],
                                                   start=True, stop=True)
                        ins.then_inc(B["sc_ps"], 1)

                def turn_p(i):
                    t, j = att_items[i]
                    if j < H:
                        pe.wait_ge(B["comb"], t * H + j + 1)
                    else:
                        pe.wait_ge(B["e"], units_of[i][-1] + 1)
                    if i:
                        pe.wait_ge(B["pt_done"], i)
                    for k in range(1 if t == 0 else 5):
                        ins = tr(bank(4, 2)[:, k * P:(k + 1) * P], E2[i % 2][:, 0, k * P:(k + 1) * P], ident)
                    ins.then_inc(B["pt_ps"], 1)

                def values(i):
                    t, j = att_items[i]
                    nkt = 1 if t == 0 else 5
                    pe.wait_ge(B["pt_done"], i + 1)
                    if i:
                        pe.wait_ge(B["o_done"], i)
                    else:
                        pe.wait_ge(B["gl_done"], ATT_PRE)
                    for k in range(nkt):
                        if j < H:
                            val = (vcb if t and k == 0 else ptok[:, k, C_VB:C_VB + 256])[:, j * DK:(j + 1) * DK]
                        else:
                            kv = (j - H) // 2
                            val = (vcd if t and k == 0 else ptok[:, k, C_VD:C_VD + 128])[:, kv * DK:(kv + 1) * DK]
                        ins = nc.tensor.matmul(psum[:, 6, 0:DK], PT[i % 2][:, k, :], val,
                                               start=(k == 0), stop=(k == nkt - 1))
                    ins.then_inc(B["o_ps"], 1)

                scores(0)
                for i in range(len(att_items) + 1):
                    if i + 1 < len(att_items):
                        scores(i + 1)
                    if ATT_PRE <= i < len(att_items):
                        fill(KD // 2)
                    if i < len(att_items):
                        turn_p(i)
                    if ATT_PRE <= i < len(att_items):
                        fill(KD // 2)
                    if i:
                        values(i - 1)

            @block.scalar
            def _(act):
                own = Own(act, B["own_a"])
                evac = gate_evacuator(act, own, B, att_gate_bank)
                act.wait_ge(B["in_b"], 16 * 7)
                act.wait_ge(B["lam_e"], 1)
                own.tell(nc.scalar.activation(lsum, lsum, ACT.Exp), B["lam"])
                act.wait_ge(B["rstd_in"], 1)
                own.link(nc.scalar.activation(qss, qss, ACT.Sqrt, bias=eps_col, scale=1.0 / DK))
                act.wait_ge(B["vss"], 1)
                own.tell(nc.scalar.activation(vss, vss, ACT.Sqrt, bias=eps_col, scale=1.0 / 256), B["rstd"])
                evac(2)
                act.wait_ge(B["wt_ps"], 1)
                own.tell(nc.scalar.activation(wsT, psum[:, 2, :].rearrange("p (a b) -> p a b", a=H), ACT.Copy),
                         B["wt_done"])
                evac(4)
                for i in range(6):
                    act.wait_ge(B["tr_ps"], i + 1)
                    cols = slice(i * P, (i + 1) * P)
                    if i != 1:
                        own.link(nc.scalar.activation(qk[:, 0:2, cols], psum[:, 0, 0:256]
                                                      .rearrange("p (a b) -> p a b", a=2), ACT.Copy, scale=SC_B))
                        own.link(nc.scalar.activation(qk[:, 2:4, cols], psum[:, 0, 256:512]
                                                      .rearrange("p (a b) -> p a b", a=2), ACT.Copy, scale=DK ** -0.5))
                    own.tell(nc.scalar.activation(qk[:, 4:7, cols], psum[:, 1, 0:384]
                                                  .rearrange("p (a b) -> p a b", a=3), ACT.Copy), B["tr_done"])
                    evac(5 + i)

                def exps(i):
                    for u, n in enumerate(units_of[i]):
                        nk = P if units[n][0] == 0 else 5 * P
                        act.wait_ge(B["mx"], n + 1)
                        if i >= 2:
                            act.wait_ge(B["pt_ps"], i - 1)
                            act.wait_ge(B["rl"], i - 1)
                        own.send(nc.scalar.activation(E2[i % 2][:, u, 0:nk], bank(2 * (n % 2), 2)[:, 0:nk], ACT.Exp,
                                                      bias=mx[:, n % 2:n % 2 + 1], accum_out=lsm[:, i % 2, u:u + 1]),
                                 B["e"])

                exps(0)
                for i, (t, j) in enumerate(att_items):
                    nk = P if t == 0 else 5 * P
                    if i + 1 < len(att_items):
                        exps(i + 1)
                    act.wait_ge(B["pt_ps"], i + 1)
                    if i >= 2:
                        act.wait_ge(B["o_ps"], i - 1)
                    own.send(nc.scalar.activation(PT[i % 2][:, 0:nk // P, :].rearrange("p a b -> p (a b)"),
                                                  bank(4, 2)[:, 0:nk], ACT.Copy), B["pt_done"])
                    if i >= ATT_PRE:
                        evac(i + 1)
                act.wait_ge(B["ssd"], 1)
                own.tell(nc.scalar.activation(dss, dss, ACT.Sqrt, bias=eps_col, scale=1.0 / DK), B["sstd"])

            @block.vector
            def _(v):
                own = Own(v, B["own_v"])
                vec = nc.vector
                v.wait_ge(B["in_b"], 16 * 7)
                own.link(vec.tensor_tensor(lprod, lamp[:, 0::2, :], lamp[:, 1::2, :], ALU.mult))
                own.tell(vec.tensor_reduce(lsum, lprod, AX.X, ALU.add), B["lam_e"])
                v.wait_ge(B["lam"], 1)
                own.link(vec.tensor_tensor(neglam, lsum[:, 1:2], lsum[:, 0:1], ALU.subtract))
                own.link(vec.tensor_tensor(neglam, neglam, lamc[:, 0:1], ALU.subtract))
                own.link(vec.tensor_scalar(dng, dng, lamc[:, 1:2], None, ALU.mult))
                v.wait_ge(B["sq"], 1)
                own.tell(vec.tensor_reduce(qss, rt1[:, :, 0:384].rearrange("p t (h d) -> p t h d", h=6), AX.X, ALU.add),
                         B["rstd_in"])
                own.link(vec.tensor_tensor(vn, ptok[:, :, C_V:C_V + 256], ptok[:, :, C_V:C_V + 256], ALU.mult))
                own.tell(vec.tensor_reduce(vss, vn, AX.X, ALU.add), B["vss"])
                v.wait_ge(B["rstd"], 1)
                own.link(vec.reciprocal(qss, qss))
                own.link(vec.reciprocal(vss, vss))
                for t in range(NT):
                    x = ptok[:, t, C_QD:C_QD + 384].rearrange("p (h d) -> p h d", h=6)
                    own.link(vec.tensor_tensor(x, x, bc(qss[:, t * 6:(t + 1) * 6], [6, DK], 2), ALU.mult))
                    xq = ptok[:, t, C_QD:C_QD + 256].rearrange("p (a c d) -> p a c d", a=2, c=2)
                    oq_ = qdn[:, t, 0:256].rearrange("p (c a d) -> p a c d", a=2, c=2)
                    own.link(vec.tensor_tensor(oq_, xq, qg.unsqueeze(1).unsqueeze(1).broadcast_to([P, 2, 2, DK]),
                                               ALU.mult))
                    own.tell(vec.tensor_tensor(qdn[:, t, 256:384].rearrange("p (h d) -> p h d", h=2), x[:, 4:6, :],
                                               bc(kg, [2, DK], 1), ALU.mult), B["qd_ready"])
                for t in range(NT):
                    own.link(vec.scalar_tensor_tensor(vn[:, t, :], ptok[:, t, C_V:C_V + 256], vss[:, t:t + 1], sgn,
                                                      ALU.mult, ALU.mult))
                own.tell(vec.memset(rl[:, 0, 3:4], 0.0), B["vn"])
                for g in range(H):
                    v.wait_ge(B["z_ps"], g + 1)
                    own.tell(vec.scalar_tensor_tensor(
                        o_all[:, :, 512 + g * DK:512 + (g + 1) * DK],
                        psum[:, 2 + g % 2, 0:NT * DK].rearrange("p (t d) -> p t d", t=NT), bT[:, g:g + 1],
                        ptok[:, :, C_U + g * DK:C_U + (g + 1) * DK], ALU.add, ALU.mult), B["z_done"])

                def maxima(i):
                    for n in units_of[i]:
                        nk = P if units[n][0] == 0 else 5 * P
                        v.wait_ge(B["sc_ps"], n + 1)
                        if n >= 2:
                            v.wait_ge(B["e"], n - 1)
                        own.send(vec.tensor_reduce(mx[:, n % 2:n % 2 + 1], bank(2 * (n % 2), 2)[:, 0:nk], AX.X,
                                                   ALU.max, negate=True), B["mx"])

                def combine(i):
                    t, j = att_items[i]
                    nk = P if t == 0 else 5 * P
                    v.wait_ge(B["e"], units_of[i][-1] + 1)
                    if i >= 2:
                        v.wait_ge(B["o_done"], i - 1)
                    r, sums, E_ = rl[:, i % 2, :], lsm[:, i % 2, :], E2[i % 2]
                    if j < H:
                        own.link(vec.reciprocal(r[:, 0:2], sums))
                        own.tell(vec.scalar_tensor_tensor(r[:, 2:3], sums[:, 0:1], r[:, 1:2], neglam,
                                                          ALU.mult, ALU.mult), B["rl"])
                        own.send(vec.scalar_tensor_tensor(E_[:, 0, 0:nk], E_[:, 1, 0:nk], r[:, 2:3], E_[:, 0, 0:nk],
                                                          ALU.mult, ALU.add), B["comb"])
                    else:
                        own.tell(vec.reciprocal(r[:, 0:1], sums[:, 0:1]), B["rl"])

                def outputs(i):
                    t, j = att_items[i]
                    v.wait_ge(B["o_ps"], i + 1)
                    at = (256 + j * DK) if j < H else (768 + (j - H) * DK)
                    own.send(vec.tensor_scalar(o_all[:, t, at:at + DK], psum[:, 6, 0:DK], rl[:, i % 2, 0:1],
                                               None, ALU.mult), B["o_done"])

                maxima(0)
                for i in range(len(att_items) + 1):
                    if i + 1 < len(att_items):
                        maxima(i + 1)
                    if i < len(att_items):
                        combine(i)
                    if i:
                        outputs(i - 1)
                own.settle(B["o_done"])
                own.link(vec.tensor_tensor(vn, o_all[:, :, 256:512], o_all[:, :, 256:512], ALU.mult))
                own.tell(vec.tensor_reduce(dss, vn.rearrange("p t (h d) -> p (t h) d", h=H), AX.X, ALU.add), B["ssd"])
                v.wait_ge(B["sstd"], 1)
                own.link(vec.reciprocal(dss, dss))
                for t in range(NT):
                    x = o_all[:, t, 256:512].rearrange("p (h d) -> p h d", h=H)
                    own.link(vec.tensor_tensor(x, x, bc(dss[:, t * H:(t + 1) * H], [H, DK], 2), ALU.mult))
                    own.link(vec.tensor_tensor(x, x, bc(dng, [H, DK], 1), ALU.mult))

            @block.gpsimd
            def _(g):
                own = Own(g, B["own_p"])
                gt = nc.gpsimd.tensor_tensor
                own.tell(gt(rt1[:, :, 0:384], ptok[:, :, C_QD:C_QD + 384], ptok[:, :, C_QD:C_QD + 384], ALU.mult), B["sq"])
                g.wait_ge(B["rstd_in"], 1)
                g.wait_ge(B["qd_ready"], 1)
                own.tell(nc.gpsimd.memset(rt2[:, 0:1], 0.0), B["roped"])
                for t in range(1, NT):
                    for heads, d, x, co, si in ((16, 32, ptok[:, t, C_QB:C_QB + 512], cb, sb_),
                                                (6, 64, qdn[:, t, :], cd, sd)):
                        if heads == 6:
                            g.wait_ge(B["qd_ready"], t + 1)
                        w, nf = heads * d, d // 4
                        p1 = rt1[:, 0, 0:w]
                        own.link(gt(p1.rearrange("p (h d) -> p h d", h=heads), x.rearrange("p (h d) -> p h d", h=heads),
                                    bc(co[:, t - 1, :], [heads, d], 1), ALU.mult))
                        x5 = x.rearrange("p (h f s n) -> p h f s n", h=heads, f=2, s=2)
                        o5 = rt2[:, 0:w].rearrange("p (h f s n) -> p h f s n", h=heads, f=2, s=2)
                        s4 = si[:, t - 1, :].rearrange("p (f s n) -> p f s n", f=2, s=2)
                        for sw in range(2):
                            own.link(gt(o5[:, :, :, sw, :], x5[:, :, :, 1 - sw, :],
                                        bc(s4[:, :, sw, :], [heads, 2, nf], 1), ALU.mult))
                        ins = gt(x, p1, rt2[:, 0:w], ALU.add)
                        if heads == 6:
                            own.tell(ins, B["roped"])
                        else:
                            own.link(ins)

        merged = ar(MERGED, NT, D)
        oT = ar(OT, KD, T)
        wbr = [ar(RING + i * 1024, 2, 512) for i in range(2)]
        lgt = [ar(RING + 2048 + i * NT * 512, NT, 512) for i in range(3)]
        sg = ar(RING + 2048 + 3 * NT * 512, 2, 512)
        wout = ar(QPRE, KD, D)
        pr = ar(TMP, 2, 512)
        wM, lM = [M["wa0"], M["wa1"]], [M["lg0"], M["lg1"], M["lg2"]]
        gparts = [(n, c, t) for c in range(2) for n in range(H) for t in range(NT)]
        with nc.Block() as block:
            @block.sync
            def _(sp):
                clear(sp, "att")
                for i in range(2 * H):
                    c, n = i // H, i % H
                    if i >= 2:
                        sp.wait_ge(M["up_ps"], NT * (i - 1))
                    sp.dma_start(wbr[i % 2], a["w_branch"][ds(l, 1), n, :, c * 512:(c + 1) * 512]
                                 .rearrange("a (k p) n -> p (a k) n", p=P)).then_inc(wM[i % 2], 16)
                    if i >= 3:
                        sp.wait_ge(M["sig"], NT * (i - 2))
                    at = n * D + c * 512
                    sp.dma_start(lgt[i % 3], gate_rows[:, :, at:at + 512].rearrange("t p n -> p t n"))\
                      .then_inc(lM[i % 3], 16)
                    if i == 2:
                        for st in range(2):
                            sp.dma_start(modb[:, st, :], mod_rows[st, 2 * D:3 * D].partition_broadcast(P))\
                              .then_inc(M["g1"], 16)
                        sp.dma_start(h[:, :, :], h_rows).then_inc(M["h_in"], 16)
                        sp.wait_ge(M["tr_done"], NT)
                        sp.dma_start(wout, a["w_out"][ds(l, 1)].rearrange("a (k p) n -> p (a k) n", p=P))\
                          .then_inc(M["wo"], 16)

            @block.tensor
            def _(pe):
                def turn(src, t, S_done, S_ps):
                    if t >= 2:
                        pe.wait_ge(S_done, t - 1)
                    for k in range(KD):
                        ins = nc.tensor.transpose(bank(2 * (t % 2), 2)[:, k * P:(k + 1) * P],
                                                  src[:, t, k * P:(k + 1) * P], ident)
                    ins.then_inc(S_ps, 1)

                def branch_up(i):
                    n, c, t = gparts[i]
                    slot = (i // NT) % 2
                    if t == 0:
                        pe.wait_ge(wM[slot], 16 * (i // NT // 2 + 1))
                    if i >= 4:
                        pe.wait_ge(M["prod"], i - 3)
                    for k in range(2):
                        ins = nc.tensor.matmul(psum[:, 4 + i % 4, :], oT[:, 2 * n + k, t * P:(t + 1) * P],
                                               wbr[slot][:, k, :], start=(k == 0), stop=(k == 1))
                    ins.then_inc(M["up_ps"], 1)

                def output(i):
                    c, t = i // NT, i % NT
                    if i >= 2:
                        pe.wait_ge(M["gprod"], i - 1)
                    for k in range(KD):
                        ins = nc.tensor.matmul(psum[:, 4 + i % 2, :], xt[:, k, t * P:(t + 1) * P],
                                               wout[:, k, c * 512:(c + 1) * 512], start=(k == 0), stop=(k == KD - 1))
                    ins.then_inc(M["out_ps"], 1)

                turn(o_all, 0, M["tr_done"], M["tr_ps"])
                for i in range(len(gparts)):
                    if i + 1 < NT:
                        turn(o_all, i + 1, M["tr_done"], M["tr_ps"])
                    if i < NT:
                        pe.wait_ge(M["tr_done"], i + 1)
                    branch_up(i)
                for i in range(-1, 2 * NT):
                    if i + 1 < NT:
                        pe.wait_ge(M["sum"], len(gparts) - NT + i + 2)
                        turn(merged, i + 1, M["mt_done"], M["mt_ps"])
                    if i < 0:
                        continue
                    if i < NT:
                        pe.wait_ge(M["mt_done"], i + 1)
                    if i == 0:
                        pe.wait_ge(M["wo"], 16)
                    output(i)

            @block.scalar
            def _(act):
                own = Own(act, M["own_a"])
                for dst, S_ps, S_done in ((oT, M["tr_ps"], M["tr_done"]), (None, None, None), (xt, M["mt_ps"], M["mt_done"])):
                    if dst is None:
                        for i in range(len(gparts)):
                            j = i // NT
                            act.wait_ge(lM[j % 3], 16 * (j // 3 + 1))
                            if i >= 2:
                                act.wait_ge(M["prod"], i - 1)
                            own.send(nc.scalar.activation(sg[:, i % 2, :], lgt[j % 3][:, i % NT, :], ACT.Sigmoid), M["sig"])
                        continue
                    for t in range(NT):
                        act.wait_ge(S_ps, t + 1)
                        own.tell(nc.scalar.activation(dst[:, :, t * P:(t + 1) * P],
                                                      bank(2 * (t % 2), 2).rearrange("p (k t) -> p k t", k=KD),
                                                      ACT.Copy), S_done)

            @block.vector
            def _(v):
                own = Own(v, M["own_v"])
                for i, (n, c, t) in enumerate(gparts):
                    v.wait_ge(M["sig"], i + 1)
                    v.wait_ge(M["up_ps"], i + 1)
                    if i >= 2:
                        v.wait_ge(M["sum"], i - 1)
                    own.send(nc.vector.tensor_tensor(pr[:, i % 2, :], sg[:, i % 2, :], psum[:, 4 + i % 4, :], ALU.mult),
                             M["prod"])
                v.wait_ge(M["g1"], 32)
                v.wait_ge(M["h_in"], 16)
                v.wait_ge(M["sum"], len(gparts))
                for i in range(2 * NT):
                    c, t = i // NT, i % NT
                    v.wait_ge(M["out_ps"], i + 1)
                    own.tell(nc.vector.tensor_tensor(pr[:, i % 2, :], psum[:, 4 + i % 2, :],
                                                     modb[:, 0 if t == 0 else 1, c * 512:(c + 1) * 512], ALU.mult),
                             M["gprod"])
                    own.link(nc.vector.tensor_tensor(h[:, t, c * 512:(c + 1) * 512], h[:, t, c * 512:(c + 1) * 512],
                                                     pr[:, i % 2, :], ALU.add))

            @block.gpsimd
            def _(g):
                own = Own(g, M["own_p"])
                for i, (n, c, t) in enumerate(gparts):
                    g.wait_ge(M["prod"], i + 1)
                    dst = merged[:, t, c * 512:(c + 1) * 512]
                    if n == 0:
                        own.send(nc.gpsimd.tensor_copy(dst, pr[:, i % 2, :]), M["sum"])
                    else:
                        g.wait_ge(M["sum"], i - NT + 1)
                        own.send(nc.gpsimd.tensor_tensor(dst, dst, pr[:, i % 2, :], ALU.add), M["sum"])

        xm5 = ar(PTOK, NT, D)
        wge = ar(RING, KD, 20)
        junk2 = ar(OALL, NT, D)
        lg = sm(20, NT, 20)
        bge = sm(120, 20)
        m4, oh_g = sm(140, NT, 4), sm(160, NT, 4)
        gmax, gsum = sm(180, NT), sm(185, NT)
        ein, oh1, oh2 = sm(190, NT, 4), sm(210, NT, 4), sm(230, NT, 4)
        v1, v2, ee = sm(250, NT), sm(255, NT), sm(260, NT)
        wtop = sm(266, NT, 2)
        e16 = sm(280, NT, 16)
        sel1, sel2, assign = sm(360, NT, 16), sm(440, NT, 16), sm(520, NT, 16)
        slot_f = sm(600, NT, 16)
        tiles_e, cum, cum2 = sm(680, 16), sm(696, 16), sm(712, 16)
        stile = sm(728, NT * 2)
        cmp_ = ar(TMP, MT, 16)
        texp = sm(740, MT)
        with nc.Block() as block:
            @block.sync
            def _(sp):
                clear(sp, "merge")
                load_modb(sp, R["modb"], 4, 3)
                sp.dma_start(wge[:, :, 0:4], a["moe_wg"][ds(l, 1)].rearrange("a (k p) n -> p (a k) n", p=P)).then_inc(R["w_in"], 16)
                sp.dma_start(wge[:, :, 4:20], a["moe_we"][ds(l, 1)].rearrange("a (k p) n -> p (a k) n", p=P)).then_inc(R["w_in"], 16)
                sp.dma_start(bge[:, 0:4], a["moe_bg"][ds(l, 1)].rearrange("a n -> (a n)").partition_broadcast(P)).then_inc(R["w_in"], 16)
                sp.dma_start(bge[:, 4:20], a["moe_be"][ds(l, 1)].rearrange("a n -> (a n)").partition_broadcast(P)).then_inc(R["w_in"], 16)
                for t in range(NT):
                    sp.wait_ge(R["xm"], t + 1)
                    sp.dma_start(tok_rows[t * P:(t + 1) * P, :], xm5[:, t, :]).then_inc(R["stored"], 16)
                sp.wait_ge(R["stored"], 16 * NT)

            @block.tensor
            def _(pe):
                for t in range(NT):
                    pe.wait_ge(R["xm"], t + 1)
                    if t >= 2:
                        pe.wait_ge(R["xt_done"], t - 1)
                    for k in range(KD):
                        ins = nc.tensor.transpose(bank(2 * (t % 2), 2)[:, k * P:(k + 1) * P],
                                                  xm5[:, t, k * P:(k + 1) * P], ident)
                    ins.then_inc(R["xt_ps"], 1)
                pe.wait_ge(R["xt_done"], NT)
                pe.wait_ge(R["w_in"], 64)
                for t in range(NT):
                    for k in range(KD):
                        ins = nc.tensor.matmul(psum[:, 4, t * 20:(t + 1) * 20], xt[:, k, t * P:(t + 1) * P],
                                               wge[:, k, :], start=(k == 0), stop=(k == KD - 1))
                ins.then_inc(R["lg_ps"], 1)
                pe.wait_ge(R["assign"], 1)
                for t in range(NT):
                    o = psum[:, 5, t * 16:(t + 1) * 16]
                    for t2 in range(t):
                        nc.tensor.matmul(o, ones, assign[:, t2, :], start=(t2 == 0), stop=False)
                    nc.tensor.matmul(o, c_("before"), assign[:, t, :], start=(t == 0), stop=True)
                for t in range(NT):
                    ins = nc.tensor.matmul(psum[:, 5, NT * 16:(NT + 1) * 16], ones, assign[:, t, :],
                                           start=(t == 0), stop=(t == NT - 1))
                ins.then_inc(R["rank_ps"], 1)

            @block.scalar
            def _(act):
                own = Own(act, R["own_a"])
                for t in range(NT):
                    own.send(nc.scalar.activation(junk2[:, t, :], h[:, t, :], ACT.Square, accum_out=ss[:, t:t + 1]), R["own_a"])
                own.settle(R["own_a"])
                own.tell(nc.scalar.activation(rstd, ss, ACT.Sqrt, bias=eps_col, scale=1.0 / D), R["std"])
                for t in range(NT):
                    act.wait_ge(R["xt_ps"], t + 1)
                    own.tell(nc.scalar.activation(xt[:, :, t * P:(t + 1) * P],
                                                  bank(2 * (t % 2), 2).rearrange("p (k t) -> p k t", k=KD), ACT.Copy),
                             R["xt_done"])
                act.wait_ge(R["e_in"], 1)
                own.tell(nc.scalar.activation(m4, m4, ACT.Exp), R["e_out"])
                act.wait_ge(R["e2_in"], 1)
                own.tell(nc.scalar.activation(ee, ee, ACT.Exp), R["e2_out"])

            @block.vector
            def _(v):
                own = Own(v, R["own_v"])
                vec, link = nc.vector, own.link
                v.wait_ge(R["std"], 1)
                link(vec.reciprocal(rstd, rstd))
                v.wait_ge(R["modb"], 64)
                for t in range(NT):
                    st = 0 if t == 0 else 1
                    link(vec.scalar_tensor_tensor(xm5[:, t, :], h[:, t, :], rstd[:, t:t + 1], modb[:, st, :],
                                                  ALU.mult, ALU.mult))
                    own.tell(vec.tensor_tensor(xm5[:, t, :], xm5[:, t, :], modb[:, 2 + st, :], ALU.add), R["xm"])
                v.wait_ge(R["w_in"], 64)
                v.wait_ge(R["lg_ps"], 1)
                link(vec.tensor_tensor(lg, psum[:, 4, 0:NT * 20].rearrange("p (t n) -> p t n", t=NT),
                                       bc(bge, [NT, 20], 1), ALU.add))
                first = bc(c_("first"), [NT, 4], 1)

                def argmax(onehot, x, top):
                    link(vec.tensor_reduce(top, x, AX.X, ALU.max))
                    link(vec.tensor_tensor(onehot, x, bc(top, [NT, 4], 2), ALU.is_equal))
                    link(vec.tensor_tensor(onehot, onehot, first, ALU.mult))
                    link(vec.tensor_reduce(gsum, onehot, AX.X, ALU.max))
                    link(vec.tensor_tensor(onehot, onehot, bc(gsum, [NT, 4], 2), ALU.is_equal))

                gl = lg[:, :, 0:4]
                argmax(oh_g, gl, gmax)
                own.tell(vec.tensor_tensor(m4, gl, bc(gmax, [NT, 4], 2), ALU.subtract), R["e_in"])
                el = lg[:, :, 4:20].rearrange("p t (g e) -> p t g e", g=NG)
                for t in range(NT):
                    link(vec.tensor_tensor(e16[:, t, :].rearrange("p (g e) -> p g e", g=NG), el[:, t],
                                           bc(oh_g[:, t, :], [NG, EPG], 2), ALU.mult))
                link(vec.tensor_reduce(ein, e16.rearrange("p t (g e) -> p t e g", g=NG), AX.X, ALU.add))
                argmax(oh1, ein, v1)
                link(vec.scalar_tensor_tensor(ein, oh1, -BIG, ein, ALU.mult, ALU.add))
                argmax(oh2, ein, v2)
                own.tell(vec.tensor_tensor(ee, v2, v1, ALU.subtract), R["e2_in"])
                v.wait_ge(R["e_out"], 1)
                link(vec.tensor_reduce(gsum, m4, AX.X, ALU.add))
                v.wait_ge(R["e2_out"], 1)
                link(vec.tensor_scalar(v1, ee, 1.0, None, ALU.add))
                link(vec.tensor_tensor(v1, v1, gsum, ALU.mult))
                link(vec.reciprocal(v1, v1))
                link(vec.tensor_copy(wtop[:, :, 0], v1))
                link(vec.tensor_tensor(wtop[:, :, 1], v1, ee, ALU.mult))
                for sel, oh in ((sel1, oh1), (sel2, oh2)):
                    for t in range(NT):
                        link(vec.tensor_tensor(sel[:, t, :].rearrange("p (g e) -> p g e", g=NG),
                                               bc(oh_g[:, t, :], [NG, EPG], 2), bc(oh[:, t, :], [NG, EPG], 1), ALU.mult))
                own.tell(vec.tensor_tensor(assign, sel1, sel2, ALU.add), R["assign"])
                v.wait_ge(R["rank_ps"], 1)
                link(vec.tensor_copy(slot_f, psum[:, 5, 0:NT * 16].rearrange("p (t e) -> p t e", t=NT)))
                link(vec.tensor_copy(cum2, psum[:, 5, NT * 16:(NT + 1) * 16]))
                link(vec.tensor_scalar(tiles_e, cum2, 0.0, None, ALU.is_gt))
                for k in range(1, NT):
                    link(vec.scalar_tensor_tensor(tiles_e, cum2, float(k * P), tiles_e, ALU.is_gt, ALU.add))
                link(vec.tensor_copy(cum, tiles_e))
                bufs = [cum, cum2]
                for i, sh in enumerate((1, 2, 4, 8)):
                    x, y = bufs[i % 2], bufs[1 - i % 2]
                    link(vec.tensor_copy(y[:, 0:sh], x[:, 0:sh]))
                    link(vec.tensor_tensor(y[:, sh:16], x[:, sh:16], x[:, 0:16 - sh], ALU.add))
                link(vec.tensor_tensor(cum2, cum, tiles_e, ALU.subtract))
                link(vec.tensor_scalar(cum2, cum2, float(P), None, ALU.mult))
                link(vec.tensor_tensor(slot_f, slot_f, bc(cum2, [NT, 16], 1), ALU.add))
                for k, sel in enumerate((sel1, sel2)):
                    link(vec.tensor_tensor(e16, slot_f, sel, ALU.mult))
                    link(vec.tensor_reduce(stile[:, k * NT:(k + 1) * NT], e16, AX.X, ALU.add))
                link(vec.tensor_copy(slots[:, :], stile))
                own.tell(vec.tensor_copy(slot_col[:, :, 0], slots[:, :]), R["slots"])
                link(vec.tensor_tensor(cmp_, bc(c_("tile_no"), [MT, 16], 2), bc(cum, [MT, 16], 1), ALU.is_ge))
                link(vec.tensor_reduce(texp, cmp_, AX.X, ALU.add))
                link(vec.tensor_scalar(texp, texp, float(NE - 1), None, ALU.min))
                link(vec.tensor_copy(tile_expert[:, :], texp))

            @block.gpsimd
            def _(g):
                g.wait_ge(R["slots"], 1)
                for k in range(2):
                    for t in range(NT):
                        nc.gpsimd.indirect_dma_start(
                            out=slot_table, out_offset=bass.IndirectOffsetOnAxis(ap=slot_col[:, k * NT + t, :], axis=0),
                            in_=ids[:, t:t + 1], in_offset=None).then_inc(Q["scat"], 16)
                g.wait_ge(Q["scat"], 16 * 2 * NT)
                forget(g, "scatter")

        U = 5
        wslot = [ar(u * 6144, 6144) for u in range(U)]
        xg = ar(30720, 2, D)
        xgT = ar(32768, 2, D)
        hT = ar(34816, 2, 256)
        sgx = ar(35328, 2, 256)
        yv = ar(35840, 2, D)
        fin = [ar(i * D, D) for i in range(8)]
        g2b = ar(8 * D, 2, D)
        wX = [X["w0"], X["w1"], X["w2"], X["w3"], X["w4"]]
        gX = [Q["g0"], Q["g1"]]
        stX = [X["st0"], X["st1"]]
        fX = [Q["f0"], Q["f1"], Q["f2"], Q["f3"]]
        C, CY = 2, U
        PER = (3, 2)

        def free(j, u):
            return j if u == 0 else j - 1

        with nc.Block() as block:
            @block.sync
            def _(sp):
                clear(sp, "route")
                clear(sp, "scatter")
                sp.dma_start(slot_ids, slot_table.rearrange("(j p) o -> p (j o)", p=P),
                             allow_slow_non_contiguous=True).then_inc(X["ids_in"], 16)
                with sp.Fori(0, MT // U) as i:
                    for u in range(U):
                        e = sp.value_load(tile_expert[0:1, ds(i * U + u, 1)], min_val=0, max_val=NE - 1)
                        sp.wait_ge(X["y_ps"], i * U + u + 1)
                        w = wslot[u]
                        w13 = w[:, 0:4096].rearrange("p (k n) -> p k n", k=KD)
                        sp.dma_start(w13[:, :, 0:FE], a["moe_w1"][ds(l, 1), ds(e, 1)]
                                     .rearrange("a e (k p) n -> p (a e k) n", p=P)).then_inc(wX[u], 16)
                        sp.dma_start(w13[:, :, FE:2 * FE], a["moe_w3"][ds(l, 1), ds(e, 1)]
                                     .rearrange("a e (k p) n -> p (a e k) n", p=P)).then_inc(wX[u], 16)
                        sp.dma_start(w[:, 4096:6144].rearrange("p (k n) -> p k n", k=2), a["moe_w2"][ds(l, 1), ds(e, 1)]
                                     .rearrange("a e (k p) n -> p (a e k) n", p=P)).then_inc(wX[u], 16)
                sp.wait_ge(X["y_ps"], MT + CY)
                for st in range(2):
                    sp.dma_start(g2b[:, st, :], mod_rows[st, 5 * D:6 * D].partition_broadcast(P)).then_inc(X["g2"], 16)

            @block.gpsimd
            def _(g):
                g.wait_ge(X["ids_in"], 16)
                for j in range(MT):
                    u = j % U
                    g.wait_ge(X["xt_ps"], free(j, u) + C)
                    nc.gpsimd.indirect_dma_start(
                        out=xg[:, u % 2, :], out_offset=None, in_=tok_rows,
                        in_offset=bass.IndirectOffsetOnAxis(ap=slot_cols[:, j, :], axis=0)).then_inc(gX[u % 2], 16)
                for b in range(2):
                    g.wait_ge(stX[b], 16 * (PER[b] * (MT // U) + 1))
                for t in range(NT):
                    if t == 4:
                        g.wait_ge(X["fused"], 1)
                    for k in range(2):
                        nc.gpsimd.indirect_dma_start(
                            out=fin[2 * (t % 4) + k], out_offset=None, in_=y_rows,
                            in_offset=bass.IndirectOffsetOnAxis(ap=slot_col[:, k * NT + t, :], axis=0))\
                            .then_inc(fX[t % 4], 16)
                g.wait_ge(X["fused"], NT)
                forget(g, "gathers")

            @block.tensor
            def _(pe):
                pe.sem_inc(X["xt_ps"], C)
                pe.sem_inc(X["h_ps"], C)
                pe.sem_inc(X["y_ps"], CY)

                def turn(i, u):
                    j = i * U + u
                    pe.wait_ge(gX[u % 2], (i * PER[u % 2] + u // 2 + 1) * 16)
                    pe.wait_ge(X["xt_done"], j + C)
                    for k in range(KD):
                        ins = nc.tensor.transpose(bank(0, 2)[:, k * P:(k + 1) * P], xg[:, u % 2, k * P:(k + 1) * P],
                                                  ident)
                    ins.then_inc(X["xt_ps"], 1)

                with pe.Fori(0, MT // U) as i:
                    turn(i, 0)
                    for u in range(U):
                        j = i * U + u
                        w13 = wslot[u][:, 0:4096].rearrange("p (k n) -> p k n", k=KD)
                        w2 = wslot[u][:, 4096:6144].rearrange("p (k n) -> p k n", k=2)
                        pe.wait_ge(X["xt_done"], j + 1 + C)
                        pe.wait_ge(wX[u], (i + 1) * 48)
                        pe.wait_ge(X["hdn"], free(j, u) + C)
                        for c in range(4):
                            for k in range(KD):
                                ins = nc.tensor.matmul(psum[:, 2 + u % 2, c * P:(c + 1) * P],
                                                       w13[:, k, c * P:(c + 1) * P], xgT[:, u % 2, k * P:(k + 1) * P],
                                                       start=(k == 0), stop=(k == KD - 1))
                        ins.then_inc(X["h_ps"], 1)
                        if u < U - 1:
                            turn(i, u + 1)
                        pe.wait_ge(X["hdn"], j + 1 + C)
                        pe.wait_ge(X["y_v"], free(j, u) + C)
                        for c in range(2):
                            for k in range(2):
                                ins = nc.tensor.matmul(psum[:, 4 + 2 * (u % 2) + c, :], hT[:, u % 2, k * P:(k + 1) * P],
                                                       w2[:, k, c * 512:(c + 1) * 512], start=(k == 0), stop=(k == 1))
                        ins.then_inc(X["y_ps"], 1)

            @block.scalar
            def _(act):
                act.sem_inc(X["xt_done"], C)
                for b in range(2):
                    act.sem_inc(stX[b], 16)

                def evac(i, u):
                    j = i * U + u
                    act.wait_ge(X["xt_ps"], j + 1 + C)
                    act.wait_ge(X["h_ps"], free(j, u) + C)
                    nc.scalar.activation(xgT[:, u % 2, :], bank(0, 2), ACT.Copy).then_inc(X["xt_done"], 1)

                with act.Fori(0, MT // U) as i:
                    evac(i, 0)
                    for u in range(U):
                        j = i * U + u
                        act.wait_ge(X["h_ps"], j + 1 + C)
                        act.wait_ge(X["hdn"], free(j, u) + C)
                        nc.scalar.activation(sgx[:, u % 2, :], psum[:, 2 + u % 2, 0:256], ACT.Silu).then_inc(X["sig"], 1)
                        if u < U - 1:
                            evac(i, u + 1)
                        act.wait_ge(X["y_v"], j + 1 + C)
                        act.dma_start(y_rows[ds(j * P, P), :], yv[:, u % 2, :]).then_inc(stX[u % 2], 16)
                for t in range(NT):
                    f1 = fin[2 * (t % 4)]
                    act.wait_ge(fX[t % 4], 32 * (t // 4 + 1))
                    nc.scalar.activation(f1, f1, ACT.Copy, scale=wtop[:, t, 0:1]).then_inc(X["f1"], 1)

            @block.vector
            def _(v):
                vec = nc.vector
                v.sem_inc(X["hdn"], C)
                v.sem_inc(X["y_v"], C)
                with v.Fori(0, MT // U) as i:
                    for u in range(U):
                        j = i * U + u
                        v.wait_ge(X["sig"], j + 1)
                        v.wait_ge(X["y_ps"], free(j, u) + CY)
                        vec.tensor_tensor(hT[:, u % 2, :], sgx[:, u % 2, :], psum[:, 2 + u % 2, 256:512], ALU.mult)\
                            .then_inc(X["hdn"], 1)
                        v.wait_ge(X["y_ps"], j + 1 + CY)
                        v.wait_ge(stX[u % 2], (i * PER[u % 2] + u // 2 + 1) * 16)
                        vec.tensor_copy(yv[:, u % 2, :], bank(4 + 2 * (u % 2), 2)).then_inc(X["y_v"], 1)
                v.wait_ge(X["g2"], 32)
                own = Own(v, X["own_v"])
                for t in range(NT):
                    f1, f2 = fin[2 * (t % 4)], fin[2 * (t % 4) + 1]
                    v.wait_ge(fX[t % 4], 32 * (t // 4 + 1))
                    v.wait_ge(X["f1"], t + 1)
                    own.link(vec.scalar_tensor_tensor(f1, f2, wtop[:, t, 1:2], f1, ALU.mult, ALU.add))
                    own.link(vec.tensor_tensor(f1, f1, g2b[:, 0 if t == 0 else 1, :], ALU.mult))
                    own.tell(vec.tensor_tensor(h[:, t, :], h[:, t, :], f1, ALU.add), X["fused"])

        layer_loop.__exit__(None, None, None)

        F = sems("fin", "gain own_a own_v std done out")
        fout = ar(0, NT, D)
        fgain = ar(NT * D, D)
        fjunk = ar(NT * D + D, D)
        with nc.Block() as block:
            @block.sync
            def _(sp):
                sp.dma_start(fgain, a["final_norm"].partition_broadcast(P)).then_inc(F["gain"], 16)
                for t in range(NT):
                    sp.wait_ge(F["done"], t + 1)
                    dst = outs["y_prompt"][0] if t == 0 else outs["y_sample"][0, (t - 1) * P:t * P, :]
                    sp.dma_start(dst, fout[:, t, :]).then_inc(F["out"], 16)
                sp.wait_ge(F["out"], 16 * NT)

            @block.scalar
            def _(act):
                own = Own(act, F["own_a"])
                for t in range(NT):
                    own.link(nc.scalar.activation(fjunk, h[:, t, :], ACT.Square, accum_out=ss[:, t:t + 1]))
                own.tell(nc.scalar.activation(rstd, ss, ACT.Sqrt, bias=eps_col, scale=1.0 / D), F["std"])

            @block.vector
            def _(v):
                own = Own(v, F["own_v"])
                v.wait_ge(F["std"], 1)
                own.link(nc.vector.reciprocal(rstd, rstd))
                v.wait_ge(F["gain"], 16)
                for t in range(NT):
                    own.tell(nc.vector.scalar_tensor_tensor(fout[:, t, :], h[:, t, :], rstd[:, t:t + 1], fgain,
                                                            ALU.mult, ALU.mult), F["done"])


_INS = ['x_prompt', 'x_sample', 'state_gdn', 'cache_diff_k', 'cache_diff_v', 'cache_gqa_k', 'cache_gqa_v', 'c', 'c_ctx',
        'ada_w', 'ada_b', 'norm1', 'norm2', 'w_in', 'gdn_conv', 'gdn_a_log', 'gdn_dt_bias', 'gdn_norm', 'diff_lambda',
        'diff_norm', 'sgu_norm', 'sgu_ws', 'sgu_b', 'gqa_qnorm', 'gqa_knorm', 'w_branch', 'w_out', 'moe_wg', 'moe_bg',
        'moe_we', 'moe_be', 'moe_w1', 'moe_w3', 'moe_w2', 'final_norm']
_OUTS = [('y_prompt', (1, CTX, D)), ('y_sample', (1, LAT, D)), ('state', (1, DEPTH, 2, H, DK, DK)),
         ('dk', (1, DEPTH, CTX, H, DK)), ('dv', (1, DEPTH, CTX, H, DK)),
         ('gk', (1, DEPTH, CTX, 2, DK)), ('gv', (1, DEPTH, CTX, 2, DK))]


def kernel(**inputs):
    import concourse.bacc as _bacc
    from concourse.bass_utils import run_bass_kernel_spmd as _run

    nc = _bacc.Bacc("TRN2", target_bir_lowering=False, num_devices=1)
    table, where, layer, ids = constants()
    arrays, args = {}, {}
    given = {name: np.ascontiguousarray(inputs[name]) for name in _INS}
    given.update(consts=table, layer_consts=layer, ids=ids)
    for name, x in given.items():
        arrays[f"in_{name}"] = x
        args[name] = nc.dram_tensor(f"in_{name}", x.shape, mybir.dt.from_np(x.dtype), kind="ExternalInput").ap()
    outs = {name: nc.dram_tensor(f"out_{name}", shape, F32, kind="ExternalOutput").ap() for name, shape in _OUTS}
    build(nc, args, outs, where)
    r = _run(nc, [arrays], core_ids=[0])
    return tuple(r.results[0][f"out_{name}"] for name, _ in _OUTS)
```
